# Optimizing a Trainium2 kernel written in Bass

```python
import jax, jax.numpy as jnp
from jax import lax
import numpy as np

D_MODEL = 1024
BATCH = 1
SEQ = 256
DEPTH = 2

HEAD_DIM = 64
ROPE_THETA = 10000.0
Q_BLOCK = 128
LN_EPS = 1e-5

NSA_HEADS = 8
NSA_KV_HEADS = 2
NSA_GROUP = NSA_HEADS // NSA_KV_HEADS
CMP_BLOCK = 32
CMP_STRIDE = 16
CMP_HIDDEN = 2 * HEAD_DIM
SLC_BLOCK = 64
SLC_TOPN = 16
WINDOW = 512
FORCE_BONUS = 1.0e4

MOBA_HEADS = 8
MOBA_BLOCK = 256
MOBA_TOPK = 3
MOBA_Q_BLOCK = 32

SB_HEADS = 16

N_GROUPS = 4
EXPERTS_PER_GROUP = 4
N_EXPERTS = N_GROUPS * EXPERTS_PER_GROUP
TOPK_IN_GROUP = 2
EXPERT_HIDDEN = 256

DEEPNORM_ALPHA = float((2 * DEPTH) ** 0.25)
DEEPNORM_BETA = float((8 * DEPTH) ** -0.25)

N_EVEN = (DEPTH + 1) // 2
N_ODD = DEPTH // 2

NSA_Q_W = NSA_HEADS * HEAD_DIM
NSA_KV_W = NSA_KV_HEADS * HEAD_DIM
NSA_GATE_W = 3 * NSA_HEADS
MOBA_W = MOBA_HEADS * HEAD_DIM
EVEN_WIDTHS = (NSA_Q_W, NSA_KV_W, NSA_KV_W, NSA_KV_W, NSA_KV_W, NSA_KV_W, NSA_KV_W,
               NSA_GATE_W, MOBA_W, MOBA_W, MOBA_W)
EVEN_IN_W = sum(EVEN_WIDTHS)
EVEN_SPLITS = tuple(int(v) for v in np.cumsum(EVEN_WIDTHS)[:-1])
EVEN_OUT_W = NSA_Q_W + MOBA_W
SB_W = SB_HEADS * HEAD_DIM


def layer_norm(x, g, b):
    xf = x.astype(jnp.float32)
    mu = jnp.mean(xf, axis=-1, keepdims=True)
    var = jnp.mean(jnp.square(xf - mu), axis=-1, keepdims=True)
    return ((xf - mu) * lax.rsqrt(var + LN_EPS) * g + b).astype(x.dtype)

def rope(x, positions):
    half = x.shape[-1] // 2
    inv_freq = ROPE_THETA ** (-jnp.arange(half, dtype=jnp.float32) / half)
    ang = positions.astype(jnp.float32)[..., None] * inv_freq
    cos = jnp.cos(ang)[:, :, None, :]
    sin = jnp.sin(ang)[:, :, None, :]
    x1 = x[..., :half].astype(jnp.float32)
    x2 = x[..., half:].astype(jnp.float32)
    return jnp.concatenate([x1 * cos - x2 * sin, x2 * cos + x1 * sin], axis=-1).astype(x.dtype)

def masked_softmax(s, mask):
    s = jnp.where(mask, s.astype(jnp.float32), -jnp.inf)
    m = jnp.max(s, axis=-1, keepdims=True)
    m = jnp.where(jnp.isfinite(m), m, 0.0)
    e = jnp.where(mask, jnp.exp(s - m), 0.0)
    return e / jnp.maximum(jnp.sum(e, axis=-1, keepdims=True), 1e-30)

def nsa_attention(q, k_cmp, v_cmp, k_slc, v_slc, k_win, v_win, gates,
                  cmp_pos_k, cmp_pos_v, cmp_w1_k, cmp_w2_k, cmp_w1_v, cmp_w2_v):
    B, S = q.shape[0], q.shape[1]
    scale = HEAD_DIM ** -0.5
    n_cmp = (S - CMP_BLOCK) // CMP_STRIDE + 1
    cmp_start = jnp.arange(n_cmp) * CMP_STRIDE
    cmp_end = cmp_start + CMP_BLOCK - 1
    tok_idx = cmp_start[:, None] + jnp.arange(CMP_BLOCK)[None, :]

    def compress(kv, pos_emb, w1, w2):
        blocks = kv[:, tok_idx] + pos_emb[None, None, :, None, :]
        flat = blocks.transpose(0, 1, 3, 2, 4).reshape(B, n_cmp, NSA_KV_HEADS, CMP_BLOCK * HEAD_DIM)
        return jax.nn.gelu(flat @ w1) @ w2

    kc = compress(k_cmp, cmp_pos_k, cmp_w1_k, cmp_w2_k)
    vc = compress(v_cmp, cmp_pos_v, cmp_w1_v, cmp_w2_v)

    n_slc = S // SLC_BLOCK
    slc_start = jnp.arange(n_slc) * SLC_BLOCK
    overlap = ((cmp_start[:, None] < slc_start[None, :] + SLC_BLOCK)
               & (cmp_end[:, None] >= slc_start[None, :])).astype(jnp.float32)
    top_n = min(SLC_TOPN, n_slc)
    kb = k_slc.reshape(B, n_slc, SLC_BLOCK, NSA_KV_HEADS, HEAD_DIM).transpose(0, 3, 1, 2, 4)
    vb = v_slc.reshape(B, n_slc, SLC_BLOCK, NSA_KV_HEADS, HEAD_DIM).transpose(0, 3, 1, 2, 4)
    pad = ((0, 0), (WINDOW, 0), (0, 0), (0, 0))
    kwp = jnp.pad(k_win, pad)
    vwp = jnp.pad(v_win, pad)
    bi = jnp.arange(B)[:, None, None, None]
    hi = jnp.arange(NSA_KV_HEADS)[None, :, None, None]
    blk_ids = jnp.arange(n_slc)

    def one_block(b):
        q0 = b * Q_BLOCK
        t = q0 + jnp.arange(Q_BLOCK)
        qb = lax.dynamic_slice_in_dim(q, q0, Q_BLOCK, axis=1).reshape(
            B, Q_BLOCK, NSA_KV_HEADS, NSA_GROUP, HEAD_DIM)
        gb = lax.dynamic_slice_in_dim(gates, q0, Q_BLOCK, axis=1).reshape(
            B, Q_BLOCK, NSA_KV_HEADS, NSA_GROUP, 3)
        s_c = jnp.einsum('bqkgd,bnkd->bkgqn', qb, kc) * scale
        p_c = masked_softmax(s_c, cmp_end[None, :] <= t[:, None])
        o_c = jnp.einsum('bkgqn,bnkd->bqkgd', p_c.astype(vc.dtype), vc)
        imp = jnp.einsum('bkgqn,nj->bkqj', p_c, overlap)
        cur = t // SLC_BLOCK
        forced = ((blk_ids[None, :] == 0) | (blk_ids[None, :] == cur[:, None])
                  | (blk_ids[None, :] == cur[:, None] - 1))
        valid = blk_ids[None, :] <= cur[:, None]
        score = jnp.where(forced, imp + FORCE_BONUS, jnp.where(valid, imp, -1.0))
        _, sel = lax.top_k(score, top_n)
        sel_ok = sel <= cur[None, None, :, None]
        ks = kb[bi, hi, sel]
        vs = vb[bi, hi, sel]
        kpos = sel[..., None] * SLC_BLOCK + jnp.arange(SLC_BLOCK)
        m_s = sel_ok[..., None] & (kpos <= t[None, None, :, None, None])
        n_keys = top_n * SLC_BLOCK
        s_s = jnp.einsum('bqkgd,bkqnld->bkgqnl', qb, ks).reshape(
            B, NSA_KV_HEADS, NSA_GROUP, Q_BLOCK, n_keys) * scale
        p_s = masked_softmax(s_s, m_s.reshape(B, NSA_KV_HEADS, Q_BLOCK, n_keys)[:, :, None])
        o_s = jnp.einsum('bkgqm,bkqmd->bqkgd', p_s.astype(vs.dtype),
                         vs.reshape(B, NSA_KV_HEADS, Q_BLOCK, n_keys, HEAD_DIM))
        kw = lax.dynamic_slice_in_dim(kwp, q0, WINDOW + Q_BLOCK, axis=1)
        vw = lax.dynamic_slice_in_dim(vwp, q0, WINDOW + Q_BLOCK, axis=1)
        wpos = q0 - WINDOW + jnp.arange(WINDOW + Q_BLOCK)
        dist = t[:, None] - wpos[None, :]
        m_w = (dist >= 0) & (dist < WINDOW) & (wpos[None, :] >= 0)
        s_w = jnp.einsum('bqkgd,bskd->bkgqs', qb, kw) * scale
        p_w = masked_softmax(s_w, m_w)
        o_w = jnp.einsum('bkgqs,bskd->bqkgd', p_w.astype(vw.dtype), vw)
        o = gb[..., 0:1] * o_c + gb[..., 1:2] * o_s + gb[..., 2:3] * o_w
        return o.reshape(B, Q_BLOCK, NSA_Q_W)

    out = lax.map(one_block, jnp.arange(S // Q_BLOCK))
    return out.transpose(1, 0, 2, 3).reshape(B, S, NSA_Q_W)

def moba_attention(q, k, v):
    B, S = q.shape[0], q.shape[1]
    scale = HEAD_DIM ** -0.5
    n_blk = -(-S // MOBA_BLOCK)
    pad = n_blk * MOBA_BLOCK - S
    kp = jnp.pad(k, ((0, 0), (0, pad), (0, 0), (0, 0)))
    vp = jnp.pad(v, ((0, 0), (0, pad), (0, 0), (0, 0)))
    kb = kp.reshape(B, n_blk, MOBA_BLOCK, MOBA_HEADS, HEAD_DIM).transpose(0, 3, 1, 2, 4)
    vb = vp.reshape(B, n_blk, MOBA_BLOCK, MOBA_HEADS, HEAD_DIM).transpose(0, 3, 1, 2, 4)
    k_mean = jnp.mean(kb.astype(jnp.float32), axis=3).astype(k.dtype)
    top_k = min(MOBA_TOPK, n_blk)
    bi = jnp.arange(B)[:, None, None, None]
    hi = jnp.arange(MOBA_HEADS)[None, :, None, None]
    blk_ids = jnp.arange(n_blk)
    n_sel = top_k * MOBA_BLOCK

    def one_block(b):
        q0 = b * MOBA_Q_BLOCK
        t = q0 + jnp.arange(MOBA_Q_BLOCK)
        cur = q0 // MOBA_BLOCK
        qb = lax.dynamic_slice_in_dim(q, q0, MOBA_Q_BLOCK, axis=1)
        gate = jnp.einsum('bqhd,bhnd->bhqn', qb, k_mean).astype(jnp.float32)
        gate = jnp.where(blk_ids < cur, gate, -jnp.inf)
        _, sel = lax.top_k(gate, top_k)
        sel_ok = sel < cur
        ks = kb[bi, hi, sel]
        vs = vb[bi, hi, sel]
        s_sel = jnp.einsum('bqhd,bhqnld->bhqnl', qb, ks).reshape(B, MOBA_HEADS, MOBA_Q_BLOCK, n_sel) * scale
        m_sel = jnp.broadcast_to(sel_ok[..., None], sel.shape + (MOBA_BLOCK,)).reshape(
            B, MOBA_HEADS, MOBA_Q_BLOCK, n_sel)
        k_own = lax.dynamic_index_in_dim(kb, cur, axis=2, keepdims=False)
        v_own = lax.dynamic_index_in_dim(vb, cur, axis=2, keepdims=False)
        s_own = jnp.einsum('bqhd,bhld->bhql', qb, k_own) * scale
        own_pos = cur * MOBA_BLOCK + jnp.arange(MOBA_BLOCK)
        m_own = jnp.broadcast_to(own_pos[None, :] <= t[:, None], (B, MOBA_HEADS, MOBA_Q_BLOCK, MOBA_BLOCK))
        p = masked_softmax(jnp.concatenate([s_sel, s_own], axis=-1),
                           jnp.concatenate([m_sel, m_own], axis=-1)).astype(v.dtype)
        o = (jnp.einsum('bhqm,bhqmd->bqhd', p[..., :n_sel],
                        vs.reshape(B, MOBA_HEADS, MOBA_Q_BLOCK, n_sel, HEAD_DIM))
             + jnp.einsum('bhql,bhld->bqhd', p[..., n_sel:], v_own))
        return o.reshape(B, MOBA_Q_BLOCK, MOBA_W)

    out = lax.map(one_block, jnp.arange(S // MOBA_Q_BLOCK))
    return out.transpose(1, 0, 2, 3).reshape(B, S, MOBA_W)

def stick_breaking_attention(q, k, v):
    B, S = q.shape[0], q.shape[1]
    scale = HEAD_DIM ** -0.5
    kpos = jnp.arange(S)

    def one_block(b):
        q0 = b * Q_BLOCK
        t = q0 + jnp.arange(Q_BLOCK)
        qb = lax.dynamic_slice_in_dim(q, q0, Q_BLOCK, axis=1)
        z = jnp.einsum('bqhd,bshd->bhqs', qb, k).astype(jnp.float32) * scale
        mask = kpos[None, :] < t[:, None]
        log_1m = jnp.where(mask, jax.nn.log_sigmoid(-z), 0.0)
        between = lax.cumsum(log_1m, axis=3, reverse=True) - log_1m
        w = jnp.where(mask, jnp.exp(jax.nn.log_sigmoid(z) + between), 0.0)
        o = jnp.einsum('bhqs,bshd->bqhd', w.astype(v.dtype), v)
        return o.reshape(B, Q_BLOCK, SB_W)

    out = lax.map(one_block, jnp.arange(S // Q_BLOCK))
    return out.transpose(1, 0, 2, 3).reshape(B, S, SB_W)

def nsa_moba_mixer(x, positions, w_in, w_out, cmp_pos_k, cmp_pos_v, cmp_w1_k, cmp_w2_k, cmp_w1_v, cmp_w2_v):
    B, S = x.shape[0], x.shape[1]
    proj = x @ w_in
    qa, kc, vc, ksl, vsl, kw, vw, ga, qm, km, vm = jnp.split(proj, EVEN_SPLITS, axis=-1)
    heads = lambda a, h: a.reshape(B, S, h, HEAD_DIM)
    qa = rope(heads(qa, NSA_HEADS), positions)
    kc = rope(heads(kc, NSA_KV_HEADS), positions)
    ksl = rope(heads(ksl, NSA_KV_HEADS), positions)
    kw = rope(heads(kw, NSA_KV_HEADS), positions)
    gates = jax.nn.sigmoid(ga.astype(jnp.float32)).astype(x.dtype).reshape(B, S, NSA_HEADS, 3)
    o_a = nsa_attention(qa, kc, heads(vc, NSA_KV_HEADS), ksl, heads(vsl, NSA_KV_HEADS),
                        kw, heads(vw, NSA_KV_HEADS), gates,
                        cmp_pos_k, cmp_pos_v, cmp_w1_k, cmp_w2_k, cmp_w1_v, cmp_w2_v)
    o_b = moba_attention(rope(heads(qm, MOBA_HEADS), positions),
                         rope(heads(km, MOBA_HEADS), positions), heads(vm, MOBA_HEADS))
    return jnp.concatenate([o_a, o_b], axis=-1) @ w_out

def stick_breaking_mixer(x, w_in, w_out):
    B, S = x.shape[0], x.shape[1]
    q, k, v = jnp.split(x @ w_in, 3, axis=-1)
    heads = lambda a: a.reshape(B, S, SB_HEADS, HEAD_DIM)
    return stick_breaking_attention(heads(q), heads(k), heads(v)) @ w_out

def hierarchical_moe(x, w_grp, b_grp, w_rt, b_rt, w_gate, w_up, w_down):
    p_grp = jax.nn.softmax((x @ w_grp + b_grp).astype(jnp.float32), axis=-1)
    g = jnp.argmax(p_grp, axis=-1)
    w_g = jnp.max(p_grp, axis=-1)
    logits_all = jnp.einsum('bsd,gde->bsge', x, w_rt) + b_rt
    logits = jnp.take_along_axis(logits_all, g[..., None, None], axis=2)[..., 0, :].astype(jnp.float32)
    top_val, top_idx = lax.top_k(logits, TOPK_IN_GROUP)
    w_e = jax.nn.softmax(top_val, axis=-1) * w_g[..., None]
    expert_id = g[..., None] * EXPERTS_PER_GROUP + top_idx
    combine = jnp.sum(jax.nn.one_hot(expert_id, N_EXPERTS, dtype=jnp.float32) * w_e[..., None], axis=2)

    def per_sequence(args):
        xs, cs = args
        h = jax.nn.silu(jnp.einsum('sd,edf->sef', xs, w_gate)) * jnp.einsum('sd,edf->sef', xs, w_up)
        return jnp.einsum('sef,efd->sd', h * cs[..., None].astype(h.dtype), w_down)

    return lax.map(per_sequence, (x, combine))

def _normal(key, shape, std):
    return jax.random.normal(key, shape, jnp.float32) * std

def first_inputs(seed: int = 0) -> dict:
    key = jax.random.key(seed)
    ks = jax.random.split(key, 24)
    D = D_MODEL
    flat_cmp = CMP_BLOCK * HEAD_DIM
    return {
        'x': jax.random.normal(ks[0], (BATCH, SEQ, D), jnp.float32),
        'positions': jnp.broadcast_to(jnp.arange(SEQ, dtype=jnp.int32), (BATCH, SEQ)),
        'ab_w_in': _normal(ks[1], (N_EVEN, D, EVEN_IN_W), D ** -0.5),
        'ab_w_out': _normal(ks[2], (N_EVEN, EVEN_OUT_W, D), DEEPNORM_BETA * EVEN_OUT_W ** -0.5),
        'nsa_cmp_pos_k': _normal(ks[3], (N_EVEN, CMP_BLOCK, HEAD_DIM), 0.02),
        'nsa_cmp_pos_v': _normal(ks[4], (N_EVEN, CMP_BLOCK, HEAD_DIM), 0.02),
        'nsa_cmp_w1_k': _normal(ks[5], (N_EVEN, flat_cmp, CMP_HIDDEN), flat_cmp ** -0.5),
        'nsa_cmp_w2_k': _normal(ks[6], (N_EVEN, CMP_HIDDEN, HEAD_DIM), CMP_HIDDEN ** -0.5),
        'nsa_cmp_w1_v': _normal(ks[7], (N_EVEN, flat_cmp, CMP_HIDDEN), flat_cmp ** -0.5),
        'nsa_cmp_w2_v': _normal(ks[8], (N_EVEN, CMP_HIDDEN, HEAD_DIM), CMP_HIDDEN ** -0.5),
        'sb_w_in': _normal(ks[9], (N_ODD, D, 3 * SB_W), D ** -0.5),
        'sb_w_out': _normal(ks[10], (N_ODD, SB_W, D), DEEPNORM_BETA * SB_W ** -0.5),
        'ln_mix_g': 1.0 + _normal(ks[11], (DEPTH, D), 0.02),
        'ln_mix_b': _normal(ks[12], (DEPTH, D), 0.02),
        'ln_ffn_g': 1.0 + _normal(ks[13], (DEPTH, D), 0.02),
        'ln_ffn_b': _normal(ks[14], (DEPTH, D), 0.02),
        'moe_w_grp': _normal(ks[15], (DEPTH, D, N_GROUPS), D ** -0.5),
        'moe_b_grp': _normal(ks[16], (DEPTH, N_GROUPS), 0.01),
        'moe_w_rt': _normal(ks[17], (DEPTH, N_GROUPS, D, EXPERTS_PER_GROUP), D ** -0.5),
        'moe_b_rt': _normal(ks[18], (DEPTH, N_GROUPS, EXPERTS_PER_GROUP), 0.01),
        'moe_w_gate': _normal(ks[19], (DEPTH, N_EXPERTS, D, EXPERT_HIDDEN), D ** -0.5),
        'moe_w_up': _normal(ks[20], (DEPTH, N_EXPERTS, D, EXPERT_HIDDEN), D ** -0.5),
        'moe_w_down': _normal(ks[21], (DEPTH, N_EXPERTS, EXPERT_HIDDEN, D), DEEPNORM_BETA * EXPERT_HIDDEN ** -0.5),
    }

def first_block(x, positions, ab_w_in, ab_w_out, nsa_cmp_pos_k, nsa_cmp_pos_v, nsa_cmp_w1_k, nsa_cmp_w2_k,
              nsa_cmp_w1_v, nsa_cmp_w2_v, sb_w_in, sb_w_out, ln_mix_g, ln_mix_b, ln_ffn_g, ln_ffn_b,
              moe_w_grp, moe_b_grp, moe_w_rt, moe_b_rt, moe_w_gate, moe_w_up, moe_w_down):
    for layer in range(DEPTH):
        i = layer // 2
        if layer % 2 == 0:
            mix = nsa_moba_mixer(x, positions, ab_w_in[i], ab_w_out[i], nsa_cmp_pos_k[i], nsa_cmp_pos_v[i],
                                 nsa_cmp_w1_k[i], nsa_cmp_w2_k[i], nsa_cmp_w1_v[i], nsa_cmp_w2_v[i])
        else:
            mix = stick_breaking_mixer(x, sb_w_in[i], sb_w_out[i])
        x = layer_norm(DEEPNORM_ALPHA * x + mix, ln_mix_g[layer], ln_mix_b[layer])
        ffn = hierarchical_moe(x, moe_w_grp[layer], moe_b_grp[layer], moe_w_rt[layer], moe_b_rt[layer],
                               moe_w_gate[layer], moe_w_up[layer], moe_w_down[layer])
        x = layer_norm(DEEPNORM_ALPHA * x + ffn, ln_ffn_g[layer], ln_ffn_b[layer])
    return x


DEPTH_2 = 1

GLA_HEADS = 4
GLA_VAL_WIDTH = D_MODEL // 2
GLA_DV = GLA_VAL_WIDTH // GLA_HEADS
GLA_DK = GLA_DV // 2
GLA_KEY_WIDTH = GLA_HEADS * GLA_DK
GLA_GATE_RANK = 16
GLA_TAU = 16.0
GLA_CHUNK = 64
ATT_WIDTH = D_MODEL - GLA_VAL_WIDTH
ATT_HEAD_DIM = 64
ATT_HEADS = ATT_WIDTH // ATT_HEAD_DIM
ROT_DIM = ATT_HEAD_DIM // 4
ROPE_THETA_2 = 500000.0
DILATED_PATTERNS = ((128, 1), (512, 4), (2048, 16))
MIX_WIDTH = GLA_VAL_WIDTH + ATT_WIDTH
IN_WIDTH = 2 * GLA_KEY_WIDTH + 2 * GLA_VAL_WIDTH + 2 * GLA_GATE_RANK + 3 * ATT_WIDTH
MOE_GROUPS = 4
MOE_EXPERTS_PER_GROUP = 8
MOE_N_EXPERTS = MOE_GROUPS * MOE_EXPERTS_PER_GROUP
MOE_TOP_K = 2
MOE_D_FF = D_MODEL // 2
MOE_BLOCK = 128
EPS = 1e-6
NEG_INF = -1e30


def _rmsnorm(x, w):
    xf = x.astype(jnp.float32)
    y = xf * lax.rsqrt(jnp.mean(xf * xf, axis=-1, keepdims=True) + EPS)
    return (y * w.astype(jnp.float32)).astype(x.dtype)

def _gla_one_direction(q, k, v, log_a):
    B, H, S, dk = q.shape
    dv = v.shape[-1]
    C = GLA_CHUNK
    n = S // C
    q = q.reshape(B, H, n, C, dk)
    k = k.reshape(B, H, n, C, dk)
    v = v.reshape(B, H, n, C, dv)
    b = jnp.cumsum(log_a.reshape(B, H, n, C, dk), axis=-2)
    b_last = b[..., -1:, :]
    q_dec = q * jnp.exp(b)
    k_inv = k * jnp.exp(-b)
    k_end = k * jnp.exp(b_last - b)
    lower = jnp.tril(jnp.ones((C, C), dtype=bool))
    attn = jnp.where(lower, jnp.einsum('bhncd,bhnsd->bhncs', q_dec, k_inv), 0.0)
    o_intra = jnp.einsum('bhncs,bhnsv->bhncv', attn, v)
    chunk_kv = jnp.einsum('bhncd,bhncv->bhndv', k_end, v)
    chunk_decay = jnp.exp(b_last[..., 0, :])

    def step(state, inp):
        kv_n, dec_n = inp
        return state * dec_n[..., None] + kv_n, state

    init = jnp.zeros((B, H, dk, dv), jnp.float32)
    _, states = lax.scan(step, init, (jnp.moveaxis(chunk_kv, 2, 0), jnp.moveaxis(chunk_decay, 2, 0)))
    states = jnp.moveaxis(states, 0, 2)
    o_inter = jnp.einsum('bhncd,bhndv->bhncv', q_dec, states)
    return (o_intra + o_inter).reshape(B, H, S, dv)

def _gla_mixer(q, k, v, g_out, lr_f, lr_b, wf, bf, wb, bb, norm_w):
    B, S, _ = q.shape
    f32 = jnp.float32

    def heads(t, d):
        return t.reshape(B, S, GLA_HEADS, d).transpose(0, 2, 1, 3).astype(f32)

    qh = heads(q, GLA_DK) * (GLA_DK ** -0.5)
    kh = heads(k, GLA_DK)
    vh = heads(v, GLA_DV)
    log_a_f = heads(jax.nn.log_sigmoid(lr_f.astype(f32) @ wf.astype(f32) + bf.astype(f32)), GLA_DK) / GLA_TAU
    log_a_b = heads(jax.nn.log_sigmoid(lr_b.astype(f32) @ wb.astype(f32) + bb.astype(f32)), GLA_DK) / GLA_TAU

    def flip(t):
        return jnp.flip(t, axis=2)

    o = _gla_one_direction(qh, kh, vh, log_a_f) + flip(
        _gla_one_direction(flip(qh), flip(kh), flip(vh), flip(log_a_b)))
    o = o.transpose(0, 2, 1, 3)
    gate = g_out.reshape(B, S, GLA_HEADS, GLA_DV).astype(f32)
    o = _rmsnorm(o, norm_w) * jax.nn.silu(gate)
    return o.reshape(B, S, GLA_VAL_WIDTH).astype(q.dtype)

def _rope_tables(S):
    inv = ROPE_THETA_2 ** (-(jnp.arange(0, ROT_DIM, 2, dtype=jnp.float32) / ROT_DIM))
    ang = jnp.arange(S, dtype=jnp.float32)[:, None] * inv[None, :]
    return jnp.cos(ang), jnp.sin(ang)

def _apply_partial_rope(t, cos, sin):
    half = ROT_DIM // 2
    t1 = t[..., :half]
    t2 = t[..., half:ROT_DIM]
    c = cos[None, :, None, :]
    s = sin[None, :, None, :]
    return jnp.concatenate([t1 * c - t2 * s, t2 * c + t1 * s, t[..., ROT_DIM:]], axis=-1)

def _banded_attention(q, k, v, radius):
    N, L, hd = q.shape
    R = radius
    nb = -(-L // R)
    Lp = nb * R
    q_p = jnp.pad(q, ((0, 0), (0, Lp - L), (0, 0))).reshape(N, nb, R, hd)
    k_p = jnp.pad(k, ((0, 0), (R, Lp - L + R), (0, 0))).reshape(N, nb + 2, R, hd)
    v_p = jnp.pad(v, ((0, 0), (R, Lp - L + R), (0, 0))).reshape(N, nb + 2, R, hd)
    k_win = jnp.concatenate([k_p[:, :-2], k_p[:, 1:-1], k_p[:, 2:]], axis=2)
    v_win = jnp.concatenate([v_p[:, :-2], v_p[:, 1:-1], v_p[:, 2:]], axis=2)
    s = jnp.einsum('nbqd,nbkd->nbqk', q_p, k_win) * (hd ** -0.5)
    qpos = (jnp.arange(nb)[:, None] * R + jnp.arange(R)[None, :])[:, :, None]
    kpos = (jnp.arange(nb)[:, None] * R - R + jnp.arange(3 * R)[None, :])[:, None, :]
    valid = (jnp.abs(qpos - kpos) <= R) & (kpos >= 0) & (kpos < L)
    s = jnp.where(valid, s, NEG_INF)
    m = jnp.max(s, axis=-1, keepdims=True)
    p = jnp.exp(s - m)
    z = jnp.sum(p, axis=-1, keepdims=True)
    o = jnp.einsum('nbqk,nbkd->nbqd', p / z, v_win)
    lse = (m + jnp.log(z))[..., 0]
    return o.reshape(N, Lp, hd)[:, :L], lse.reshape(N, Lp)[:, :L]

def _dilated_attention(q, k, v, window, dilation):
    B, S, H, hd = q.shape
    L = S // dilation

    def to_classes(t):
        return t.reshape(B, L, dilation, H, hd).transpose(0, 2, 3, 1, 4).reshape(B * dilation * H, L, hd)

    o, lse = _banded_attention(to_classes(q), to_classes(k), to_classes(v), window // (2 * dilation))
    o = o.reshape(B, dilation, H, L, hd).transpose(0, 3, 1, 2, 4).reshape(B, S, H, hd)
    lse = lse.reshape(B, dilation, H, L).transpose(0, 3, 1, 2).reshape(B, S, H)
    return o, lse

def _dilated_mixer(q, k, v):
    B, S, _ = q.shape
    cos, sin = _rope_tables(S)

    def heads(t):
        return t.reshape(B, S, ATT_HEADS, ATT_HEAD_DIM).astype(jnp.float32)

    qh = _apply_partial_rope(heads(q), cos, sin)
    kh = _apply_partial_rope(heads(k), cos, sin)
    vh = heads(v)
    outs, lses = [], []
    for window, dilation in DILATED_PATTERNS:
        o, lse = _dilated_attention(qh, kh, vh, window, dilation)
        outs.append(o)
        lses.append(lse)
    w = jax.nn.softmax(jnp.stack(lses, axis=0), axis=0)
    o = jnp.einsum('pbsh,pbshd->bshd', w, jnp.stack(outs, axis=0))
    return o.reshape(B, S, ATT_WIDTH).astype(q.dtype)

def _hier_moe(h, wg, bg, we, be, w_gate, w_up, w_down):
    T, D = h.shape
    f32 = jnp.float32
    hf = h.astype(f32)
    g_logits = hf @ wg.astype(f32) + bg.astype(f32)
    g_prob = jax.nn.softmax(g_logits, axis=-1)
    g_sel = jnp.argmax(g_logits, axis=-1)
    rows = jnp.arange(T)
    g_w = g_prob[rows, g_sel]
    e_logits = jnp.einsum('td,gde->tge', hf, we.astype(f32)) + be.astype(f32)
    e_sel_logits = e_logits[rows, g_sel]
    top_v, top_i = lax.top_k(e_sel_logits, MOE_TOP_K)
    weights = g_w[:, None] * jax.nn.softmax(top_v, axis=-1)
    expert = g_sel[:, None] * MOE_EXPERTS_PER_GROUP + top_i

    A = T * MOE_TOP_K
    e_flat = expert.reshape(-1)
    tok_flat = jnp.repeat(rows, MOE_TOP_K)
    w_flat = weights.reshape(-1)
    order = jnp.argsort(e_flat)
    e_s, tok_s, w_s = e_flat[order], tok_flat[order], w_flat[order]
    counts = jnp.zeros((MOE_N_EXPERTS,), jnp.int32).at[e_flat].add(1)
    padded = ((counts + MOE_BLOCK - 1) // MOE_BLOCK) * MOE_BLOCK
    start = jnp.cumsum(counts) - counts
    pend = jnp.cumsum(padded)
    pstart = pend - padded
    dest = pstart[e_s] + (jnp.arange(A) - start[e_s])
    n_blocks = -(-A // MOE_BLOCK) + MOE_N_EXPERTS
    cap = n_blocks * MOE_BLOCK
    buf_tok = jnp.full((cap,), T, jnp.int32).at[dest].set(tok_s.astype(jnp.int32))
    h_pad = jnp.concatenate([h, jnp.zeros((1, D), h.dtype)], axis=0)
    xb = h_pad[buf_tok].reshape(n_blocks, MOE_BLOCK, D)
    block_expert = jnp.clip(jnp.searchsorted(pend, jnp.arange(n_blocks) * MOE_BLOCK, side='right'),
                            0, MOE_N_EXPERTS - 1)

    def expert_block(args):
        xblk, eid = args
        return (jax.nn.silu(xblk @ w_gate[eid]) * (xblk @ w_up[eid])) @ w_down[eid]

    yb = lax.map(expert_block, (xb, block_expert)).reshape(cap, D)
    y_s = yb[dest] * w_s[:, None].astype(h.dtype)
    return jnp.zeros((T, D), h.dtype).at[tok_s].add(y_s)

def second_inputs(seed: int = 0) -> dict:
    key = jax.random.key(seed)
    ks = jax.random.split(key, 18)

    def nrm(k, shape, scale):
        return jax.random.normal(k, shape, jnp.float32) * scale

    return {
        'x': nrm(ks[0], (BATCH, SEQ, D_MODEL), 1.0),
        'norm1_w': 1.0 + nrm(ks[1], (DEPTH_2, D_MODEL), 0.02),
        'w_in': nrm(ks[2], (DEPTH_2, D_MODEL, IN_WIDTH), D_MODEL ** -0.5),
        'gla_fwd_gate_w': nrm(ks[3], (DEPTH_2, GLA_GATE_RANK, GLA_KEY_WIDTH), GLA_GATE_RANK ** -0.5),
        'gla_fwd_gate_b': nrm(ks[4], (DEPTH_2, GLA_KEY_WIDTH), 0.1),
        'gla_bwd_gate_w': nrm(ks[5], (DEPTH_2, GLA_GATE_RANK, GLA_KEY_WIDTH), GLA_GATE_RANK ** -0.5),
        'gla_bwd_gate_b': nrm(ks[6], (DEPTH_2, GLA_KEY_WIDTH), 0.1),
        'gla_norm_w': 1.0 + nrm(ks[7], (DEPTH_2, GLA_DV), 0.02),
        'w_out': nrm(ks[8], (DEPTH_2, MIX_WIDTH, D_MODEL), MIX_WIDTH ** -0.5),
        'norm2_w': 1.0 + nrm(ks[9], (DEPTH_2, D_MODEL), 0.02),
        'router_group_w': nrm(ks[10], (DEPTH_2, D_MODEL, MOE_GROUPS), D_MODEL ** -0.5),
        'router_group_b': nrm(ks[11], (DEPTH_2, MOE_GROUPS), 0.01),
        'router_expert_w': nrm(ks[12], (DEPTH_2, MOE_GROUPS, D_MODEL, MOE_EXPERTS_PER_GROUP), D_MODEL ** -0.5),
        'router_expert_b': nrm(ks[13], (DEPTH_2, MOE_GROUPS, MOE_EXPERTS_PER_GROUP), 0.01),
        'expert_w_gate': nrm(ks[14], (DEPTH_2, MOE_N_EXPERTS, D_MODEL, MOE_D_FF), D_MODEL ** -0.5),
        'expert_w_up': nrm(ks[15], (DEPTH_2, MOE_N_EXPERTS, D_MODEL, MOE_D_FF), D_MODEL ** -0.5),
        'expert_w_down': nrm(ks[16], (DEPTH_2, MOE_N_EXPERTS, MOE_D_FF, D_MODEL), MOE_D_FF ** -0.5),
        'final_norm_w': 1.0 + nrm(ks[17], (D_MODEL,), 0.02),
    }

def second_block(x, norm1_w, w_in, gla_fwd_gate_w, gla_fwd_gate_b, gla_bwd_gate_w, gla_bwd_gate_b,
              gla_norm_w, w_out, norm2_w, router_group_w, router_group_b, router_expert_w,
              router_expert_b, expert_w_gate, expert_w_up, expert_w_down, final_norm_w):
    B, S, D = x.shape
    sizes = [GLA_KEY_WIDTH, GLA_KEY_WIDTH, GLA_VAL_WIDTH, GLA_VAL_WIDTH,
             GLA_GATE_RANK, GLA_GATE_RANK, ATT_WIDTH, ATT_WIDTH]
    split_at = [int(c) for c in np.cumsum(sizes)]
    h = x
    for l in range(DEPTH_2):
        u = _rmsnorm(h, norm1_w[l])
        proj = u @ w_in[l]
        gq, gk, gv, gg, glf, glb, aq, ak, av = jnp.split(proj, split_at, axis=-1)
        gla_out = _gla_mixer(gq, gk, gv, gg, glf, glb, gla_fwd_gate_w[l], gla_fwd_gate_b[l],
                             gla_bwd_gate_w[l], gla_bwd_gate_b[l], gla_norm_w[l])
        att_out = _dilated_mixer(aq, ak, av)
        mixed = jnp.concatenate([gla_out, att_out], axis=-1)
        h = h + mixed @ w_out[l]
        u = _rmsnorm(h, norm2_w[l])
        moe = _hier_moe(u.reshape(B * S, D), router_group_w[l], router_group_b[l],
                        router_expert_w[l], router_expert_b[l], expert_w_gate[l],
                        expert_w_up[l], expert_w_down[l])
        h = h + moe.reshape(B, S, D)
    return _rmsnorm(h, final_norm_w)


def setup_inputs(seed=0):
    out = dict(first_inputs(seed))
    for name, value in second_inputs(seed + 1).items():
        if name != "x":
            out[name + "_2"] = value
    return out


def reference(
    x, positions, ab_w_in, ab_w_out, nsa_cmp_pos_k, nsa_cmp_pos_v, nsa_cmp_w1_k, nsa_cmp_w2_k,
    nsa_cmp_w1_v, nsa_cmp_w2_v, sb_w_in, sb_w_out, ln_mix_g, ln_mix_b, ln_ffn_g, ln_ffn_b,
    moe_w_grp, moe_b_grp, moe_w_rt, moe_b_rt, moe_w_gate, moe_w_up, moe_w_down, norm1_w_2,
    w_in_2, gla_fwd_gate_w_2, gla_fwd_gate_b_2, gla_bwd_gate_w_2, gla_bwd_gate_b_2,
    gla_norm_w_2, w_out_2, norm2_w_2, router_group_w_2, router_group_b_2, router_expert_w_2,
    router_expert_b_2, expert_w_gate_2, expert_w_up_2, expert_w_down_2, final_norm_w_2,
):
    x = first_block(
        x, positions, ab_w_in, ab_w_out, nsa_cmp_pos_k, nsa_cmp_pos_v, nsa_cmp_w1_k,
        nsa_cmp_w2_k, nsa_cmp_w1_v, nsa_cmp_w2_v, sb_w_in, sb_w_out, ln_mix_g, ln_mix_b,
        ln_ffn_g, ln_ffn_b, moe_w_grp, moe_b_grp, moe_w_rt, moe_b_rt, moe_w_gate, moe_w_up,
        moe_w_down,
    )
    return second_block(
        x, norm1_w_2, w_in_2, gla_fwd_gate_w_2, gla_fwd_gate_b_2, gla_bwd_gate_w_2,
        gla_bwd_gate_b_2, gla_norm_w_2, w_out_2, norm2_w_2, router_group_w_2, router_group_b_2,
        router_expert_w_2, router_expert_b_2, expert_w_gate_2, expert_w_up_2, expert_w_down_2,
        final_norm_w_2,
    )


_drawn_inputs = setup_inputs


def setup_inputs(seed=0):
    import zlib

    import numpy as np

    out = dict(_drawn_inputs(seed))
    spreads = {}
    factors = {'nsa_cmp_pos_k': 34.641,
     'nsa_cmp_pos_v': 4.882,
     'moe_b_grp': 5.964,
     'moe_b_rt': 3.05,
     'gla_fwd_gate_b_2': 3.784,
     'gla_norm_w_2': 9.542,
     'router_group_b_2': 19.604,
     'router_expert_b_2': 4.121,
     'final_norm_w_2': 8.102,
     'norm2_w_2': 3.534}
    for name, (base, spread) in spreads.items():
        noise = np.random.default_rng([zlib.crc32(name.encode()), seed]).standard_normal(out[name].shape)
        drawn = base * np.exp(spread * noise) if base else spread * noise
        out[name] = __import__('jax').numpy.asarray(drawn.astype(out[name].dtype))
    for name, factor in factors.items():
        out[name] = (out[name] * factor).astype(out[name].dtype)
    return out
```

```python
import numpy as np
import concourse.bass as bass
from concourse import mybir
from concourse.alu_op_type import AluOpType as ALU
from contextlib import ExitStack

F32 = mybir.dt.float32
I32 = mybir.dt.int32
ACT = mybir.ActivationFunctionType
AX = mybir.AxisListType.X

P = 128
S = 256
T = S // P
D = 1024
KT = D // P
HD = 64
HALF = HD // 2
CH = 512
SLOT = 4096
NSLOT = 6
BIG = 1e30
ALPHA = float((2 * 2) ** 0.25)
LN_EPS = 1e-5
RMS_EPS = 1e-6
SCALE = HD ** -0.5

CMP_STRIDE = 16
NBLK = (S - 32) // CMP_STRIDE + 1
NC16 = S // CMP_STRIDE

NQ = 512
C_KC, C_VC, C_KS, C_VS, C_KW, C_VW, C_GA, C_QM, C_KM, C_VM = (
    512, 640, 768, 896, 1024, 1152, 1280, 1304, 1816, 2328)
W_AB = 2840
C_GV, C_GG, C_LF, C_LB, C_AQ, C_AK, C_AV = 512, 1024, 1536, 1552, 1568, 2080, 2592
W_2 = 3104
RANK = 16
GCH = 64
ROT = 8

MOE = [(4, 256, 2, 20), (4, 256, 2, 20), (8, 512, 8, 36)]
G = 4
NB = G + 1
NMOE = len(MOE)


def _constants():
    j = np.arange(P)[:, None]
    i = np.arange(P)[None, :]
    t = np.arange(S)
    tok = np.arange(P)[:, None] + P * np.arange(T)[None, :]
    same = (j // GCH) == (i // GCH)
    z = np.zeros((P, P))
    c = {}
    c["ident"] = np.eye(P)
    tri = np.where(i > j, BIG, 0.0)
    c["causal"] = np.concatenate([tri, z, tri], 1)
    st = np.where(j < i, 0.0, -BIG)
    c["strict"] = np.concatenate([st, z, st], 1)
    c["neg_suffix"] = np.where(j >= i, -1.0, 0.0)
    c["neg_ones"] = np.full((P, P), -1.0)
    c["ones"] = np.full((P, P), 1.0)
    c["before"] = np.where(j < i, 1.0, 0.0)
    c["up_to"] = np.where(same & (j <= i), 1.0, 0.0)
    c["from_on"] = np.where(same & (j >= i), 1.0, 0.0)
    n = np.arange(NC16)
    seen = (n[None, None, :] * CMP_STRIDE + 31 <= tok[:, :, None]) & (n < NBLK)[None, None, :]
    c["cmp_big"] = np.where(seen, 0.0, BIG).reshape(P, T * NC16)
    c["cmp_seen"] = np.where(seen, 1.0, 0.0).reshape(P, T * NC16)
    c["own_head"] = np.where(j // NC16 == np.arange(8)[None, :], 1.0, 0.0)
    c["spread"] = np.where((j < NC16) & (i % NC16 == j), 1.0, 0.0)
    c["iota"] = np.broadcast_to(i, (P, P))
    c["descend"] = np.broadcast_to(8.0 - np.arange(8)[None, :], (P, 8))
    c["group_no"] = np.broadcast_to(np.arange(G)[None, :], (P, G))
    c["inv_freq"] = np.broadcast_to(
        (np.float32(10000.0) ** (-np.arange(HALF, dtype=np.float32) / np.float32(HALF)))[None, :], (P, HALF))
    inv2 = np.float32(500000.0) ** (-(np.arange(0, 2 * ROT, 2, dtype=np.float32) / np.float32(2 * ROT)))
    ang = tok[:, :, None].astype(np.float32) * inv2[None, None, :].astype(np.float32)
    c["cos2"] = np.cos(ang).reshape(P, T * ROT)
    c["sin2"] = np.sin(ang).reshape(P, T * ROT)
    d = np.abs(tok[:, :, None] - t[None, None, :])
    count = (d <= 64).astype(float) + (d % 4 == 0) + (d % 16 == 0)
    c["count"] = count.reshape(P, T * S)
    c["unseen"] = np.where(count > 0, 0.0, BIG).reshape(P, T * S)
    return {k: np.ascontiguousarray(v, dtype=np.float32) for k, v in c.items()}


CONST = _constants()
CONST_AT = {}
_at = 0
for _k, _v in CONST.items():
    CONST_AT[_k] = (_at, _v.shape[1])
    _at += _v.shape[1]
CONST_W = _at


UNITS = [G * m[2] for m in MOE]
N_AB = 0
CMP_CHUNK = 6
N_M0 = N_AB + 9
N_SB = N_M0 + 3 * UNITS[0]
N_M1 = N_SB + 8
N_2 = N_M1 + 3 * UNITS[1]
N_M2 = N_2 + 9
N_END = N_M2 + 3 * UNITS[2]
N_MOE = [N_M0, N_M1, N_M2]
CMP_DMAS = 4


def loaded_value(n):
    v = 16 * (n // NSLOT + 1)
    if n >= CMP_CHUNK and (n - CMP_CHUNK) % NSLOT == 0:
        v += 16 * (CMP_DMAS - 1)
    return v


def down_order(units):
    order = []
    for u in range(units):
        order += [("gate", u), ("up", u)]
        if u:
            order.append(("down", u - 1))
    return order + [("down", units - 1)]


AB_JOBS = [("moba", h) for h in range(8)]
for _i in range(4):
    AB_JOBS += [("slc", 2 * _i), ("slc", 2 * _i + 1), ("win", 2 * _i), ("win", 2 * _i + 1)]
DIL_JOBS = [("dil", h) for h in range(8)]


def job_pair(job):
    kind, h = job
    return h // 2 + (4 if kind in ("slc", "win") else 0)


def job_tile(job):
    kind, h = job
    return h // 2 + (0 if kind in ("slc", "win") else 4)


def last_of_pair(jobs, j):
    return j + 1 == len(jobs) or job_pair(jobs[j + 1]) != job_pair(jobs[j])


def first_of_pair(jobs, j):
    return j == 0 or job_pair(jobs[j - 1]) != job_pair(jobs[j])


def build(nc, a, out):
    ctx = ExitStack()
    with ctx:
        def sb(name, cols, dt=F32):
            return ctx.enter_context(nc.sbuf_tensor(name, [P, cols], dt))

        def sem(name):
            return ctx.enter_context(nc.semaphore(name))

        WEIGHTS = sb("weights", NSLOT * SLOT)
        CONSTS = sb("consts", CONST_W)
        X_ = sb("residual", T * D)
        XT_ = sb("x_transposed", KT * S)
        MIX = sb("mixed", T * D)
        NORM_ = sb("norm_params", 2 * 2 * D)
        PJ = sb("projected", 6208)
        QK = sb("heads_transposed", 14 * S)
        WK = sb("work", 4352)
        SMALL = sb("small_params", 2000)
        MISC = sb("misc", 2200)
        GATE_W = sb("gla_gate_w", 2 * S)
        POS_I = sb("positions", T, I32)
        OVER_I = sb("overflow", 2, I32)
        BANK = [ctx.enter_context(nc.psum_tensor(f"bank{i}", [P, CH], F32)) for i in range(8)]

        def const(name):
            o, n = CONST_AT[name]
            return CONSTS[:, o:o + n]

        ident = const("ident")
        X = X_[:, :].rearrange("p (t d) -> p t d", t=T)
        XT = XT_[:, :].rearrange("p (k s) -> p k s", k=KT)
        mixT = MIX[:, :].rearrange("p (k s) -> p k s", k=KT)
        U = MIX[:, :].rearrange("p (t d) -> p t d", t=T)
        NORM = NORM_[:, :].rearrange("p (b w d) -> p b w d", b=2, w=2)

        def slot(n):
            return WEIGHTS[:, (n % NSLOT) * SLOT:(n % NSLOT + 1) * SLOT]

        small_at = [0]

        def small(n):
            small_at[0] += n
            assert small_at[0] <= 2000
            return SMALL[:, small_at[0] - n:small_at[0]]

        misc_at = [0]

        def misc(n):
            misc_at[0] += n
            assert misc_at[0] <= 2200
            return MISC[:, misc_at[0] - n:misc_at[0]]

        router_w = [small(KT * m[3]).rearrange("p (k n) -> p k n", k=KT) for m in MOE]
        router_b = [small(m[3]) for m in MOE]
        cmp_w2 = small(2 * HD).rearrange("p (v d) -> p v d", v=2)
        cmp_pos = small(2 * P).rearrange("p (v d) -> p v d", v=2)
        gla_norm = small(P)

        cos1, sin1, angle, turns = (misc(T * HALF) for _ in range(4))
        pos_f = misc(T)
        cmp_posT = misc(2 * NC16).rearrange("p (v c) -> p v c", v=2)
        stats = misc(T * 12).rearrange("p (t w) -> p t w", t=T)
        mean_var = misc(T * 2).rearrange("p (t w) -> p t w", t=T)
        veps, lnv, rstd, newton = (misc(8) for _ in range(4))
        least = misc(8).rearrange("p (b t) -> p b t", b=4)
        psums = misc(8).rearrange("p (b t) -> p b t", b=4)
        rinv = misc(8).rearrange("p (b t) -> p b t", b=4)

        slot_loaded = [sem(f"slot{i}_loaded") for i in range(NSLOT)]
        x_loaded = sem("x_loaded")
        consts_loaded = sem("consts_loaded")
        small_loaded = sem("small_loaded")
        norm_loaded = [sem("norm0_loaded"), sem("norm1_loaded")]
        chunk_done = sem("chunk_done")
        xt_psum = sem("xt_psum")
        xt_act = sem("xt_act")
        xt_dve = sem("xt_dve")
        proj_copied = sem("proj_copied")
        roped = sem("roped")
        qt_psum = sem("qt_psum")
        qt_act = sem("qt_act")
        kv2_ready = sem("kv2_ready")
        angle_ready = sem("angle_ready")
        sines_ready = sem("sines_ready")
        gates_exp = sem("gates_exp")
        gates_ready = sem("gates_ready")
        dve_step = sem("dve_step")
        act_step = sem("act_step")
        pool_step = sem("pool_step")
        pos_psum = sem("pos_psum")
        pos_ready = sem("pos_ready")
        hid_exp_in = sem("hid_exp_in")
        hid_exp = sem("hid_exp")
        hid_ready = sem("hid_ready")
        hidT_psum = sem("hidT_psum")
        hidT_ready = sem("hidT_ready")
        kcvc_psum = sem("kcvc_psum")
        kcvc_ready = sem("kcvc_ready")
        cmp_scores = sem("cmp_scores")
        cmp_exp_in = sem("cmp_exp_in")
        cmp_exp = sem("cmp_exp")
        cmp_probs = sem("cmp_probs")
        cmp_pT_psum = sem("cmp_pT_psum")
        cmp_pT = sem("cmp_pT")
        scores_ready = sem("scores_ready")
        mins_ready = sem("mins_ready")
        probs_ready = sem("probs_ready")
        rinv_ready = sem("rinv_ready")
        diag_ready = sem("diag_ready")
        pt_psum = sem("pt_psum")
        pt_copied = sem("pt_copied")
        pv_done = sem("pv_done")
        o_copied = sem("o_copied")
        var_ready = sem("var_ready")
        rstd_ready = sem("rstd_ready")
        normed = sem("normed")
        logits_psum = sem("logits_psum")
        rexp_in = sem("rexp_in")
        rexp = sem("rexp")
        onehot_ready = sem("onehot_ready")
        rank_psum = sem("rank_psum")
        over_ready = sem("over_ready")
        scatter_psum = sem("scatter_psum")
        z_psum = sem("z_psum")
        z_abs = sem("z_abs")
        z_log = sem("z_log")
        sp_ready = sem("sp_ready")
        r_psum = sem("r_psum")
        w_log = sem("w_log")
        w_ready = sem("w_ready")
        sbo_psum = sem("sbo_psum")
        sbo_copied = sem("sbo_copied")
        gz_psum = sem("gz_psum")
        gz_abs = sem("gz_abs")
        gz_log = sem("gz_log")
        la_ready = sem("la_ready")
        bt_psum = sem("bt_psum")
        bs_ready = sem("bs_ready")
        eb_ready = sem("eb_ready")
        qk_ready = sem("qk_ready")
        ket_psum = sem("ket_psum")
        ket_ready = sem("ket_ready")
        att_psum = sem("att_psum")
        att_ready = sem("att_ready")
        kv_psum = sem("kv_psum")
        state_ready = sem("state_ready")
        go_psum = sem("go_psum")
        go_square = sem("go_square")
        go_ready = sem("go_ready")
        goT_psum = sem("goT_psum")
        goT_ready = sem("goT_ready")
        silu_exp = sem("silu_exp")
        out_stored = sem("out_stored")

        BLOCK_SIGNALS = ("p_ready", "pT_psum", "pT_copied", "c_ready", "xc_psum", "xc_act", "xc_dve",
                         "up_done", "silu_done", "h_ready", "hT_psum", "hT_ready", "y_copied")
        main = {k: sem("moe_" + k) for k in BLOCK_SIGNALS}
        over = [{k: sem(f"over{L}_" + k) for k in BLOCK_SIGNALS + ("loaded", "chunk_done", "scattered", "added")}
                for L in range(NMOE)]

        pj = PJ[:, 0:T * W_AB].rearrange("p (t n) -> p t n", t=T)
        qk = QK[:, :].rearrange("p (n s) -> p n s", s=S)
        kv2 = MIX[:, 0:4 * S].rearrange("p (v h s) -> p v h s", v=2, h=2)
        ROPE_TMP = [WK[:, 512 * i:512 * (i + 1)] for i in range(4)]
        SM = [WK[:, 512 * i:512 * (i + 1)] for i in range(2)]
        PR = [WK[:, 1024 + 512 * i:1024 + 512 * (i + 1)] for i in range(3)]
        PTS = [WK[:, 2560 + 512 * i:2560 + 512 * (i + 1)] for i in range(2)]
        DIAG = [WK[:, 3584 + 256 * i:3584 + 256 * (i + 1)].rearrange("p (t s) -> p t s", t=T) for i in range(3)]

        hid_g = misc(2 * P)
        hid_t = misc(2 * P)
        hidT = misc(2 * 32).rearrange("p (v n) -> p v n", v=2)
        kcT = misc(NC16)
        vc = misc(P)
        v_blocks = PJ[:, 5680:5680 + 512].rearrange("p (h d) -> p h d", h=8)
        cmp_p = hid_g.rearrange("p (t h n) -> p t h n", t=T, h=8)
        cmp_m = misc(16).rearrange("p (t h) -> p t h", t=T)
        cmp_pT_sb = misc(S)

        def heads(view, col, n):
            return view[:, :, col:col + n * HD].rearrange("p t (h x d) -> p t h x d", x=2, d=HALF)

        def job_operands(job):
            kind, h = job
            if kind == "moba":
                r = HD * (h % 2)
                return qk[r:r + HD, 6 + h // 2, :], qk[r:r + HD, 10 + h // 2, :], pj[:, :, C_VM + HD * h:C_VM + HD * h + HD], None
            if kind == "dil":
                r = HD * (h % 2)
                return qk[r:r + HD, h // 2, :], qk[r:r + HD, 4 + h // 2, :], AV[:, :, HD * h:HD * h + HD], None
            kv = h // 4
            r = HD * kv
            k, v, gate = (4, C_VS, 1) if kind == "slc" else (5, C_VW, 2)
            return qk[r:r + HD, h % 4, :], qk[r:r + HD, k, :], pj[:, :, v + HD * kv:v + HD * kv + HD], pj[:, :, C_GA + 3 * h + gate]

        sbQ = PJ[:, 0:8 * S].rearrange("p (n s) -> p n s", s=S)
        sbK = PJ[:, 8 * S:16 * S].rearrange("p (n s) -> p n s", s=S)
        sbV = PJ[:, 16 * S:16 * S + T * D].rearrange("p (t n) -> p t n", t=T)
        BL = 3 * P
        ZM = [QK[:, BL * i:BL * (i + 1)] for i in range(4)]
        WT = [QK[:, BL * (4 + i):BL * (5 + i)] for i in range(3)]
        AN = [WK[:, BL * i:BL * (i + 1)] for i in range(2)]
        SP_ = [WK[:, BL * (2 + i):BL * (3 + i)] for i in range(3)]
        WL = [WK[:, BL * (5 + i):BL * (6 + i)] for i in range(2)]

        GV, GG, AQ, AK, AV = (PJ[:, 1024 * i:1024 * (i + 1)].rearrange("p (t n) -> p t n", t=T) for i in range(5))
        W5 = PJ[:, 5120:6144]
        gqT, gkT = qk[:, 8:10, :], qk[:, 10:12, :]
        LR = QK[:, 12 * S:14 * S].rearrange("p (r s) -> p r s", r=2)
        W0, W1, W2, W3 = (WK[:, 1024 * i:1024 * (i + 1)] for i in range(4))
        by_tok = lambda w: w.rearrange("p (r t n) -> p r t n", r=2, t=T)
        by_key = lambda w: w.rearrange("p (r k s) -> p r k s", r=2, k=2)
        gw = GATE_W[:, :].rearrange("p (r n) -> p r n", r=2)
        decay = misc(16).rearrange("p (r k n) -> p r k n", r=2, k=2)
        state = MIX[:, 0:1536].rearrange("p (r k n v) -> p r k n v", r=2, k=2, n=3)
        att = W5.rearrange("p (i s) -> p i s", s=P)
        go_ms = misc(8)
        go_r = misc(8)
        go_l = misc(8)
        go_n = misc(8)

        yg = PJ[:, 0:G * D].rearrange("p (g d) -> p g d", g=G)
        PG = PJ[:, 5120:5120 + T * P].rearrange("p (t s) -> p t s", t=T)
        pT = QK[:, 0:NB * S].rearrange("p (g s) -> p g s", g=NB)
        yo = PJ[:, G * D:G * D + D]
        xcT = QK[:, NB * S:NB * S + KT * P].rearrange("p (k s) -> p k s", k=KT)
        SG = [WK[:, 512 * i:512 * (i + 1)] for i in range(2)]
        HB = [WK[:, 1024 + 512 * i:1024 + 512 * (i + 1)] for i in range(2)]
        HT = [WK[:, 2048 + 512 * i:2048 + 512 * (i + 1)].rearrange("p (f s) -> p f s", f=4) for i in range(2)]
        rlog = WK[:, 3072:3072 + T * 36]
        rt = WK[:, 3200:3200 + T * 32]
        small_r = [WK[:, 3300 + 16 * i:3316 + 16 * i] for i in range(16)]
        rcode = misc(T * NB).rearrange("p (t g) -> p t g", t=T)
        cw = misc(T * 8)
        cblk = misc(8)
        over_f = misc(2)

        W_NCOLS = [512, 512, 280, 512, 512, 512]
        W_COL0 = [0, 512, 1024, 1304, 1816, 2328]
        W2_NCOLS = [512, 512, 512, 32, 512, 512, 512]
        W2_COL0 = [0, 512, 1024, 1536, 1568, 2080, 2592]

        block = ctx.enter_context(nc.Block())

        @block.sync
        def _(sp):
            def free_slot(n):
                if n >= NSLOT:
                    sp.wait_ge(chunk_done, n - NSLOT + 1)

            def load_cols(n, w, col, ncols):
                free_slot(n)
                sp.dma_start(slot(n)[:, 0:KT * ncols].rearrange("p (k c) -> p k c", k=KT),
                             w.rearrange("(p k) c -> p k c", k=KT)[:, :, col:col + ncols]).then_inc(slot_loaded[n % NSLOT], 16)

            def load_out(n, w, half):
                free_slot(n)
                sp.dma_start(slot(n).rearrange("p (k c) -> p k c", k=KT),
                             w.rearrange("(k p) c -> p k c", p=P)[:, :, half * CH:(half + 1) * CH]).then_inc(slot_loaded[n % NSLOT], 16)

            def load_norm(k, params):
                if k >= 2:
                    sp.wait_ge(normed, 2 * (k - 1))
                for i, v in enumerate(params):
                    sp.dma_start(NORM[:, k % 2, i, :], v.partition_broadcast(P)).then_inc(norm_loaded[k % 2], 16)

            def expert_source(L, kind, e):
                name = ("moe_w_", "moe_w_", "expert_w_")[L] + kind + ("", "", "_2")[L]
                w = a[name][L if L < 2 else 0]
                if MOE[L][1] == CH:
                    w = w[bass.ds(e, 1)]
                    if kind == "down":
                        return w.rearrange("a (p f) d -> p (a f d)", p=P)
                    return w.rearrange("a (p k) f -> p (a k f)", p=P)
                w = w[bass.ds(e * 2, 2)]
                if kind == "down":
                    return w.rearrange("a (p f) d -> p a (f d)", p=P)
                return w.rearrange("a (p k) f -> p a (k f)", p=P)

            def unit_slot(L, n):
                return slot(n) if MOE[L][1] == CH else slot(n).rearrange("p (a w) -> p a w", a=2)

            def moe(L):
                n0, ug = N_MOE[L], MOE[L][2]
                with sp.Fori(0, G) as g:
                    for j, (kind, u) in enumerate(down_order(ug)):
                        n = n0 + j
                        sp.wait_ge(chunk_done, g * (3 * ug) + (n - NSLOT + 1))
                        sp.dma_start(unit_slot(L, n), expert_source(L, kind, g * ug + u)).then_inc(slot_loaded[n % NSLOT], 16)
                v = over[L]
                n_end = n0 + 3 * G * ug
                sp.wait_ge(over_ready, L + 1)
                flag = sp.value_load(OVER_I[0:1, 0:1], min_val=0, max_val=G)
                with sp.If(flag > 0):
                    group = sp.value_load(OVER_I[0:1, 1:2], min_val=0, max_val=G - 1)
                    sp.wait_ge(chunk_done, n_end)
                    for u in range(ug):
                        if u:
                            sp.wait_ge(v["chunk_done"], 3 * u)
                        for kind in ("gate", "up", "down"):
                            i = ("gate", "up", "down").index(kind)
                            sp.dma_start(unit_slot(L, i), expert_source(L, kind, group * ug + u)).then_inc(v["loaded"], 16)
                    sp.wait_ge(v["chunk_done"], 3 * ug)

            x_src = a["x"][0].rearrange("(t p) d -> p t d", p=P)
            for t in range(T):
                sp.dma_start(X[:, t, :], x_src[:, t, :]).then_inc(x_loaded, 16)
            w = a["ab_w_in"][0]
            for c in range(6):
                load_cols(N_AB + c, w, W_COL0[c], W_NCOLS[c])
            free_slot(CMP_CHUNK)
            cslot = slot(CMP_CHUNK).rearrange("p (v c n) -> p v c n", v=2, c=NC16)
            for i, name in enumerate(("nsa_cmp_w1_k", "nsa_cmp_w1_v")):
                for h in range(2):
                    sp.dma_start(cslot[HD * h:HD * h + HD, i, :, :],
                                 a[name][0][h * 1024:(h + 1) * 1024, :].rearrange("(c d) n -> d c n", d=HD)
                                 ).then_inc(slot_loaded[CMP_CHUNK % NSLOT], 16)
            load_norm(0, (a["ln_mix_g"][0], a["ln_mix_b"][0]))
            for half in range(2):
                load_out(N_AB + 7 + half, a["ab_w_out"][0], half)
            moe(0)
            load_norm(1, (a["ln_ffn_g"][0], a["ln_ffn_b"][0]))
            for c in range(6):
                load_cols(N_SB + c, a["sb_w_in"][0], c * CH, CH)
            load_norm(2, (a["ln_mix_g"][1], a["ln_mix_b"][1]))
            for half in range(2):
                load_out(N_SB + 6 + half, a["sb_w_out"][0], half)
            moe(1)
            load_norm(3, (a["ln_ffn_g"][1], a["ln_ffn_b"][1]))
            load_norm(4, (a["norm1_w_2"][0],))
            for c in range(7):
                load_cols(N_2 + c, a["w_in_2"][0], W2_COL0[c], W2_NCOLS[c])
            load_norm(5, (a["norm2_w_2"][0],))
            for half in range(2):
                load_out(N_2 + 7 + half, a["w_out_2"][0], half)
            moe(2)
            load_norm(6, (a["final_norm_w_2"],))
            o = out[0].rearrange("(t p) d -> p t d", p=P)
            for t in range(T):
                sp.wait_ge(normed, 12 + t + 1)
                sp.dma_start(o[:, t, :], X[:, t, :]).then_inc(out_stored, 16)
            sp.wait_ge(out_stored, 16 * T)

        @block.gpsimd
        def _(pool):
            def diagonals(jobs, first):
                for j, job in enumerate(jobs):
                    J = first + j
                    gate = job_operands(job)[3]
                    pool.wait_ge(rinv_ready, J + 1)
                    if J >= 3:
                        pool.wait_ge(pt_psum, J - 2)
                    for t in range(T):
                        if gate is None:
                            i = nc.gpsimd.tensor_scalar(DIAG[J % 3][:, t, :], ident, rinv[:, J % 4, t:t + 1], None, ALU.mult)
                        else:
                            if first == 0 and j == 8 and t == 0:
                                pool.wait_ge(gates_ready, 1)
                            i = nc.gpsimd.tensor_scalar(DIAG[J % 3][:, t, :], ident, rinv[:, J % 4, t:t + 1], gate[:, t:t + 1], ALU.mult, ALU.mult)
                    i.then_inc(diag_ready, 1)

            pool.wait_ge(consts_loaded, 16)
            diagonals(AB_JOBS, 0)
            pool.wait_ge(normed, 10)
            nc.gpsimd.memset(LR[0:RANK + 1, :, :], 1.0).then_inc(pool_step, 1)
            diagonals(DIL_JOBS, len(AB_JOBS))

        @block.tensor
        def _(pe):
            mm = nc.tensor.matmul

            def chunk_loaded(n):
                pe.wait_ge(slot_loaded[n % NSLOT], loaded_value(n))

            def transpose_x(k, src, waits):
                for t in range(T):
                    waits(t)
                    for kt in range(KT):
                        i = nc.tensor.transpose(BANK[kt // 2][:, (kt % 2) * S + t * P:(kt % 2) * S + (t + 1) * P],
                                                src[:, t, kt::KT], ident)
                        if t == T - 1 and kt % 2:
                            i.then_inc(xt_psum, 1)
                pe.wait_ge(xt_act, 2 * k + 2)
                pe.wait_ge(xt_dve, 2 * k + 2)

            def project(n, ncols, seq):
                if seq >= 2:
                    pe.wait_ge(proj_copied, seq - 1)
                chunk_loaded(n)
                w = slot(n)[:, 0:KT * ncols].rearrange("p (k c) -> p k c", k=KT)
                for t in range(T):
                    for kt in range(KT):
                        i = mm(BANK[4 + 2 * (seq % 2) + t][:, 0:ncols], XT[:, kt, t * P:(t + 1) * P], w[:, kt, :],
                               start=kt == 0, stop=kt == KT - 1)
                i.then_inc(chunk_done, 1)

            def project_T(n, seq, tiles, width=P):
                if seq >= 2:
                    pe.wait_ge(proj_copied, seq - 1)
                chunk_loaded(n)
                w = slot(n)[:, 0:KT * tiles * width].rearrange("p (k c) -> p k c", k=KT)
                for c in range(tiles):
                    for kt in range(KT):
                        i = mm(BANK[4 + 2 * (seq % 2) + c // 2][0:width, (c % 2) * S:(c % 2 + 1) * S],
                               w[:, kt, c * width:(c + 1) * width], XT[:, kt, :], start=kt == 0, stop=kt == KT - 1)
                i.then_inc(chunk_done, 1)

            def project_out(n):
                for half in range(2):
                    chunk_loaded(n + half)
                    w = slot(n + half).rearrange("p (k c) -> p k c", k=KT)
                    for t in range(T):
                        for kt in range(KT):
                            i = mm(BANK[4 + 2 * half + t][:, :], mixT[:, kt, t * P:(t + 1) * P], w[:, kt, :],
                                   start=kt == 0, stop=kt == KT - 1)
                    i.then_inc(chunk_done, 1)

            def attention(jobs, first, pairs0, extras):
                dil = jobs[0][0] == "dil"

                def scores(j):
                    J = first + j
                    q, k, _, _ = job_operands(jobs[j])
                    if J >= 2:
                        pe.wait_ge(mins_ready, J - 1)
                    if dil:
                        for t in range(T):
                            i = mm(BANK[J % 2][:, t * S:(t + 1) * S], q[:, t * P:(t + 1) * P], k, start=True, stop=True)
                    else:
                        mm(BANK[J % 2][:, 0:P], q[:, 0:P], k[:, 0:P], start=True, stop=True)
                        i = mm(BANK[J % 2][:, P:3 * P], q[:, P:S], k, start=True, stop=True)
                    i.then_inc(scores_ready, 1)

                def transposed(j):
                    J = first + j
                    pe.wait_ge(probs_ready, J + 1)
                    pe.wait_ge(diag_ready, J + 1)
                    if J >= 2:
                        pe.wait_ge(pt_copied, J - 1)
                    pr, dg, b = PR[J % 3], DIAG[J % 3], BANK[2 + J % 2]
                    if dil:
                        for kt in range(T):
                            for t in range(T):
                                i = mm(b[:, kt * S + t * P:kt * S + (t + 1) * P], pr[:, t * S + kt * P:t * S + (kt + 1) * P],
                                       dg[:, t, :], start=True, stop=True)
                    else:
                        for blk, t in enumerate((0, 1, 1)):
                            i = mm(b[:, blk * P:(blk + 1) * P], pr[:, blk * P:(blk + 1) * P], dg[:, t, :], start=True, stop=True)
                    i.then_inc(pt_psum, 1)

                def values(j):
                    J = first + j
                    kind, h = jobs[j]
                    pair = job_pair(jobs[j]) + pairs0
                    if dil:
                        pair = jobs[j][1] // 2 + pairs0
                    ob = BANK[4 + pair % 2]
                    if first_of_pair(jobs, j) and pair >= 2:
                        pe.wait_ge(o_copied, pair - 1)
                    gated = kind in ("slc", "win")
                    if gated and first_of_pair(jobs, j):
                        if h == 0:
                            pe.wait_ge(cmp_pT, 1)
                        mm(ob[:, 0:S], v_blocks[:, h:h + 2, :], cmp_pT_sb, start=True, stop=False)
                    pe.wait_ge(pt_copied, J + 1)
                    _, _, v, _ = job_operands(jobs[j])
                    r = HD * (h % 2)
                    last = not gated or (kind == "win")
                    if dil:
                        mm(ob[r:r + HD, 0:S], v[:, 0, :], PTS[J % 2][:, 0:S], start=True, stop=False)
                        i = mm(ob[r:r + HD, 0:S], v[:, 1, :], PTS[J % 2][:, S:2 * S], start=False, stop=True)
                    else:
                        mm(ob[r:r + HD, 0:S], v[:, 0, :], PTS[J % 2][:, 0:S], start=not gated, stop=False)
                        i = mm(ob[r:r + HD, P:S], v[:, 1, :], PTS[J % 2][:, S:3 * P], start=False, stop=last)
                    i.then_inc(pv_done, 1)

                for s in range(len(jobs) + 3):
                    if s < len(jobs):
                        scores(s)
                    if s in extras:
                        extras[s]()
                    if 0 <= s - 2 < len(jobs):
                        transposed(s - 2)
                    if s >= 3:
                        values(s - 3)

            pe.wait_ge(consts_loaded, 16)
            transpose_x(0, X, lambda t: pe.wait_ge(x_loaded, 16 * T) if t == 0 else None)

            def tr(k, aps):
                if k >= 4:
                    for s_, v in {4: [(qt_act, 1)], 5: [(qt_act, 2)], 6: [(kv2_ready, 1)], 7: [(kv2_ready, 2)], 8: [(qt_act, 3)]}[k]:
                        pe.wait_ge(s_, v)
                for n, ap in enumerate(aps):
                    i = nc.tensor.transpose(BANK[k % 4][:, n * P:(n + 1) * P], ap, ident)
                i.then_inc(qt_psum, 1)

            project(0, 512, 0)
            project(1, 512, 1)
            pe.wait_ge(small_loaded, SMALL_TOTAL)
            for v in range(2):
                i = nc.tensor.transpose(BANK[3][:, v * NC16:(v + 1) * NC16], cmp_pos[0:NC16, v, :], ident[0:NC16, 0:NC16])
            i.then_inc(pos_psum, 1)
            pe.wait_ge(roped, 1)
            for k in range(2):
                tr(k, [pj[:, t, P * j:P * (j + 1)] for j in (2 * k, 2 * k + 1) for t in range(T)])
            project(2, 280, 2)
            pe.wait_ge(roped, 2)
            pe.wait_ge(pos_ready, 1)
            tr(2, [pj[:, t, c:c + P] for c in (C_KS, C_KC) for t in range(T)])
            tr(3, [pj[:, t, C_VC:C_VC + P] for t in range(T)])
            project(3, 512, 3)
            pe.wait_ge(roped, 3)
            tr(4, [pj[:, t, C_KW:C_KW + P] for t in range(T)])
            project(4, 512, 4)
            pe.wait_ge(roped, 4)
            for k in range(2):
                tr(5 + k, [pj[:, t, C_QM + P * j:C_QM + P * (j + 1)] for j in (2 * k, 2 * k + 1) for t in range(T)])
            project(5, 512, 5)
            pe.wait_ge(roped, 5)
            for k in range(2):
                tr(7 + k, [pj[:, t, C_KM + P * j:C_KM + P * (j + 1)] for j in (2 * k, 2 * k + 1) for t in range(T)])

            cw1 = slot(CMP_CHUNK).rearrange("p (v c n) -> p v c n", v=2, c=NC16)

            def cmp_hidden():
                chunk_loaded(CMP_CHUNK)
                pe.wait_ge(kv2_ready, 2)
                pe.wait_ge(proj_copied, 6)
                for v in range(2):
                    kvv = kv2[:, v, :, :].rearrange("p h (n c) -> p (h n) c", c=NC16)
                    for c in range(NC16):
                        i = mm(BANK[6][0:2 * NC16, v * P:(v + 1) * P], kvv[:, :, c], cw1[:, v, c, :],
                               start=c == 0, stop=c == NC16 - 1)
                i.then_inc(chunk_done, 1)

            def cmp_hiddenT():
                pe.wait_ge(hid_ready, 1)
                for v in range(2):
                    i = nc.tensor.transpose(BANK[7][:, v * 32:v * 32 + 2 * NC16], hid_g[0:2 * NC16, v * P:(v + 1) * P],
                                            ident[0:2 * NC16, 0:2 * NC16])
                i.then_inc(hidT_psum, 1)

            def cmp_keys():
                pe.wait_ge(hidT_ready, 1)
                for h in range(2):
                    mm(BANK[7][HD * h:HD * h + HD, 64:64 + NBLK], cmp_w2[:, 0, :], hidT[:, 0, NC16 * h:NC16 * h + NBLK], start=True, stop=True)
                for h in range(2):
                    i = mm(BANK[7][0:NBLK, P + HD * h:P + HD * (h + 1)], hidT[:, 1, NC16 * h:NC16 * h + NBLK], cmp_w2[:, 1, :], start=True, stop=True)
                i.then_inc(kcvc_psum, 1)

            def cmp_score():
                pe.wait_ge(kcvc_ready, 1)
                mm(BANK[7][:, 0:P], const("spread")[0:NBLK, :], vc[0:NBLK, :], start=True, stop=True)
                for h in range(8):
                    for t in range(T):
                        r = HD * (h // 4)
                        col = S + (t * 4 + h % 4) * NC16
                        i = mm(BANK[7 - h // 4][:, col:col + NBLK], qk[r:r + HD, h % 4, t * P:(t + 1) * P], kcT[r:r + HD, 0:NBLK], start=True, stop=True)
                i.then_inc(cmp_scores, 1)

            def cmp_transpose():
                pe.wait_ge(cmp_probs, 1)
                for t in range(T):
                    i = nc.tensor.transpose(BANK[6][:, S + t * P:S + (t + 1) * P], cmp_p[:, t, :, :].rearrange("p h n -> p (h n)"), ident)
                i.then_inc(cmp_pT_psum, 1)

            pe.wait_ge(qt_act, 7)
            attention(AB_JOBS, 0, 0, {1: cmp_hidden, 3: cmp_hiddenT, 4: cmp_keys, 5: cmp_score, 8: cmp_transpose})
            pe.wait_ge(o_copied, 8)
            project_out(N_AB + 7)

            def expert_block(L, src, v, blk, unit, wait_loaded, pipelined, g, chunk_sem):
                E, F, ug, _ = MOE[L]
                pe.wait_ge(v["p_ready"], blk + 1)
                for t in range(T):
                    i = nc.tensor.transpose(BANK[7][:, t * P:(t + 1) * P], PG[:, t, :], ident)
                i.then_inc(v["pT_psum"], 1)
                for t in range(T):
                    mm(BANK[4][:, 0:E], PG[:, t, :], cw[:, t * E:(t + 1) * E], start=t == 0, stop=t == T - 1)
                for kt in range(KT):
                    for t in range(T):
                        i = mm(BANK[5 + kt // 4][:, (kt % 4) * P:(kt % 4 + 1) * P], src[:, t, kt::KT], PG[:, t, :],
                               start=t == 0, stop=t == T - 1)
                    if kt % 4 == 3:
                        i.then_inc(v["xc_psum"], 1)
                pe.wait_ge(v["xc_act"], blk + 1)
                pe.wait_ge(v["xc_dve"], blk + 1)
                order = down_order(ug) if pipelined else [(k, u) for u in range(ug) for k in ("gate", "up", "down")]

                def hidden_T(u):
                    pe.wait_ge(v["h_ready"], unit + u + 1)
                    for f in range(4):
                        if F == CH:
                            ap = HB[u % 2][:, f::4]
                        else:
                            ap = HB[u % 2][:, (f // 2) * F + f % 2:(f // 2 + 1) * F:2]
                        i = nc.tensor.transpose(BANK[4][:, f * P:(f + 1) * P], ap, ident)
                    i.then_inc(v["hT_psum"], 1)

                for j, (kind, u) in enumerate(order):
                    if kind == "gate" and u >= 2:
                        pe.wait_ge(v["silu_done"], unit + u - 1)
                    if kind == "up" and pipelined and u >= 1:
                        hidden_T(u - 1)
                    if kind == "up" and u >= 2:
                        pe.wait_ge(v["h_ready"], unit + u - 1)
                    w = wait_loaded(j)
                    if kind != "down":
                        if F == CH:
                            wv = w.rearrange("p (k f) -> p k f", k=KT)
                        else:
                            wv = w.rearrange("p (a k f) -> p k a f", a=2, k=KT)
                        b = BANK[(0 if kind == "gate" else 2) + u % 2]
                        for kt in range(KT):
                            i = mm(b[:, :], xcT[:, kt, :], wv[:, kt], start=kt == 0, stop=kt == KT - 1)
                    else:
                        if not pipelined or u == ug - 1:
                            hidden_T(u)
                        pe.wait_ge(v["hT_ready"], unit + u + 1)
                        wv = w.rearrange("p (f d) -> p f d", f=4)
                        for half in range(2):
                            for f in range(4):
                                i = mm(BANK[5 + half][:, :], HT[u % 2][:, f, :], wv[:, f, half * CH:(half + 1) * CH],
                                       start=u == 0 and f == 0, stop=u == ug - 1 and f == 3)
                    i.then_inc(chunk_sem, 1)

            def moe(L, k, src):
                E, F, ug, NR = MOE[L]
                transpose_x(k, src, lambda t: pe.wait_ge(normed, NORM_OF_XT[k] + t + 1))
                for t in range(T):
                    for kt in range(KT):
                        i = mm(BANK[0][:, t * 64:t * 64 + NR], XT[:, kt, t * P:(t + 1) * P], router_w[L][:, kt, :],
                               start=kt == 0, stop=kt == KT - 1)
                i.then_inc(logits_psum, 1)
                pe.wait_ge(onehot_ready, L + 1)
                oh = [small_r[2][:, t * G:(t + 1) * G] for t in range(T)]
                mm(BANK[1][:, 0:G], const("before"), oh[0], start=True, stop=True)
                mm(BANK[1][:, G:2 * G], const("ones"), oh[0], start=True, stop=False)
                mm(BANK[1][:, G:2 * G], const("before"), oh[1], start=False, stop=True)
                mm(BANK[1][:, 2 * G:3 * G], const("ones"), oh[0], start=True, stop=False)
                i = mm(BANK[1][:, 2 * G:3 * G], const("ones"), oh[1], start=False, stop=True)
                i.then_inc(rank_psum, 1)
                n0 = N_MOE[L]
                units0 = sum(UNITS[:L])
                with pe.Fori(0, G) as g:
                    def wait_loaded(j):
                        n = n0 + j
                        pe.wait_ge(slot_loaded[n % NSLOT], g * (16 * 3 * ug // NSLOT) + loaded_value(n))
                        return slot(n)

                    expert_block(L, src, main, g + G * L, g * ug + units0, wait_loaded, True, g, chunk_done)
                v = over[L]
                pe.wait_ge(over_ready, L + 1)
                flag = pe.value_load(OVER_I[0:1, 0:1], min_val=0, max_val=G)
                with pe.If(flag > 0):
                    def wait_over(j):
                        if j % 3 == 0:
                            pe.wait_ge(v["loaded"], 48 * (j // 3 + 1))
                        return slot(j % 3)

                    expert_block(L, src, v, 0, 0, wait_over, False, None, v["chunk_done"])
                    pe.wait_ge(v["pT_copied"], 1)
                    pe.wait_ge(v["y_copied"], 1)
                    for t in range(T):
                        for half in range(2):
                            i = mm(BANK[t * 2 + half][:, :], pT[:, G, t * P:(t + 1) * P], yo[:, half * CH:(half + 1) * CH],
                                   start=True, stop=True)
                    i.then_inc(v["scattered"], 1)
                    pe.wait_ge(v["added"], 1)
                pe.wait_ge(main["y_copied"], G * (L + 1))
                pe.wait_ge(main["pT_copied"], G * (L + 1))
                for t in range(T):
                    for half in range(2):
                        for gg in range(G):
                            i = mm(BANK[t * 2 + half][:, :], pT[:, gg, t * P:(t + 1) * P], yg[:, gg, half * CH:(half + 1) * CH],
                                   start=gg == 0, stop=gg == G - 1)
                        i.then_inc(scatter_psum, 1)

            moe(0, 1, X)

            transpose_x(2, X, lambda t: pe.wait_ge(normed, NORM_OF_XT[2] + t + 1))
            for c in range(4):
                project_T(N_SB + c, 6 + c, 4)
            for c in range(2):
                project(N_SB + 4 + c, CH, 10 + c)
            pe.wait_ge(proj_copied, 12)

            def sb_scores(h):
                r, n = HD * (h % 2), h // 2
                if h >= 2:
                    pe.wait_ge(z_abs, h - 1)
                mm(BANK[h % 2][:, 0:S], sbK[r:r + HD, n, 0:P], sbQ[r:r + HD, n, :], start=True, stop=True)
                mm(BANK[h % 2][:, S:BL], sbK[r:r + HD, n, P:S], sbQ[r:r + HD, n, P:S], start=True, stop=True).then_inc(z_psum, 1)

            def sb_suffix(h):
                pe.wait_ge(sp_ready, h + 1)
                if h >= 2:
                    pe.wait_ge(w_log, h - 1)
                b, spv = BANK[2 + h % 2], SP_[h % 3]
                mm(b[:, 0:S], const("neg_suffix"), spv[:, 0:S], start=True, stop=False)
                mm(b[:, P:S], const("neg_ones"), spv[:, S:BL], start=False, stop=True)
                mm(b[:, S:BL], const("neg_suffix"), spv[:, S:BL], start=True, stop=True).then_inc(r_psum, 1)

            def sb_values(h):
                r, pair = HD * (h % 2), h // 2
                if h % 2 == 0 and pair >= 2:
                    pe.wait_ge(sbo_copied, pair - 1)
                pe.wait_ge(w_ready, h + 1)
                b = BANK[4 + pair % 2]
                mm(b[r:r + HD, 0:S], sbV[:, 0, HD * h:HD * h + HD], WT[h % 3][:, 0:S], start=True, stop=False)
                mm(b[r:r + HD, P:S], sbV[:, 1, HD * h:HD * h + HD], WT[h % 3][:, S:BL], start=False, stop=True).then_inc(sbo_psum, 1)

            for s in range(16 + 4):
                if s < 16:
                    sb_scores(s)
                if 0 <= s - 2 < 16:
                    sb_suffix(s - 2)
                if s >= 4:
                    sb_values(s - 4)
            pe.wait_ge(sbo_copied, 8)
            project_out(N_SB + 6)
            moe(1, 3, X)

            transpose_x(4, U, lambda t: pe.wait_ge(normed, NORM_OF_XT[4] + t + 1))
            project_T(N_2, 12, 4)
            project(N_2 + 1, CH, 13)
            project(N_2 + 2, CH, 14)
            project_T(N_2 + 3, 15, 2, RANK)
            project(N_2 + 4, CH, 16)
            project(N_2 + 5, CH, 17)
            project(N_2 + 6, CH, 18)
            for m, src in enumerate((AQ, AK)):
                pe.wait_ge(roped, 6 + m)
                for k in range(2):
                    for n in range(4):
                        j, t = 2 * k + n // 2, n % 2
                        i = nc.tensor.transpose(BANK[2 * m + k][:, n * P:(n + 1) * P], src[:, t, P * j:P * (j + 1)], ident)
                    i.then_inc(qt_psum, 1)
            pe.wait_ge(qt_act, 11)
            for r in range(2):
                for t in range(T):
                    i = mm(BANK[r][:, t * S:(t + 1) * S], LR[0:RANK + 1, r, t * P:(t + 1) * P], gw[0:RANK + 1, r, :], start=True, stop=True)
                i.then_inc(gz_psum, 1)
            pe.wait_ge(la_ready, 1)
            la = by_tok(W3)
            for r in range(2):
                for k in range(2):
                    for t in range(T):
                        i = mm(BANK[2 + r][:, k * S + t * P:k * S + (t + 1) * P], la[:, r, t, k * P:(k + 1) * P],
                               const("up_to" if r == 0 else "from_on"), start=True, stop=True)
                i.then_inc(bt_psum, 1)
            qd, ki, ke = by_key(W1), by_key(W2), by_key(W3)
            ket = by_tok(W0)
            pe.wait_ge(qk_ready, 3)
            pe.wait_ge(proj_copied, 19)
            for r in range(2):
                for t in range(T):
                    for k in range(2):
                        i = nc.tensor.transpose(BANK[4 + r][:, t * S + k * P:t * S + (k + 1) * P], ke[:, r, k, t * P:(t + 1) * P], ident)
                i.then_inc(ket_psum, 1)
            for r in range(2):
                for i8 in range(8):
                    h, t = i8 // 4 + 2 * (i8 % 2), (i8 % 4) // 2
                    rows = slice(HD * (h % 2), HD * (h % 2) + HD)
                    i = mm(BANK[2 * r + i8 // 4][:, (i8 % 4) * P:(i8 % 4 + 1) * P], ki[rows, r, h // 2, t * P:(t + 1) * P],
                           qd[rows, r, h // 2, t * P:(t + 1) * P], start=True, stop=True)
                    if i8 % 4 == 3:
                        i.then_inc(att_psum, 1)
            pe.wait_ge(ket_ready, 2)
            for r in range(2):
                for n in ((0, 2, 1) if r == 0 else (3, 1, 2)):
                    for k in range(2):
                        rows = slice(GCH * (n % 2), GCH * (n % 2) + GCH)
                        for hh in range(2):
                            h = 2 * k + hh
                            col = (n // 2) * S + k * P
                            i = mm(BANK[4 + 2 * r + n % 2][HD * hh:HD * hh + HD, col:col + P],
                                   ket[rows, r, n // 2, h * HD:(h + 1) * HD], GV[rows, n // 2, h * P:(h + 1) * P], start=True, stop=True)
                i.then_inc(kv_psum, 1)
            pe.wait_ge(att_ready, 1)
            pe.wait_ge(state_ready, 1)
            for t in range(T):
                for h in range(4):
                    rows = slice(HD * (h % 2), HD * (h % 2) + HD)
                    b, cols = BANK[2 * t + h % 2], slice((h // 2) * P, (h // 2 + 1) * P)
                    i = mm(b[:, cols], att[:, (h % 2) * 4 + t * 2 + h // 2, :], GV[:, t, h * P:(h + 1) * P], start=True, stop=False)
                    for cc in range(2):
                        n = 2 * t + cc
                        for r in range(2):
                            if (r == 0 and n == 0) or (r == 1 and n == 3):
                                continue
                            sl = n - 1 if r == 0 else 2 - n
                            last = r == 1 or n == 3
                            i = mm(b[GCH * cc:GCH * cc + GCH, cols], qd[rows, r, h // 2, n * GCH:(n + 1) * GCH],
                                   state[rows, r, h // 2, sl, :], start=False, stop=last)
                i.then_inc(go_psum, 1)
            pe.wait_ge(go_ready, 1)
            for k in range(2):
                for n in range(4):
                    j, t = 2 * k + n // 2, n % 2
                    i = nc.tensor.transpose(BANK[4 + k][:, n * P:(n + 1) * P], by_tok2(W0)[:, t, P * j:P * (j + 1)], ident)
                i.then_inc(goT_psum, 1)
            pe.wait_ge(goT_ready, 1)
            attention(DIL_JOBS, len(AB_JOBS), 8, {})
            pe.wait_ge(o_copied, 12)
            project_out(N_2 + 7)
            moe(2, 5, U)

        @block.scalar
        def _(act):
            ac = nc.scalar.activation
            steps = [0]

            def link(i):
                steps[0] += 1
                i.then_inc(act_step, 1)
                act.wait_ge(act_step, steps[0])

            act.dma_start(CONSTS[:, :], a["constants"]).then_inc(consts_loaded, 16)
            act.dma_start(POS_I[:, :], a["positions"][0].rearrange("(t p) -> p t", p=P), allow_slow_non_contiguous=True).then_inc(small_loaded, 16)
            for i, n in enumerate(("nsa_cmp_w2_k", "nsa_cmp_w2_v")):
                act.dma_start(cmp_w2[:, i, :], a[n][0]).then_inc(small_loaded, 16)
            for i, n in enumerate(("nsa_cmp_pos_k", "nsa_cmp_pos_v")):
                act.dma_start(cmp_pos[0:NC16, i, :].rearrange("p (h d) -> p h d", h=2),
                              a[n][0].rearrange("(h c) d -> c h d", h=2)).then_inc(small_loaded, 16)
            for L in range(NMOE):
                E = MOE[L][0]
                wg, bg, we, be = ((a["moe_w_grp"][L], a["moe_b_grp"][L], a["moe_w_rt"][L], a["moe_b_rt"][L]) if L < 2 else
                                  (a["router_group_w_2"][0], a["router_group_b_2"][0], a["router_expert_w_2"][0], a["router_expert_b_2"][0]))
                act.dma_start(router_w[L][:, :, 0:G], wg.rearrange("(p k) g -> p k g", k=KT)).then_inc(small_loaded, 16)
                for g in range(G):
                    act.dma_start(router_w[L][:, :, G + g * E:G + (g + 1) * E], we[g].rearrange("(p k) e -> p k e", k=KT)).then_inc(small_loaded, 16)
                act.dma_start(router_b[L][:, 0:G], bg.partition_broadcast(P)).then_inc(small_loaded, 16)
                act.dma_start(router_b[L][:, G:G + G * E], be.rearrange("g e -> (g e)").partition_broadcast(P)).then_inc(small_loaded, 16)
            for r, n in enumerate(("gla_fwd_gate_", "gla_bwd_gate_")):
                act.dma_start(gw[0:RANK, r, :], a[n + "w_2"][0]).then_inc(small_loaded, 16)
                act.dma_start(gw[RANK:RANK + 1, r, :], a[n + "b_2"]).then_inc(small_loaded, 16)
            act.dma_start(gla_norm, a["gla_norm_w_2"][0].partition_broadcast(P)).then_inc(small_loaded, 16)

            def transpose_x(k):
                for b in range(2):
                    act.wait_ge(xt_psum, 4 * k + b + 1)
                    ac(XT[:, 2 * b:2 * b + 2, :], BANK[b][:, :].rearrange("p (k s) -> p k s", k=2), ACT.Copy).then_inc(xt_act, 1)

            def take(seq, n, parts):
                act.wait_ge(chunk_done, n + 1)
                for b, o, rows, ncols, scale in parts:
                    src = BANK[4 + 2 * (seq % 2) + b][0:rows, 0:ncols]
                    if seq == 0:
                        o = o.rearrange("p (j a d) -> p a j d", a=2, j=4)
                        src = src.rearrange("p (a j d) -> p a j d", a=2, j=4)
                    i = ac(o, src, ACT.Copy, scale=scale)
                i.then_inc(proj_copied, 1)

            def rstd_from(k, n):
                act.wait_ge(var_ready, k + 1)
                link(ac(lnv[:, 0:n], veps[:, 0:n], ACT.Ln))
                ac(rstd[:, 0:n], lnv[:, 0:n], ACT.Exp, scale=-0.5).then_inc(rstd_ready, 1)

            act.wait_ge(angle_ready, 2)
            ac(sin1, angle, ACT.Sin)
            ac(cos1, turns, ACT.Sin).then_inc(sines_ready, 1)
            nc.scalar.preload_act_table_set("natural_log_exp_and_others")
            transpose_x(0)
            for c in range(6):
                sc = -SCALE if c in (0, 3) else 1.0
                take(c, c, [(t, pj[:, t, W_COL0[c]:W_COL0[c] + W_NCOLS[c]], P, W_NCOLS[c], sc) for t in range(T)])
                if c == 2:
                    act.wait_ge(proj_copied, 3)
                    ac(pj[:, :, C_GA:C_GA + 24], pj[:, :, C_GA:C_GA + 24], ACT.Exp, scale=-1.0).then_inc(gates_exp, 1)
                if c == 2:
                    for k in range(2):
                        act.wait_ge(qt_psum, k + 1)
                        ac(qk[:, 2 * k:2 * k + 2, :], BANK[k][:, :].rearrange("p (n s) -> p n s", n=2), ACT.Copy).then_inc(qt_act, 1)
                if c == 4:
                    act.wait_ge(qt_psum, 5)
                    ac(qk[:, 5, :], BANK[0][:, 0:S], ACT.Copy).then_inc(qt_act, 1)
                if c == 5:
                    for k in (5, 6):
                        act.wait_ge(qt_psum, k + 1)
                        ac(qk[:, 6 + 2 * (k - 5):8 + 2 * (k - 5), :], BANK[k % 4][:, :].rearrange("p (n s) -> p n s", n=2), ACT.Copy).then_inc(qt_act, 1)
            for k in (7, 8):
                act.wait_ge(qt_psum, k + 1)
                ac(qk[:, 10 + 2 * (k - 7):12 + 2 * (k - 7), :], BANK[k % 4][:, :].rearrange("p (n s) -> p n s", n=2), ACT.Copy).then_inc(qt_act, 1)

            def attention(jobs, first, extras):
                dil = jobs[0][0] == "dil"
                for s in range(len(jobs) + 2):
                    if s < len(jobs):
                        J = first + s
                        act.wait_ge(mins_ready, J + 1)
                        if J >= 3:
                            act.wait_ge(pt_psum, J - 2)
                        for t, (c0, c1) in enumerate(((0, S), (S, 2 * S)) if dil else ((0, P), (P, 3 * P))):
                            i = ac(PR[J % 3][:, c0:c1], SM[J % 2][:, c0:c1], ACT.Exp, scale=-1.0,
                                   bias=least[:, J % 4, t:t + 1], accum_out=psums[:, J % 4, t:t + 1])
                        i.then_inc(probs_ready, 1)
                    if s in extras:
                        extras[s]()
                    if s >= 2:
                        J = first + s - 2
                        n = 2 * S if dil else 3 * P
                        act.wait_ge(pt_psum, J + 1)
                        if J >= 2:
                            act.wait_ge(pv_done, J - 1)
                        ac(PTS[J % 2][:, 0:n], BANK[2 + J % 2][:, 0:n], ACT.Copy).then_inc(pt_copied, 1)

            def gelu_exp():
                act.wait_ge(hid_exp_in, 1)
                ac(hid_t[0:2 * NC16, :], hid_t[0:2 * NC16, :], ACT.Exp, scale=-2.0 * float(np.sqrt(2.0 / np.pi))).then_inc(hid_exp, 1)

            def hiddenT():
                act.wait_ge(hidT_psum, 1)
                ac(hidT, BANK[7][:, 0:64].rearrange("p (v n) -> p v n", v=2), ACT.Copy).then_inc(hidT_ready, 1)

            def cmp_exponent():
                act.wait_ge(cmp_exp_in, 1)
                ac(cmp_p, cmp_p, ACT.Exp, scale=-1.0).then_inc(cmp_exp, 1)

            def cmp_pT_copy():
                act.wait_ge(cmp_pT_psum, 1)
                ac(cmp_pT_sb, BANK[6][:, S:2 * S], ACT.Copy).then_inc(cmp_pT, 1)

            attention(AB_JOBS, 0, {2: gelu_exp, 3: hiddenT, 6: cmp_exponent, 8: cmp_pT_copy})
            rstd_from(0, T)

            def expert_block(L, v, blk, unit, dst, chunk):
                ug = MOE[L][2]
                act.wait_ge(v["pT_psum"], blk + 1)
                ac(dst, BANK[7][:, 0:S].rearrange("p (o s) -> p o s", o=1), ACT.Copy).then_inc(v["pT_copied"], 1)
                act.wait_ge(v["xc_psum"], 2 * blk + 1)
                ac(xcT[:, 0:4, :], BANK[5][:, :].rearrange("p (k s) -> p k s", k=4), ACT.Copy).then_inc(v["xc_act"], 1)
                for u in range(ug):
                    chunk(u)
                    if u >= 2:
                        act.wait_ge(v["h_ready"], unit + u - 1)
                    ac(SG[u % 2], BANK[u % 2][:, :], ACT.Silu).then_inc(v["silu_done"], 1)

            def moe(L, k):
                transpose_x(k)
                for _ in range(2):
                    n = L * 2 + _ + 1
                    act.wait_ge(rexp_in, n)
                    w = small_r[1][:, 0:T * G] if _ == 0 else small_r[8][:, 0:T]
                    ac(w, w, ACT.Exp).then_inc(rexp, 1)
                nc.scalar.preload_act_table(ACT.Silu)
                ug = MOE[L][2]
                units0, n0 = sum(UNITS[:L]), N_MOE[L]
                order = down_order(ug)
                with act.Fori(0, G) as g:
                    def chunk(u):
                        act.wait_ge(chunk_done, g * (3 * ug) + (n0 + order.index(("gate", u)) + 1))

                    expert_block(L, main, g + G * L, g * ug + units0, pT[:, bass.ds(g, 1), :], chunk)
                v = over[L]
                act.wait_ge(over_ready, L + 1)
                flag = act.value_load(OVER_I[0:1, 0:1], min_val=0, max_val=G)
                with act.If(flag > 0):
                    expert_block(L, v, 0, 0, pT[:, G:G + 1, :], lambda u: act.wait_ge(v["chunk_done"], 3 * u + 1))
                nc.scalar.preload_act_table_set("natural_log_exp_and_others")

            moe(0, 1)
            rstd_from(1, T)
            transpose_x(2)
            for c in range(4):
                dst = (sbQ if c < 2 else sbK)
                take(6 + c, N_SB + c, [(b, dst[:, 4 * (c % 2) + 2 * b:4 * (c % 2) + 2 * b + 2, :], P, CH, SCALE if c < 2 else 1.0) for b in range(2)])
            for c in range(2):
                take(10 + c, N_SB + 4 + c, [(t, sbV[:, t, c * CH:(c + 1) * CH], P, CH, 1.0) for t in range(T)])
            for s in range(16 + 3):
                if s < 16:
                    act.wait_ge(z_abs, s + 1)
                    link(ac(AN[s % 2], AN[s % 2], ACT.Exp))
                    ac(AN[s % 2], AN[s % 2], ACT.Ln, bias=1.0).then_inc(z_log, 1)
                if s >= 3:
                    h = s - 3
                    act.wait_ge(w_log, h + 1)
                    if h >= 3:
                        act.wait_ge(sbo_psum, h - 2)
                    ac(WT[h % 3], WL[h % 2], ACT.Exp).then_inc(w_ready, 1)
            rstd_from(2, T)
            moe(1, 3)
            rstd_from(3, T)
            rstd_from(4, T)
            transpose_x(4)
            take(12, N_2, [(0, gqT, P, CH, SCALE), (1, gkT, P, CH, 1.0)])
            take(13, N_2 + 1, [(t, GV[:, t, :], P, CH, 1.0) for t in range(T)])
            take(14, N_2 + 2, [(t, GG[:, t, :], P, CH, 1.0) for t in range(T)])
            act.wait_ge(pool_step, 1)
            take(15, N_2 + 3, [(0, LR[0:RANK, :, :], RANK, CH, 1.0)])
            take(16, N_2 + 4, [(t, AQ[:, t, :], P, CH, -SCALE) for t in range(T)])
            take(17, N_2 + 5, [(t, AK[:, t, :], P, CH, 1.0) for t in range(T)])
            take(18, N_2 + 6, [(t, AV[:, t, :], P, CH, 1.0) for t in range(T)])
            for k in range(4):
                act.wait_ge(qt_psum, 9 + k + 1)
                ac(qk[:, 2 * k:2 * k + 2, :], BANK[k][:, :].rearrange("p (n s) -> p n s", n=2), ACT.Copy).then_inc(qt_act, 1)
            act.wait_ge(gz_abs, 1)
            link(ac(W1, W1, ACT.Exp))
            ac(W1, W1, ACT.Ln, bias=1.0).then_inc(gz_log, 1)
            act.wait_ge(bs_ready, 1)
            bs = by_key(W0)
            ac(W1, W0, ACT.Exp).then_inc(eb_ready, 1)
            ac(W2, W0, ACT.Exp, scale=-1.0).then_inc(eb_ready, 1)
            for r in range(2):
                for k in range(2):
                    for n in range(4):
                        end = n * GCH + (GCH - 1 if r == 0 else 0)
                        i = ac(by_key(W3)[:, r, k, n * GCH:(n + 1) * GCH], bs[:, r, k, n * GCH:(n + 1) * GCH], ACT.Exp,
                               scale=-1.0, bias=bs[:, r, k, end:end + 1])
            i.then_inc(eb_ready, 1)
            for r in range(2):
                act.wait_ge(ket_psum, r + 1)
                ac(W0[:, 512 * r:512 * (r + 1)], BANK[4 + r][:, :], ACT.Copy).then_inc(ket_ready, 1)
            act.wait_ge(ket_psum, 2)
            for t in range(T):
                i = ac(by_tok2(W3)[:, t, :], GG[:, t, :], ACT.Exp, scale=-1.0)
            i.then_inc(silu_exp, 1)
            for t in range(T):
                act.wait_ge(go_psum, t + 1)
                for par in range(2):
                    i = ac(by_tok2(W2)[:, t, :].rearrange("p (hh r v) -> p hh r v", hh=2, r=2)[:, :, par, :],
                           BANK[2 * t + par][:, 0:S].rearrange("p (hh v) -> p hh v", hh=2), ACT.Square)
                i.then_inc(go_square, 1)
            act.wait_ge(var_ready, 6)
            link(ac(go_l, go_ms, ACT.Ln))
            ac(go_r, go_l, ACT.Exp, scale=-0.5).then_inc(rstd_ready, 1)
            for k in range(2):
                act.wait_ge(goT_psum, k + 1)
                i = ac(mixT[:, 2 * k:2 * k + 2, :], BANK[4 + k][:, :].rearrange("p (n s) -> p n s", n=2), ACT.Copy)
            i.then_inc(goT_ready, 1)
            attention(DIL_JOBS, len(AB_JOBS), {})
            rstd_from(6, T)
            moe(2, 5)
            rstd_from(7, T)

        @block.vector
        def _(dve):
            tt, ts, stt = nc.vector.tensor_tensor, nc.vector.tensor_scalar, nc.vector.scalar_tensor_tensor
            cp = nc.vector.tensor_copy
            steps = [0]

            def link(i):
                steps[0] += 1
                i.then_inc(dve_step, 1)
                dve.wait_ge(dve_step, steps[0])

            def transpose_x(k):
                for b in (2, 3):
                    dve.wait_ge(xt_psum, 4 * k + b + 1)
                    cp(XT[:, 2 * b:2 * b + 2, :], BANK[b][:, :].rearrange("p (k s) -> p k s", k=2)).then_inc(xt_dve, 1)

            def sharpen(r, v, q):
                link(tt(q, r, r, ALU.mult))
                link(tt(q, q, v, ALU.mult))
                link(ts(q, q, -0.5, 1.5, ALU.mult, ALU.add))
                link(tt(r, r, q, ALU.mult))

            def norm(k, nvar, kind, dst):
                for t in range(T):
                    for half in range(2):
                        link(nc.vector.bn_stats(stats[:, t, 6 * half:6 * half + 6], X[:, t, half * CH:(half + 1) * CH]))
                    link(nc.vector.bn_aggr(mean_var[:, t, :], stats[:, t, :]))
                if kind == "layer":
                    ts(veps[:, 0:T], mean_var[:, :, 1], LN_EPS, None, ALU.add).then_inc(var_ready, 1)
                else:
                    link(tt(newton[:, 0:T], mean_var[:, :, 0], mean_var[:, :, 0], ALU.mult))
                    stt(veps[:, 0:T], newton[:, 0:T], RMS_EPS, mean_var[:, :, 1], ALU.add, ALU.add).then_inc(var_ready, 1)
                dve.wait_ge(rstd_ready, nvar + 1)
                sharpen(rstd[:, 0:T], veps[:, 0:T], newton[:, 0:T])
                dve.wait_ge(norm_loaded[k % 2], NORM_VALUE[k])
                for t in range(T):
                    if kind == "layer":
                        link(stt(X[:, t, :], X[:, t, :], mean_var[:, t, 0:1], NORM[:, k % 2, 0, :], ALU.subtract, ALU.mult))
                        stt(dst[:, t, :], X[:, t, :], rstd[:, t:t + 1], NORM[:, k % 2, 1, :], ALU.mult, ALU.add).then_inc(normed, 1)
                    else:
                        stt(dst[:, t, :], X[:, t, :], rstd[:, t:t + 1], NORM[:, k % 2, 0, :], ALU.mult, ALU.mult).then_inc(normed, 1)
                    dve.wait_ge(normed, 2 * k + t + 1)

            def residual(n, alpha):
                for half in range(2):
                    dve.wait_ge(chunk_done, n + half + 1)
                    for t in range(T):
                        link(stt(X[:, t, half * CH:(half + 1) * CH], X[:, t, half * CH:(half + 1) * CH], alpha,
                                 BANK[4 + 2 * half + t][:, :], ALU.mult, ALU.add))

            def rope(view, col, n):
                h = heads(view, col, n)
                x1, x2 = h[:, :, :, 0, :], h[:, :, :, 1, :]
                c, s_ = (v.rearrange("p (t d) -> p t d", t=T).unsqueeze(2).to_broadcast([P, T, n, HALF]) for v in (cos1, sin1))
                m = [w[:, 0:T * n * HALF].rearrange("p (t h d) -> p t h d", t=T, h=n) for w in ROPE_TMP]
                tt(m[0], x1, c, ALU.mult)
                tt(m[1], x2, s_, ALU.mult)
                tt(m[2], x2, c, ALU.mult)
                link(tt(m[3], x1, s_, ALU.mult))
                tt(x1, m[0], m[1], ALU.subtract)
                return tt(x2, m[2], m[3], ALU.add)

            dve.wait_ge(consts_loaded, 16)
            dve.wait_ge(small_loaded, SMALL_TOTAL)
            link(cp(pos_f, POS_I[:, :]))
            for t in range(T):
                link(ts(cos1[:, t * HALF:(t + 1) * HALF], const("inv_freq"), pos_f[:, t:t + 1], None, ALU.mult))
            TWO_PI = 2 * np.pi
            C1 = 6.28125
            C2 = float(np.float32(TWO_PI - C1))
            C3 = float(TWO_PI - C1 - float(np.float32(TWO_PI - C1)))
            for i, (o, quarter) in enumerate(((angle, 0.0), (turns, 0.25))):
                n = sin1
                link(ts(n, cos1, 1.0 / TWO_PI, quarter, ALU.mult, ALU.add))
                link(ts(n, n, 12582912.0, None, ALU.add))
                link(ts(n, n, 12582912.0, None, ALU.subtract))
                link(stt(o, n, -C1, cos1, ALU.mult, ALU.add))
                link(stt(o, n, -C2, o, ALU.mult, ALU.add))
                link(stt(o, n, -C3, o, ALU.mult, ALU.add))
                if quarter:
                    link(ts(o, o, TWO_PI * quarter, None, ALU.add))
                ts(o, o, 3.1415925, -3.1415925, ALU.min, ALU.max).then_inc(angle_ready, 1)
            transpose_x(0)
            dve.wait_ge(pos_psum, 1)
            cp(cmp_posT, BANK[3][:, 0:2 * NC16].rearrange("p (v c) -> p v c", v=2)).then_inc(pos_ready, 1)
            dve.wait_ge(sines_ready, 1)
            dve.wait_ge(proj_copied, 1)
            rope(pj, 0, 8).then_inc(roped, 1)
            dve.wait_ge(roped, 1)
            dve.wait_ge(proj_copied, 2)
            link(rope(pj, C_KC, 2))
            rope(pj, C_KS, 2).then_inc(roped, 1)
            dve.wait_ge(roped, 2)
            dve.wait_ge(proj_copied, 3)
            rope(pj, C_KW, 2).then_inc(roped, 1)
            dve.wait_ge(roped, 3)

            ga = pj[:, :, C_GA:C_GA + 24]
            dve.wait_ge(gates_exp, 1)
            link(ts(ga, ga, 1.0, None, ALU.add))
            nc.vector.reciprocal(ga, ga).then_inc(gates_ready, 1)
            dve.wait_ge(pos_ready, 1)
            dve.wait_ge(qt_psum, 3)
            cp(qk[:, 4, :], BANK[2][:, 0:S])
            link(nc.vector.memset(kv2[HD:P, :, :, NBLK * NC16:S], 0.0))
            for v, (b, col) in enumerate(((2, S), (3, 0))):
                dve.wait_ge(qt_psum, 3 + v)
                for h in range(2):
                    for half in range(2):
                        n = NC16 - half
                        rows = slice(HD * half, HD * half + HD)
                        src = BANK[b][HD * h:HD * h + HD, col + CMP_STRIDE * half:col + S].rearrange("p (n c) -> p n c", c=NC16)
                        dst = kv2[rows, v, h, 0:n * NC16].rearrange("p (n c) -> p n c", c=NC16)
                        i = tt(dst, src, cmp_posT[rows, v, :].unsqueeze(1).to_broadcast([HD, n, NC16]), ALU.add)
                i.then_inc(kv2_ready, 1)
            dve.wait_ge(proj_copied, 4)
            rope(pj, C_QM, 8).then_inc(roped, 1)
            dve.wait_ge(roped, 4)
            dve.wait_ge(proj_copied, 5)
            rope(pj, C_KM, 8).then_inc(roped, 1)
            dve.wait_ge(roped, 5)

            def attention(jobs, first, pairs0, extras):
                dil = jobs[0][0] == "dil"

                def inverse(j):
                    J = first + j
                    dve.wait_ge(probs_ready, J + 1)
                    if dil:
                        for t in range(T):
                            c = PR[J % 3][:, t * S:(t + 1) * S]
                            i = stt(c, c, 1.0, const("count")[:, t * S:(t + 1) * S], ALU.mult, ALU.mult, accum_out=psums[:, J % 4, t:t + 1])
                        link(i)
                    nc.vector.reciprocal(rinv[:, J % 4, :], psums[:, J % 4, :]).then_inc(rinv_ready, 1)

                for s in range(len(jobs) + 4):
                    if s < len(jobs):
                        J = first + s
                        dve.wait_ge(scores_ready, J + 1)
                        if J >= 2:
                            dve.wait_ge(probs_ready, J - 1)
                        for t, (c0, c1) in enumerate(((0, S), (S, 2 * S)) if dil else ((0, P), (P, 3 * P))):
                            i = nc.vector.tensor_tensor_reduce(
                                out=SM[J % 2][:, c0:c1], in0=BANK[J % 2][:, c0:c1],
                                in1=const("unseen" if dil else "causal")[:, c0:c1], scale=1.0, scalar=3e38,
                                op0=ALU.add, op1=ALU.min, accum_out=least[:, J % 4, t:t + 1])
                        i.then_inc(mins_ready, 1)
                    if 1 <= s <= len(jobs):
                        inverse(s - 1)
                    if s in extras:
                        extras[s]()
                    if s >= 4 and last_of_pair(jobs, s - 4):
                        j = s - 4
                        pair = (jobs[j][1] // 2 if dil else job_pair(jobs[j])) + pairs0
                        dve.wait_ge(pv_done, first + j + 1)
                        cp(mixT[:, job_tile(jobs[j]), :], BANK[4 + pair % 2][:, 0:S]).then_inc(o_copied, 1)

            R = slice(0, 2 * NC16)

            def gelu_in():
                dve.wait_ge(chunk_done, CMP_CHUNK + 1)
                link(cp(hid_g[R, :], BANK[6][R, 0:2 * P]))
                link(tt(hid_t[R, :], hid_g[R, :], hid_g[R, :], ALU.mult))
                link(ts(hid_t[R, :], hid_t[R, :], 0.044715, 1.0, ALU.mult, ALU.add))
                tt(hid_t[R, :], hid_t[R, :], hid_g[R, :], ALU.mult).then_inc(hid_exp_in, 1)

            def gelu_out():
                dve.wait_ge(hid_exp, 1)
                link(ts(hid_t[R, :], hid_t[R, :], 1.0, None, ALU.add))
                link(nc.vector.reciprocal(hid_t[R, :], hid_t[R, :]))
                tt(hid_g[R, :], hid_g[R, :], hid_t[R, :], ALU.mult).then_inc(hid_ready, 1)

            def keys_copy():
                dve.wait_ge(kcvc_psum, 1)
                cp(kcT[:, 0:NBLK], BANK[7][:, 64:64 + NBLK])
                cp(vc[0:NBLK, :], BANK[7][0:NBLK, P:2 * P]).then_inc(kcvc_ready, 1)

            def cmp_softmax_in():
                dve.wait_ge(cmp_scores, 1)
                for kv in range(2):
                    tt(v_blocks[:, 4 * kv:4 * kv + 4, :], BANK[7][:, HD * kv:HD * (kv + 1)].unsqueeze(1).to_broadcast([P, 4, HD]),
                       const("own_head")[:, 4 * kv:4 * kv + 4].unsqueeze(2).to_broadcast([P, 4, HD]), ALU.mult)
                link(nc.vector.memset(cmp_p, 0.0))
                big = const("cmp_big").rearrange("p (t n) -> p t n", t=T)[:, :, 0:NBLK].unsqueeze(2).to_broadcast([P, T, 4, NBLK])
                for kv in range(2):
                    sc = BANK[7 - kv][:, S:S + P].rearrange("p (t h n) -> p t h n", t=T, h=4)
                    i = tt(cmp_p[:, :, 4 * kv:4 * kv + 4, 0:NBLK], sc[:, :, :, 0:NBLK], big, ALU.add)
                link(i)
                link(nc.vector.tensor_reduce(cmp_m, cmp_p[:, :, :, 0:NBLK], AX, ALU.min))
                tt(cmp_p[:, :, :, 0:NBLK], cmp_p[:, :, :, 0:NBLK], cmp_m.unsqueeze(3).to_broadcast([P, T, 8, NBLK]), ALU.subtract).then_inc(cmp_exp_in, 1)

            def cmp_softmax_out():
                dve.wait_ge(cmp_exp, 1)
                seen = const("cmp_seen").rearrange("p (t n) -> p t n", t=T).unsqueeze(2).to_broadcast([P, T, 8, NC16])
                link(tt(cmp_p, cmp_p, seen, ALU.mult))
                link(nc.vector.reduce_sum(cmp_m, cmp_p, AX))
                link(ts(cmp_m, cmp_m, 1e-30, None, ALU.max))
                link(nc.vector.reciprocal(cmp_m, cmp_m))
                dve.wait_ge(gates_ready, 1)
                link(tt(cmp_m, cmp_m, pj[:, :, C_GA:C_GA + 24:3], ALU.mult))
                tt(cmp_p, cmp_p, cmp_m.unsqueeze(3).to_broadcast([P, T, 8, NC16]), ALU.mult).then_inc(cmp_probs, 1)

            attention(AB_JOBS, 0, 0, {1: gelu_in, 2: gelu_out, 4: keys_copy, 5: cmp_softmax_in, 7: cmp_softmax_out})
            residual(N_AB + 7, ALPHA)
            norm(0, 0, "layer", X)

            def first_max(vals, eq, m, onehot, w, n, tie):
                link(nc.vector.reduce_max(m, vals, AX))
                mb = m.unsqueeze(2).to_broadcast([P, T, n])
                link(tt(eq, vals, mb, ALU.is_equal))
                link(tt(eq, eq, tie, ALU.mult))
                link(nc.vector.reduce_max(w, eq, AX))
                return tt(onehot, eq, w.unsqueeze(2).to_broadcast([P, T, n]), ALU.is_equal)

            def expert_block(L, v, blk, unit, code, chunk, dst, y_done):
                E, F, ug, _ = MOE[L]
                for t in range(T):
                    i = ts(PG[:, t, :], const("iota"), code[t], None, ALU.is_equal)
                i.then_inc(v["p_ready"], 1)
                dve.wait_ge(v["xc_psum"], 2 * blk + 1)
                cp(cblk[:, 0:E], BANK[4][:, 0:E]).then_inc(v["c_ready"], 1)
                dve.wait_ge(v["xc_psum"], 2 * blk + 2)
                cp(xcT[:, 4:8, :], BANK[6][:, :].rearrange("p (k s) -> p k s", k=4)).then_inc(v["xc_dve"], 1)
                dve.wait_ge(v["c_ready"], blk + 1)
                for u in range(ug):
                    dve.wait_ge(v["silu_done"], unit + u + 1)
                    chunk(u)
                    if u >= 2:
                        dve.wait_ge(v["hT_psum"], unit + u - 1)
                    for e in range(CH // F):
                        c0, c1 = e * F, (e + 1) * F
                        ce = u * (CH // F) + e
                        i = stt(HB[u % 2][:, c0:c1], SG[u % 2][:, c0:c1], cblk[:, ce:ce + 1], BANK[2 + u % 2][:, c0:c1], ALU.mult, ALU.mult)
                    i.then_inc(v["h_ready"], 1)
                    dve.wait_ge(v["hT_psum"], unit + u + 1)
                    cp(HT[u % 2], BANK[4][:, :].rearrange("p (f s) -> p f s", f=4)).then_inc(v["hT_ready"], 1)
                y_done()
                cp(dst[0], BANK[5][:, :].rearrange("p (o d) -> p o d", o=1))
                cp(dst[1], BANK[6][:, :].rearrange("p (o d) -> p o d", o=1)).then_inc(v["y_copied"], 1)

            def moe(L, k, alpha):
                E, F, ug, NR = MOE[L]
                transpose_x(k)
                dve.wait_ge(logits_psum, L + 1)
                lg = rlog[:, 0:T * NR].rearrange("p (t n) -> p t n", t=T)
                bias = router_b[L].unsqueeze(1).to_broadcast([P, T, NR])
                link(tt(lg, BANK[0][:, 0:128].rearrange("p (t n) -> p t n", t=T)[:, :, 0:NR], bias, ALU.add))
                gm, wg = small_r[0][:, 0:T], small_r[0][:, 8:8 + T]
                gd = small_r[1][:, 0:T * G].rearrange("p (t g) -> p t g", t=T)
                oh = small_r[2][:, 0:T * G].rearrange("p (t g) -> p t g", t=T)
                eq = small_r[3].rearrange("p (t g) -> p t g", t=T)
                tie = const("descend").unsqueeze(1)
                i = first_max(lg[:, :, 0:G], eq[:, :, 0:G], gm, oh, small_r[4][:, 0:T], G, tie[:, :, 0:G].to_broadcast([P, T, G]))
                i.then_inc(onehot_ready, 1)
                dve.wait_ge(onehot_ready, L + 1)
                tt(gd, lg[:, :, 0:G], gm.unsqueeze(2).to_broadcast([P, T, G]), ALU.subtract).then_inc(rexp_in, 1)
                rtv = rt[:, 0:T * G * E].rearrange("p (t e g) -> p t e g", t=T, e=E)
                le = lg[:, :, G:NR].rearrange("p t (g e) -> p t e g", g=G)
                link(tt(rtv, le, oh.unsqueeze(2).to_broadcast([P, T, E, G]), ALU.mult))
                sel = small_r[5][:, 0:T * E].rearrange("p (t e) -> p t e", t=T)
                link(nc.vector.reduce_sum(sel, rtv, AX))
                oh1 = small_r[6][:, 0:T * E].rearrange("p (t e) -> p t e", t=T)
                oh2 = small_r[7][:, 0:T * E].rearrange("p (t e) -> p t e", t=T)
                v1, v2, dv = small_r[9][:, 0:T], small_r[10][:, 0:T], small_r[8][:, 0:T]
                w1, w2 = small_r[11][:, 0:T], small_r[12][:, 0:T]
                eqe = small_r[3][:, 0:T * E].rearrange("p (t e) -> p t e", t=T)
                tie_e = tie[:, :, 0:E].to_broadcast([P, T, E])
                link(first_max(sel, eqe, v1, oh1, small_r[4][:, 0:T], E, tie_e))
                link(stt(sel, oh1, -BIG, sel, ALU.mult, ALU.add))
                link(first_max(sel, eqe, v2, oh2, small_r[4][:, 0:T], E, tie_e))
                tt(dv, v2, v1, ALU.subtract).then_inc(rexp_in, 1)
                dve.wait_ge(rexp, 2 * L + 1)
                link(nc.vector.reduce_sum(wg, gd, AX))
                dve.wait_ge(rexp, 2 * L + 2)
                link(ts(w1, dv, 1.0, None, ALU.add))
                link(tt(w1, w1, wg, ALU.mult))
                link(nc.vector.reciprocal(w1, w1))
                link(tt(w2, w1, dv, ALU.mult))
                cwv = cw[:, 0:T * E].rearrange("p (t e) -> p t e", t=T)
                link(tt(oh1, oh1, w1.unsqueeze(2).to_broadcast([P, T, E]), ALU.mult))
                link(tt(oh2, oh2, w2.unsqueeze(2).to_broadcast([P, T, E]), ALU.mult))
                link(tt(cwv, oh1, oh2, ALU.add))
                dve.wait_ge(rank_psum, L + 1)
                rank = small_r[13].rearrange("p (w g) -> p w g", g=G)
                link(cp(rank[:, 0:3, :], BANK[1][:, 0:3 * G].rearrange("p (w g) -> p w g", g=G)))
                far = small_r[14][:, 0:T * G].rearrange("p (t g) -> p t g", t=T)
                link(ts(far, oh, -4096.0, 4096.0, ALU.mult, ALU.add))
                link(tt(rcode[:, :, 0:G], rank[:, 0:T, :], far, ALU.add))
                link(nc.vector.tensor_reduce(rcode[:, :, G], rcode[:, :, 0:G], AX, ALU.min))
                link(ts(rcode[:, :, G], rcode[:, :, G], float(P), None, ALU.subtract))
                link(ts(far[:, 0, :], rank[:, 2, :], float(P), None, ALU.is_gt))
                link(nc.vector.reduce_sum(over_f[:, 0:1], far[:, 0, :], AX))
                link(tt(far[:, 1, :], far[:, 0, :], const("group_no"), ALU.mult))
                link(nc.vector.reduce_sum(over_f[:, 1:2], far[:, 1, :], AX))
                cp(OVER_I[:, :], over_f).then_inc(over_ready, 1)
                units0, n0 = sum(UNITS[:L]), N_MOE[L]
                order = down_order(ug)
                with dve.Fori(0, G) as g:
                    def chunk(u):
                        dve.wait_ge(chunk_done, g * (3 * ug) + (n0 + order.index(("up", u)) + 1))

                    def y_done():
                        dve.wait_ge(chunk_done, g * (3 * ug) + (n0 + 3 * ug))

                    expert_block(L, main, g + G * L, g * ug + units0, [rcode[:, t, bass.ds(g, 1)] for t in range(T)], chunk,
                                 (yg[:, bass.ds(g, 1), 0:CH], yg[:, bass.ds(g, 1), CH:D]), y_done)
                v = over[L]
                dve.wait_ge(over_ready, L + 1)
                flag = dve.value_load(OVER_I[0:1, 0:1], min_val=0, max_val=G)
                with dve.If(flag > 0):
                    expert_block(L, v, 0, 0, [rcode[:, t, G:G + 1] for t in range(T)],
                                 lambda u: dve.wait_ge(v["chunk_done"], 3 * u + 2),
                                 (yo[:, 0:CH].rearrange("p (o d) -> p o d", o=1), yo[:, CH:D].rearrange("p (o d) -> p o d", o=1)),
                                 lambda: dve.wait_ge(v["chunk_done"], 3 * ug))
                    dve.wait_ge(v["scattered"], 1)
                    for t in range(T):
                        for half in range(2):
                            c = X[:, t, half * CH:(half + 1) * CH]
                            i = stt(c, BANK[t * 2 + half][:, :], 1.0 / alpha, c, ALU.mult, ALU.add)
                    i.then_inc(v["added"], 1)
                    dve.wait_ge(v["added"], 1)
                for t in range(T):
                    for half in range(2):
                        dve.wait_ge(scatter_psum, 4 * L + 2 * t + half + 1)
                        c = X[:, t, half * CH:(half + 1) * CH]
                        link(stt(c, c, alpha, BANK[t * 2 + half][:, :], ALU.mult, ALU.add))

            moe(0, 1, ALPHA)
            norm(1, 1, "layer", X)
            transpose_x(2)
            dve.wait_ge(proj_copied, 12)

            def sb_mask(h):
                dve.wait_ge(z_psum, h + 1)
                if h >= 4:
                    dve.wait_ge(w_log, h - 3)
                tt(ZM[h % 4], BANK[h % 2][:, 0:BL], const("strict"), ALU.add).then_inc(dve_step, 1)
                steps[0] += 1
                dve.wait_ge(dve_step, steps[0])
                stt(AN[h % 2], ZM[h % 4], -1.0, ZM[h % 4], ALU.mult, ALU.min).then_inc(z_abs, 1)

            def sb_softplus(h):
                dve.wait_ge(z_log, h + 1)
                if h >= 3:
                    dve.wait_ge(r_psum, h - 2)
                stt(SP_[h % 3], ZM[h % 4], 0.0, AN[h % 2], ALU.max, ALU.add).then_inc(sp_ready, 1)

            def sb_weight(h):
                dve.wait_ge(r_psum, h + 1)
                if h >= 2:
                    dve.wait_ge(w_ready, h - 1)
                tt(WL[h % 2], ZM[h % 4], BANK[2 + h % 2][:, 0:BL], ALU.add).then_inc(w_log, 1)

            for s in range(16 + 5):
                if s < 16:
                    sb_mask(s)
                if 0 <= s - 1 < 16:
                    sb_softplus(s - 1)
                if 0 <= s - 3 < 16:
                    sb_weight(s - 3)
                if s >= 5 and (s - 5) % 2:
                    h = s - 5
                    dve.wait_ge(sbo_psum, h + 1)
                    cp(mixT[:, h // 2, :], BANK[4 + (h // 2) % 2][:, 0:S]).then_inc(sbo_copied, 1)
            residual(N_SB + 6, ALPHA)
            norm(2, 2, "layer", X)
            moe(1, 3, ALPHA)
            norm(3, 3, "layer", X)
            norm(4, 4, "rms", U)
            transpose_x(4)

            def rope2(view):
                h = view.rearrange("p t (h d) -> p t h d", h=8)
                x1, x2 = h[:, :, :, 0:ROT], h[:, :, :, ROT:2 * ROT]
                c, s_ = (const(v).rearrange("p (t d) -> p t d", t=T).unsqueeze(2).to_broadcast([P, T, 8, ROT]) for v in ("cos2", "sin2"))
                m = [w[:, 0:T * 8 * ROT].rearrange("p (t h d) -> p t h d", t=T, h=8) for w in ROPE_TMP]
                tt(m[0], x1, c, ALU.mult)
                tt(m[1], x2, s_, ALU.mult)
                tt(m[2], x2, c, ALU.mult)
                link(tt(m[3], x1, s_, ALU.mult))
                tt(x1, m[0], m[1], ALU.subtract)
                return tt(x2, m[2], m[3], ALU.add)

            for m, view in enumerate((AQ, AK)):
                dve.wait_ge(proj_copied, 17 + m)
                rope2(view).then_inc(roped, 1)
                dve.wait_ge(roped, 6 + m)
            for r in range(2):
                dve.wait_ge(gz_psum, r + 1)
                link(cp(W0[:, 512 * r:512 * (r + 1)], BANK[r][:, :]))
            stt(W1, W0, -1.0, W0, ALU.mult, ALU.min).then_inc(gz_abs, 1)
            link(ts(W2, W0, 0.0, 1.0 / 16, ALU.min, ALU.mult))
            dve.wait_ge(gz_log, 1)
            stt(W3, W1, -1.0 / 16, W2, ALU.mult, ALU.add).then_inc(la_ready, 1)
            for r in range(2):
                dve.wait_ge(bt_psum, r + 1)
                i = cp(W0[:, 512 * r:512 * (r + 1)], BANK[2 + r][:, :])
            i.then_inc(bs_ready, 1)
            dve.wait_ge(eb_ready, 1)
            qd, ki, ke = by_key(W1), by_key(W2), by_key(W3)
            for r in range(2):
                first_ = GCH - 1 if r == 0 else 0
                link(cp(decay[:, r], qd[:, r, :, first_::GCH]))
            for n, w in enumerate((qd, ki, ke)):
                dve.wait_ge(eb_ready, n + 1)
                for r in range(2):
                    i = tt(w[:, r], w[:, r], gqT if n == 0 else gkT, ALU.mult)
                i.then_inc(qk_ready, 1)
            for b in range(2):
                dve.wait_ge(att_psum, b + 1)
                tt(att[:, 4 * b:4 * b + 4, :], BANK[b][:, :].rearrange("p (i s) -> p i s", s=P),
                   const("up_to").unsqueeze(1).to_broadcast([P, 4, P]), ALU.mult)
            dve.wait_ge(att_psum, 4)
            for b in range(2):
                i = tt(W2[:, 512 * b:512 * (b + 1)].rearrange("p (i s) -> p i s", s=P), BANK[2 + b][:, :].rearrange("p (i s) -> p i s", s=P),
                       const("from_on").unsqueeze(1).to_broadcast([P, 4, P]), ALU.mult)
            link(i)
            tt(W5, W5, W2, ALU.add).then_inc(att_ready, 1)
            dve.wait_ge(kv_psum, 2)
            dve.wait_ge(normed, 10)
            for sl in range(3):
                for r in range(2):
                    n = sl if r == 0 else 3 - sl
                    for k in range(2):
                        kvn = BANK[4 + 2 * r + n % 2][:, (n // 2) * S + k * P:(n // 2) * S + (k + 1) * P]
                        if sl == 0:
                            i = cp(state[:, r, k, 0, :], kvn)
                        else:
                            i = stt(state[:, r, k, sl, :], state[:, r, k, sl - 1, :], decay[:, r, k, n:n + 1], kvn, ALU.mult, ALU.add)
                if sl < 2:
                    link(i)
            i.then_inc(state_ready, 1)
            dve.wait_ge(silu_exp, 1)
            link(ts(W3, W3, 1.0, None, ALU.add))
            link(nc.vector.reciprocal(W3, W3))
            link(tt(by_tok2(W3), by_tok2(W3), GG, ALU.mult))
            w3h = W3.rearrange("p (i v) -> p i v", v=P)
            link(tt(w3h, w3h, gla_norm.unsqueeze(1).to_broadcast([P, 8, P]), ALU.mult))
            dve.wait_ge(go_square, 2)
            link(nc.vector.reduce_sum(go_ms, W2.rearrange("p (i v) -> p i v", v=P), AX))
            link(ts(go_ms, go_ms, 1.0 / P, RMS_EPS, ALU.mult, ALU.add))
            nc.vector.memset(go_n, 0.0).then_inc(var_ready, 1)
            dve.wait_ge(rstd_ready, 6)
            dve.wait_ge(var_ready, 6)
            sharpen(go_r, go_ms, go_n)
            w0h = W0.rearrange("p (i v) -> p i v", v=P)
            for t in range(T):
                for par in range(2):
                    i = tt(w0h[:, 4 * t + par:4 * t + 4:2, :], BANK[2 * t + par][:, 0:S].rearrange("p (i v) -> p i v", v=P),
                           go_r[:, 4 * t + par:4 * t + 4:2].unsqueeze(2).to_broadcast([P, 2, P]), ALU.mult)
            link(i)
            tt(W0, W0, W3, ALU.mult).then_inc(go_ready, 1)
            dve.wait_ge(go_ready, 1)
            dve.wait_ge(goT_ready, 1)
            attention(DIL_JOBS, len(AB_JOBS), 8, {})
            residual(N_2 + 7, 1.0)
            norm(5, 6, "rms", U)
            moe(2, 5, 1.0)
            norm(6, 7, "rms", X)


SMALL_TOTAL = 16 * (1 + 2 + 2 + NMOE * (1 + G + 2) + 4 + 1)
NORM_OF_XT = {1: 0, 2: 2, 3: 4, 4: 8, 5: 10}
NORM_VALUE = {0: 32, 1: 32, 2: 64, 3: 64, 4: 80, 5: 80, 6: 96}


def by_tok2(w):
    return w.rearrange("p (t n) -> p t n", t=T)


_INS = ["x", "positions", "ab_w_in", "ab_w_out", "nsa_cmp_pos_k", "nsa_cmp_pos_v", "nsa_cmp_w1_k", "nsa_cmp_w2_k",
        "nsa_cmp_w1_v", "nsa_cmp_w2_v", "sb_w_in", "sb_w_out", "ln_mix_g", "ln_mix_b", "ln_ffn_g", "ln_ffn_b",
        "moe_w_grp", "moe_b_grp", "moe_w_rt", "moe_b_rt", "moe_w_gate", "moe_w_up", "moe_w_down", "norm1_w_2",
        "w_in_2", "gla_fwd_gate_w_2", "gla_fwd_gate_b_2", "gla_bwd_gate_w_2", "gla_bwd_gate_b_2",
        "gla_norm_w_2", "w_out_2", "norm2_w_2", "router_group_w_2", "router_group_b_2", "router_expert_w_2",
        "router_expert_b_2", "expert_w_gate_2", "expert_w_up_2", "expert_w_down_2", "final_norm_w_2"]


def _launchable(nc, inputs):
    arrays, a = {}, {}
    for name in _INS:
        v = np.ascontiguousarray(inputs[name])
        arrays[f"in_{name}_dram"] = v
        a[name] = nc.dram_tensor(f"in_{name}_dram", v.shape, mybir.dt.from_np(v.dtype), kind="ExternalInput").ap()
    table = np.ascontiguousarray(np.concatenate([CONST[k] for k in CONST], 1))
    arrays["constants_dram"] = table
    a["constants"] = nc.dram_tensor("constants_dram", table.shape, F32, kind="ExternalInput").ap()
    out = nc.dram_tensor("out_dram", (1, S, D), F32, kind="ExternalOutput").ap()
    build(nc, a, out)
    return arrays


def kernel(**inputs):
    import concourse.bacc as bacc
    from concourse.bass_utils import run_bass_kernel_spmd
    nc = bacc.Bacc("TRN2", target_bir_lowering=False, num_devices=1, dynamic_dma_scratch_size=1024)
    arrays = _launchable(nc, inputs)
    r = run_bass_kernel_spmd(nc, [arrays], core_ids=[0])
    return r.results[0]["out_dram"]
```

```python
import numpy as np
import concourse.bass as bass
from concourse import mybir
from concourse.alu_op_type import AluOpType as ALU
from contextlib import ExitStack

F32 = mybir.dt.float32
I32 = mybir.dt.int32
ACT = mybir.ActivationFunctionType
AX = mybir.AxisListType.X

P = 128
S = 256
T = S // P
D = 1024
KT = D // P
HD = 64
HALF = HD // 2
CH = 512
SLOT = 4096
NSLOT = 6
BIG = 1e30
ALPHA = float((2 * 2) ** 0.25)
LN_EPS = 1e-5
RMS_EPS = 1e-6
SCALE = HD ** -0.5

CMP_STRIDE = 16
NBLK = (S - 32) // CMP_STRIDE + 1
NC16 = S // CMP_STRIDE

NQ = 512
C_KC, C_VC, C_KS, C_VS, C_KW, C_VW, C_GA, C_QM, C_KM, C_VM = (
    512, 640, 768, 896, 1024, 1152, 1280, 1304, 1816, 2328)
W_AB = 2840
C_GV, C_GG, C_LF, C_LB, C_AQ, C_AK, C_AV = 512, 1024, 1536, 1552, 1568, 2080, 2592
W_2 = 3104
RANK = 16
GCH = 64
ROT = 8

MOE = [(4, 256, 2, 20), (4, 256, 2, 20), (8, 512, 8, 36)]
G = 4
CAP = 64
NMOE = len(MOE)


def _constants():
    j = np.arange(P)[:, None]
    i = np.arange(P)[None, :]
    t = np.arange(S)
    tok = np.arange(P)[:, None] + P * np.arange(T)[None, :]
    same = (j // GCH) == (i // GCH)
    z = np.zeros((P, P))
    c = {}
    c["ident"] = np.eye(P)
    tri = np.where(i > j, BIG, 0.0)
    c["inv_freq"] = np.broadcast_to(
        (np.float32(10000.0) ** (-np.arange(HALF, dtype=np.float32) / np.float32(HALF)))[None, :], (P, HALF))
    c["causal"] = np.concatenate([tri, z, tri], 1)
    st = np.where(j < i, 0.0, -BIG)
    c["strict"] = np.concatenate([st, z, st], 1)
    c["neg_suffix"] = np.where(j >= i, -1.0, 0.0)
    c["neg_ones"] = np.full((P, P), -1.0)
    c["ones"] = np.full((P, P), 1.0)
    c["before"] = np.where(j < i, 1.0, 0.0)
    c["up_to"] = np.where(same & (j <= i), 1.0, 0.0)
    c["from_on"] = np.where(same & (j >= i), 1.0, 0.0)
    n = np.arange(NC16)
    seen = (n[None, None, :] * CMP_STRIDE + 31 <= tok[:, :, None]) & (n < NBLK)[None, None, :]
    c["cmp_big"] = np.where(seen, 0.0, BIG).reshape(P, T * NC16)
    c["cmp_seen"] = np.where(seen, 1.0, 0.0).reshape(P, T * NC16)
    c["own_head"] = np.where(j // NC16 == np.arange(8)[None, :], 1.0, 0.0)
    c["spread"] = np.where((j < NC16) & (i % NC16 == j), 1.0, 0.0)
    c["iota"] = np.broadcast_to(i, (P, P))
    c["descend"] = np.broadcast_to(8.0 - np.arange(8)[None, :], (P, 8))
    inv2 = np.float32(500000.0) ** (-(np.arange(0, 2 * ROT, 2, dtype=np.float32) / np.float32(2 * ROT)))
    ang = tok[:, :, None].astype(np.float32) * inv2[None, None, :].astype(np.float32)
    c["cos2"] = np.cos(ang).reshape(P, T * ROT)
    c["sin2"] = np.sin(ang).reshape(P, T * ROT)
    d = np.abs(tok[:, :, None] - t[None, None, :])
    count = (d <= 64).astype(float) + (d % 4 == 0) + (d % 16 == 0)
    c["count"] = count.reshape(P, T * S)
    c["unseen"] = np.where(count > 0, 0.0, BIG).reshape(P, T * S)
    return {k: np.ascontiguousarray(v, dtype=np.float32) for k, v in c.items()}


CONST = _constants()
CONST_AT = {}
_at = 0
for _k, _v in CONST.items():
    CONST_AT[_k] = (_at, _v.shape[1])
    _at += _v.shape[1]
CONST_W = _at
FIRST_CONSTS = P + HALF


UNITS = [m[2] // 2 for m in MOE]
PAIRS = [m[0] // 2 for m in MOE]
GATHERS = [KT * m[0] * CAP // CH for m in MOE]
N_AB = 0
CMP_CHUNK = 6
N_M0 = N_AB + 9
N_SB = N_M0 + 6 * G * UNITS[0]
N_M1 = N_SB + 8
N_2 = N_M1 + 6 * G * UNITS[1]
N_M2 = N_2 + 9
N_END = N_M2 + 6 * G * UNITS[2]
N_MOE = [N_M0, N_M1, N_M2]
CMP_DMAS = 4


def loaded_value(n):
    v = 16 * (n // NSLOT + 1)
    if n >= CMP_CHUNK and (n - CMP_CHUNK) % NSLOT == 0:
        v += 16 * (CMP_DMAS - 1)
    return v


def expert_order(units):
    order = []
    for u in range(units):
        order += [("gate", u), ("up", u)]
        if u:
            order.append(("down", u - 1))
    return order + [("down", units - 1)]


def first_chunk(units, kind, u):
    return 2 * expert_order(units).index((kind, u))


AB_JOBS = [("moba", h) for h in range(8)]
for _i in range(4):
    AB_JOBS += [("slc", 2 * _i), ("slc", 2 * _i + 1), ("win", 2 * _i), ("win", 2 * _i + 1)]
DIL_JOBS = [("dil", h) for h in range(8)]


def job_pair(job):
    kind, h = job
    return h // 2 + (4 if kind in ("slc", "win") else 0)


def job_tile(job):
    kind, h = job
    return h // 2 + (0 if kind in ("slc", "win") else 4)


def last_of_pair(jobs, j):
    return j + 1 == len(jobs) or job_pair(jobs[j + 1]) != job_pair(jobs[j])


def first_of_pair(jobs, j):
    return j == 0 or job_pair(jobs[j - 1]) != job_pair(jobs[j])


def build(nc, a, out):
    ctx = ExitStack()
    with ctx:
        def sb(name, cols, dt=F32):
            return ctx.enter_context(nc.sbuf_tensor(name, [P, cols], dt))

        def sem(name):
            return ctx.enter_context(nc.semaphore(name))

        WEIGHTS = sb("weights", NSLOT * SLOT)
        CONSTS = sb("consts", CONST_W)
        X_ = sb("residual", T * D)
        XT_ = sb("x_transposed", KT * S)
        MIX = sb("mixed", T * D)
        NORM_ = sb("norm_params", 2 * 2 * D)
        PJ = sb("projected", 6208)
        QK = sb("heads_transposed", 14 * S)
        WK = sb("work", 4352)
        SMALL = sb("small_params", 2000)
        MISC = sb("misc", 2200)
        GATE_W = sb("gla_gate_w", 2 * S)
        POS_I = sb("positions", T, I32)
        OVER_I = sb("overflow", 1, I32)
        BANK = [ctx.enter_context(nc.psum_tensor(f"bank{i}", [P, CH], F32)) for i in range(8)]

        def const(name):
            o, n = CONST_AT[name]
            return CONSTS[:, o:o + n]

        ident = const("ident")
        X = X_[:, :].rearrange("p (t d) -> p t d", t=T)
        XT = XT_[:, :].rearrange("p (k s) -> p k s", k=KT)
        mixT = MIX[:, :].rearrange("p (k s) -> p k s", k=KT)
        U = MIX[:, :].rearrange("p (t d) -> p t d", t=T)
        NORM = NORM_[:, :].rearrange("p (b w d) -> p b w d", b=2, w=2)

        def slot(n):
            return WEIGHTS[:, (n % NSLOT) * SLOT:(n % NSLOT + 1) * SLOT]

        small_at = [0]

        def small(n):
            small_at[0] += n
            assert small_at[0] <= 2000
            return SMALL[:, small_at[0] - n:small_at[0]]

        misc_at = [0]

        def misc(n):
            misc_at[0] += n
            assert misc_at[0] <= 2200
            return MISC[:, misc_at[0] - n:misc_at[0]]

        router_w = [small(KT * m[3]).rearrange("p (k n) -> p k n", k=KT) for m in MOE]
        router_b = [small(m[3]) for m in MOE]
        cmp_w2 = small(2 * HD).rearrange("p (v d) -> p v d", v=2)
        cmp_pos = small(2 * P).rearrange("p (v d) -> p v d", v=2)
        gla_norm = small(P)

        cos1, sin1, angle, turns = (misc(T * HALF) for _ in range(4))
        pos_f = misc(T)
        cmp_posT = misc(2 * NC16).rearrange("p (v c) -> p v c", v=2)
        stats = misc(T * 12).rearrange("p (t w) -> p t w", t=T)
        mean_var = misc(T * 2).rearrange("p (t w) -> p t w", t=T)
        veps, lnv, rstd, newton = (misc(8) for _ in range(4))
        least = misc(8).rearrange("p (b t) -> p b t", b=4)
        psums = misc(8).rearrange("p (b t) -> p b t", b=4)
        rinv = misc(8).rearrange("p (b t) -> p b t", b=4)

        slot_loaded = [sem(f"slot{i}_loaded") for i in range(NSLOT)]
        x_loaded = sem("x_loaded")
        first_consts_loaded = sem("first_consts_loaded")
        consts_loaded = sem("consts_loaded")
        positions_loaded = sem("positions_loaded")
        cmp_small_loaded = sem("cmp_small_loaded")
        small_loaded = sem("small_loaded")
        norm_loaded = [sem("norm0_loaded"), sem("norm1_loaded")]
        chunk_done = sem("chunk_done")
        xt_psum = sem("xt_psum")
        xt_act = sem("xt_act")
        xt_dve = sem("xt_dve")
        proj_copied = sem("proj_copied")
        roped = sem("roped")
        qt_psum = sem("qt_psum")
        qt_act = sem("qt_act")
        kv2_ready = sem("kv2_ready")
        angle_ready = sem("angle_ready")
        sines_ready = sem("sines_ready")
        gates_exp = sem("gates_exp")
        gates_ready = sem("gates_ready")
        dve_step = sem("dve_step")
        act_step = sem("act_step")
        pool_step = sem("pool_step")
        pos_psum = sem("pos_psum")
        pos_ready = sem("pos_ready")
        hid_exp_in = sem("hid_exp_in")
        hid_exp = sem("hid_exp")
        hid_ready = sem("hid_ready")
        hidT_psum = sem("hidT_psum")
        hidT_ready = sem("hidT_ready")
        kcvc_psum = sem("kcvc_psum")
        kcvc_ready = sem("kcvc_ready")
        cmp_scores = sem("cmp_scores")
        cmp_exp_in = sem("cmp_exp_in")
        cmp_exp = sem("cmp_exp")
        cmp_probs = sem("cmp_probs")
        cmp_pT_psum = sem("cmp_pT_psum")
        cmp_pT = sem("cmp_pT")
        scores_ready = sem("scores_ready")
        mins_ready = sem("mins_ready")
        probs_ready = sem("probs_ready")
        rinv_ready = sem("rinv_ready")
        diag_ready = sem("diag_ready")
        pt_psum = sem("pt_psum")
        pt_copied = sem("pt_copied")
        pv_done = sem("pv_done")
        o_copied = sem("o_copied")
        var_ready = sem("var_ready")
        rstd_ready = sem("rstd_ready")
        normed = sem("normed")
        logits_psum = sem("logits_psum")
        rexp_in = sem("rexp_in")
        rexp = sem("rexp")
        onehot_ready = sem("onehot_ready")
        rank_psum = sem("rank_psum")
        place_ready = sem("place_ready")
        over_ready = sem("over_ready")
        z_psum = sem("z_psum")
        z_abs = sem("z_abs")
        z_log = sem("z_log")
        sp_ready = sem("sp_ready")
        r_psum = sem("r_psum")
        w_log = sem("w_log")
        w_ready = sem("w_ready")
        sbo_psum = sem("sbo_psum")
        sbo_copied = sem("sbo_copied")
        gz_psum = sem("gz_psum")
        gz_abs = sem("gz_abs")
        gz_log = sem("gz_log")
        la_ready = sem("la_ready")
        bt_psum = sem("bt_psum")
        bs_ready = sem("bs_ready")
        eb_ready = sem("eb_ready")
        qk_ready = sem("qk_ready")
        ket_psum = sem("ket_psum")
        ket_ready = sem("ket_ready")
        att_psum = sem("att_psum")
        att_ready = sem("att_ready")
        kv_psum = sem("kv_psum")
        state_ready = sem("state_ready")
        go_psum = sem("go_psum")
        go_square = sem("go_square")
        go_ready = sem("go_ready")
        goT_psum = sem("goT_psum")
        goT_ready = sem("goT_ready")
        silu_exp = sem("silu_exp")
        out_stored = sem("out_stored")

        p_ready = sem("p_ready")
        pwT_psum = sem("pwT_psum")
        pwT_act = sem("pwT_act")
        pwT_dve = sem("pwT_dve")
        xc_psum = sem("xc_psum")
        xc_act = sem("xc_act")
        xc_dve = sem("xc_dve")
        silu_done = sem("silu_done")
        h_ready = sem("h_ready")
        hT_psum = sem("hT_psum")
        hT_ready = sem("hT_ready")
        y_psum = sem("y_psum")
        y_act = sem("y_act")
        y_dve = sem("y_dve")
        acc_ready = sem("acc_ready")
        GENERAL_SIGNALS = ("loaded", "psum", "silu_done", "h_ready", "hT_ready", "added")
        general = [{k: sem(f"general{L}_" + k) for k in GENERAL_SIGNALS} for L in range(NMOE)]

        pj = PJ[:, 0:T * W_AB].rearrange("p (t n) -> p t n", t=T)
        qk = QK[:, :].rearrange("p (n s) -> p n s", s=S)
        kv2 = MIX[:, 0:4 * S].rearrange("p (v h s) -> p v h s", v=2, h=2)
        ROPE_TMP = [WK[:, 512 * i:512 * (i + 1)] for i in range(4)]
        SM = [WK[:, 512 * i:512 * (i + 1)] for i in range(2)]
        PR = [WK[:, 1024 + 512 * i:1024 + 512 * (i + 1)] for i in range(3)]
        PTS = [WK[:, 2560 + 512 * i:2560 + 512 * (i + 1)] for i in range(2)]
        DIAG = [WK[:, 3584 + 256 * i:3584 + 256 * (i + 1)].rearrange("p (t s) -> p t s", t=T) for i in range(3)]

        hid_g = misc(2 * P)
        hid_t = misc(2 * P)
        hidT = misc(2 * 32).rearrange("p (v n) -> p v n", v=2)
        kcT = misc(NC16)
        vc = misc(P)
        v_blocks = PJ[:, 5680:5680 + 512].rearrange("p (h d) -> p h d", h=8)
        cmp_p = hid_g.rearrange("p (t h n) -> p t h n", t=T, h=8)
        cmp_m = misc(16).rearrange("p (t h) -> p t h", t=T)
        cmp_pT_sb = misc(S)

        def heads(view, col, n):
            return view[:, :, col:col + n * HD].rearrange("p t (h x d) -> p t h x d", x=2, d=HALF)

        def job_operands(job):
            kind, h = job
            if kind == "moba":
                r = HD * (h % 2)
                return qk[r:r + HD, 6 + h // 2, :], qk[r:r + HD, 10 + h // 2, :], pj[:, :, C_VM + HD * h:C_VM + HD * h + HD], None
            if kind == "dil":
                r = HD * (h % 2)
                return qk[r:r + HD, h // 2, :], qk[r:r + HD, 4 + h // 2, :], AV[:, :, HD * h:HD * h + HD], None
            kv = h // 4
            r = HD * kv
            k, v, gate = (4, C_VS, 1) if kind == "slc" else (5, C_VW, 2)
            return qk[r:r + HD, h % 4, :], qk[r:r + HD, k, :], pj[:, :, v + HD * kv:v + HD * kv + HD], pj[:, :, C_GA + 3 * h + gate]

        sbQ = PJ[:, 0:8 * S].rearrange("p (n s) -> p n s", s=S)
        sbK = PJ[:, 8 * S:16 * S].rearrange("p (n s) -> p n s", s=S)
        sbV = PJ[:, 16 * S:16 * S + T * D].rearrange("p (t n) -> p t n", t=T)
        BL = 3 * P
        ZM = [QK[:, BL * i:BL * (i + 1)] for i in range(4)]
        WT = [QK[:, BL * (4 + i):BL * (5 + i)] for i in range(3)]
        AN = [WK[:, BL * i:BL * (i + 1)] for i in range(2)]
        SP_ = [WK[:, BL * (2 + i):BL * (3 + i)] for i in range(3)]
        WL = [WK[:, BL * (5 + i):BL * (6 + i)] for i in range(2)]

        GV, GG, AQ, AK, AV = (PJ[:, 1024 * i:1024 * (i + 1)].rearrange("p (t n) -> p t n", t=T) for i in range(5))
        W5 = PJ[:, 5120:6144]
        gqT, gkT = qk[:, 8:10, :], qk[:, 10:12, :]
        LR = QK[:, 12 * S:14 * S].rearrange("p (r s) -> p r s", r=2)
        W0, W1, W2, W3 = (WK[:, 1024 * i:1024 * (i + 1)] for i in range(4))
        by_tok = lambda w: w.rearrange("p (r t n) -> p r t n", r=2, t=T)
        by_key = lambda w: w.rearrange("p (r k s) -> p r k s", r=2, k=2)
        gw = GATE_W[:, :].rearrange("p (r n) -> p r n", r=2)
        decay = misc(16).rearrange("p (r k n) -> p r k n", r=2, k=2)
        state = MIX[:, 0:1536].rearrange("p (r k n v) -> p r k n v", r=2, k=2, n=3)
        att = W5.rearrange("p (i s) -> p i s", s=P)
        go_ms = misc(8)
        go_r = misc(8)
        go_l = misc(8)
        go_n = misc(8)

        xcT = PJ[:, 0:KT * 8 * CAP]
        PB, PW = QK[:, 0:1024], QK[:, 1024:2048]
        PWT = QK[:, 2048:3072].rearrange("p (a s) -> p a s", a=4)
        SG, HB = WK[:, 0:512], WK[:, 512:1024]
        HT = WK[:, 1024:1536].rearrange("p (f s) -> p f s", f=4)
        YS = WK[:, 1536:3584].rearrange("p (a h d) -> p a h d", a=2, h=2)
        work_at = [3584]

        def work(n):
            work_at[0] += n
            assert work_at[0] <= 4352
            return WK[:, work_at[0] - n:work_at[0]]

        rlog = work(T * 36)
        rt = work(T * 32)
        small_r = [work(16) for i in range(14)]
        chosen_, weight_, left_ = (work(T * 32) for _ in range(3))
        place_, weight_by_place_ = (misc(T * 32) for _ in range(2))
        over_f = misc(2)

        W_NCOLS = [512, 512, 280, 512, 512, 512]
        W_COL0 = [0, 512, 1024, 1304, 1816, 2328]
        W2_NCOLS = [512, 512, 512, 32, 512, 512, 512]
        W2_COL0 = [0, 512, 1024, 1536, 1568, 2080, 2592]

        block = ctx.enter_context(nc.Block())

        @block.sync
        def _(sp):
            def free_slot(n):
                if n >= NSLOT:
                    sp.wait_ge(chunk_done, n - NSLOT + 1)

            def load_cols(n, w, col, ncols):
                free_slot(n)
                sp.dma_start(slot(n)[:, 0:KT * ncols].rearrange("p (k c) -> p k c", k=KT),
                             w.rearrange("(p k) c -> p k c", k=KT)[:, :, col:col + ncols]).then_inc(slot_loaded[n % NSLOT], 16)

            def load_out(n, w, half):
                free_slot(n)
                sp.dma_start(slot(n).rearrange("p (k c) -> p k c", k=KT),
                             w.rearrange("(k p) c -> p k c", p=P)[:, :, half * CH:(half + 1) * CH]).then_inc(slot_loaded[n % NSLOT], 16)

            def load_norm(k, params):
                if k >= 2:
                    sp.wait_ge(normed, 2 * (k - 1))
                for i, v in enumerate(params):
                    sp.dma_start(NORM[:, k % 2, i, :], v.partition_broadcast(P)).then_inc(norm_loaded[k % 2], 16)

            def expert_source(L, kind, e):
                name = ("moe_w_", "moe_w_", "expert_w_")[L] + kind + ("", "", "_2")[L]
                w = a[name][L if L < 2 else 0]
                if MOE[L][1] == CH:
                    w = w[bass.ds(e, 1)]
                    if kind == "down":
                        return w.rearrange("a (p f) d -> p (a f d)", p=P)
                    return w.rearrange("a (p k) f -> p (a k f)", p=P)
                w = w[bass.ds(e * 2, 2)]
                if kind == "down":
                    return w.rearrange("a (p f) d -> p a (f d)", p=P)
                return w.rearrange("a (p k) f -> p a (k f)", p=P)

            def unit_slot(L, n):
                return slot(n) if MOE[L][1] == CH else slot(n).rearrange("p (a w) -> p a w", a=2)

            def moe(L):
                n0, units = N_MOE[L], UNITS[L]
                per_group = 6 * units
                with sp.Fori(0, G) as g:
                    for j in range(per_group):
                        kind, u = expert_order(units)[j // 2]
                        n = n0 + j
                        sp.wait_ge(chunk_done, g * per_group + (n - NSLOT + 1))
                        sp.dma_start(unit_slot(L, n), expert_source(L, kind, g * (2 * units) + (2 * u + j % 2))
                                     ).then_inc(slot_loaded[n % NSLOT], 16)
                v = general[L]
                sp.wait_ge(over_ready, L + 1)
                flag = sp.value_load(OVER_I[0:1, 0:1], min_val=0, max_val=1)
                with sp.If(flag > 0):
                    sp.wait_ge(chunk_done, n0 + G * per_group)
                    with sp.Fori(0, G * 2 * units) as n:
                        sp.wait_ge(v["added"], n * 2 + 1)
                        for i, kind in enumerate(("gate", "up", "down")):
                            sp.dma_start(unit_slot(L, i), expert_source(L, kind, n)).then_inc(v["loaded"], 16)
                    sp.wait_ge(v["added"], 2 * G * 2 * units + 1)

            x_src = a["x"][0].rearrange("(t p) d -> p t d", p=P)
            for t in range(T):
                sp.dma_start(X[:, t, :], x_src[:, t, :]).then_inc(x_loaded, 16)
            w = a["ab_w_in"][0]
            for c in range(6):
                load_cols(N_AB + c, w, W_COL0[c], W_NCOLS[c])
            free_slot(CMP_CHUNK)
            cslot = slot(CMP_CHUNK).rearrange("p (v c n) -> p v c n", v=2, c=NC16)
            for i, name in enumerate(("nsa_cmp_w1_k", "nsa_cmp_w1_v")):
                for h in range(2):
                    sp.dma_start(cslot[HD * h:HD * h + HD, i, :, :],
                                 a[name][0][h * 1024:(h + 1) * 1024, :].rearrange("(c d) n -> d c n", d=HD)
                                 ).then_inc(slot_loaded[CMP_CHUNK % NSLOT], 16)
            load_norm(0, (a["ln_mix_g"][0], a["ln_mix_b"][0]))
            for half in range(2):
                load_out(N_AB + 7 + half, a["ab_w_out"][0], half)
            moe(0)
            load_norm(1, (a["ln_ffn_g"][0], a["ln_ffn_b"][0]))
            for c in range(6):
                load_cols(N_SB + c, a["sb_w_in"][0], c * CH, CH)
            load_norm(2, (a["ln_mix_g"][1], a["ln_mix_b"][1]))
            for half in range(2):
                load_out(N_SB + 6 + half, a["sb_w_out"][0], half)
            moe(1)
            load_norm(3, (a["ln_ffn_g"][1], a["ln_ffn_b"][1]))
            load_norm(4, (a["norm1_w_2"][0],))
            for c in range(7):
                load_cols(N_2 + c, a["w_in_2"][0], W2_COL0[c], W2_NCOLS[c])
            load_norm(5, (a["norm2_w_2"][0],))
            for half in range(2):
                load_out(N_2 + 7 + half, a["w_out_2"][0], half)
            moe(2)
            load_norm(6, (a["final_norm_w_2"],))
            o = out[0].rearrange("(t p) d -> p t d", p=P)
            for t in range(T):
                sp.wait_ge(normed, 12 + t + 1)
                sp.dma_start(o[:, t, :], X[:, t, :]).then_inc(out_stored, 16)
            sp.wait_ge(out_stored, 16 * T)

        @block.gpsimd
        def _(pool):
            def diagonals(jobs, first):
                for j, job in enumerate(jobs):
                    J = first + j
                    gate = job_operands(job)[3]
                    pool.wait_ge(rinv_ready, J + 1)
                    if J >= 3:
                        pool.wait_ge(pt_psum, J - 2)
                    for t in range(T):
                        if gate is None:
                            i = nc.gpsimd.tensor_scalar(DIAG[J % 3][:, t, :], ident, rinv[:, J % 4, t:t + 1], None, ALU.mult)
                        else:
                            if first == 0 and j == 8 and t == 0:
                                pool.wait_ge(gates_ready, 1)
                            i = nc.gpsimd.tensor_scalar(DIAG[J % 3][:, t, :], ident, rinv[:, J % 4, t:t + 1], gate[:, t:t + 1], ALU.mult, ALU.mult)
                    i.then_inc(diag_ready, 1)

            pool.wait_ge(consts_loaded, 16)
            diagonals(AB_JOBS, 0)
            pool.wait_ge(normed, 10)
            nc.gpsimd.memset(LR[0:RANK + 1, :, :], 1.0).then_inc(pool_step, 1)
            diagonals(DIL_JOBS, len(AB_JOBS))

        @block.tensor
        def _(pe):
            mm = nc.tensor.matmul

            def chunk_loaded(n):
                pe.wait_ge(slot_loaded[n % NSLOT], loaded_value(n))

            def transpose_x(k, src, waits):
                for t in range(T):
                    waits(t)
                    for kt in range(KT):
                        i = nc.tensor.transpose(BANK[kt // 2][:, (kt % 2) * S + t * P:(kt % 2) * S + (t + 1) * P],
                                                src[:, t, kt::KT], ident)
                        if t == T - 1 and kt % 2:
                            i.then_inc(xt_psum, 1)
                pe.wait_ge(xt_act, 2 * k + 2)
                pe.wait_ge(xt_dve, 2 * k + 2)

            def project(n, ncols, seq):
                if seq >= 2:
                    pe.wait_ge(proj_copied, seq - 1)
                chunk_loaded(n)
                w = slot(n)[:, 0:KT * ncols].rearrange("p (k c) -> p k c", k=KT)
                for t in range(T):
                    for kt in range(KT):
                        i = mm(BANK[4 + 2 * (seq % 2) + t][:, 0:ncols], XT[:, kt, t * P:(t + 1) * P], w[:, kt, :],
                               start=kt == 0, stop=kt == KT - 1)
                i.then_inc(chunk_done, 1)

            def project_T(n, seq, tiles, width=P):
                if seq >= 2:
                    pe.wait_ge(proj_copied, seq - 1)
                chunk_loaded(n)
                w = slot(n)[:, 0:KT * tiles * width].rearrange("p (k c) -> p k c", k=KT)
                for c in range(tiles):
                    for kt in range(KT):
                        i = mm(BANK[4 + 2 * (seq % 2) + c // 2][0:width, (c % 2) * S:(c % 2 + 1) * S],
                               w[:, kt, c * width:(c + 1) * width], XT[:, kt, :], start=kt == 0, stop=kt == KT - 1)
                i.then_inc(chunk_done, 1)

            def project_out(n):
                for half in range(2):
                    chunk_loaded(n + half)
                    w = slot(n + half).rearrange("p (k c) -> p k c", k=KT)
                    for t in range(T):
                        for kt in range(KT):
                            i = mm(BANK[4 + 2 * half + t][:, :], mixT[:, kt, t * P:(t + 1) * P], w[:, kt, :],
                                   start=kt == 0, stop=kt == KT - 1)
                    i.then_inc(chunk_done, 1)

            def attention(jobs, first, pairs0, extras):
                dil = jobs[0][0] == "dil"

                def scores(j):
                    J = first + j
                    q, k, _, _ = job_operands(jobs[j])
                    if J >= 2:
                        pe.wait_ge(mins_ready, J - 1)
                    if dil:
                        for t in range(T):
                            i = mm(BANK[J % 2][:, t * S:(t + 1) * S], q[:, t * P:(t + 1) * P], k, start=True, stop=True)
                    else:
                        mm(BANK[J % 2][:, 0:P], q[:, 0:P], k[:, 0:P], start=True, stop=True)
                        i = mm(BANK[J % 2][:, P:3 * P], q[:, P:S], k, start=True, stop=True)
                    i.then_inc(scores_ready, 1)

                def transposed(j):
                    J = first + j
                    pe.wait_ge(probs_ready, J + 1)
                    pe.wait_ge(diag_ready, J + 1)
                    if J >= 2:
                        pe.wait_ge(pt_copied, J - 1)
                    pr, dg, b = PR[J % 3], DIAG[J % 3], BANK[2 + J % 2]
                    if dil:
                        for kt in range(T):
                            for t in range(T):
                                i = mm(b[:, kt * S + t * P:kt * S + (t + 1) * P], pr[:, t * S + kt * P:t * S + (kt + 1) * P],
                                       dg[:, t, :], start=True, stop=True)
                    else:
                        for blk, t in enumerate((0, 1, 1)):
                            i = mm(b[:, blk * P:(blk + 1) * P], pr[:, blk * P:(blk + 1) * P], dg[:, t, :], start=True, stop=True)
                    i.then_inc(pt_psum, 1)

                def values(j):
                    J = first + j
                    kind, h = jobs[j]
                    pair = job_pair(jobs[j]) + pairs0
                    if dil:
                        pair = jobs[j][1] // 2 + pairs0
                    ob = BANK[4 + pair % 2]
                    if first_of_pair(jobs, j) and pair >= 2:
                        pe.wait_ge(o_copied, pair - 1)
                    gated = kind in ("slc", "win")
                    if gated and first_of_pair(jobs, j):
                        if h == 0:
                            pe.wait_ge(cmp_pT, 1)
                        mm(ob[:, 0:S], v_blocks[:, h:h + 2, :], cmp_pT_sb, start=True, stop=False)
                    pe.wait_ge(pt_copied, J + 1)
                    _, _, v, _ = job_operands(jobs[j])
                    r = HD * (h % 2)
                    last = not gated or (kind == "win")
                    if dil:
                        mm(ob[r:r + HD, 0:S], v[:, 0, :], PTS[J % 2][:, 0:S], start=True, stop=False)
                        i = mm(ob[r:r + HD, 0:S], v[:, 1, :], PTS[J % 2][:, S:2 * S], start=False, stop=True)
                    else:
                        mm(ob[r:r + HD, 0:S], v[:, 0, :], PTS[J % 2][:, 0:S], start=not gated, stop=False)
                        i = mm(ob[r:r + HD, P:S], v[:, 1, :], PTS[J % 2][:, S:3 * P], start=False, stop=last)
                    i.then_inc(pv_done, 1)

                for s in range(len(jobs) + 3):
                    if s < len(jobs):
                        scores(s)
                    if s in extras:
                        extras[s]()
                    if 0 <= s - 2 < len(jobs):
                        transposed(s - 2)
                    if s >= 3:
                        values(s - 3)

            pe.wait_ge(first_consts_loaded, 16)
            transpose_x(0, X, lambda t: pe.wait_ge(x_loaded, 16 * T) if t == 0 else None)

            def tr(k, aps):
                if k >= 4:
                    for s_, v in {4: [(qt_act, 1)], 5: [(qt_act, 2)], 6: [(kv2_ready, 1)], 7: [(kv2_ready, 2)], 8: [(qt_act, 3)]}[k]:
                        pe.wait_ge(s_, v)
                for n, ap in enumerate(aps):
                    i = nc.tensor.transpose(BANK[k % 4][:, n * P:(n + 1) * P], ap, ident)
                i.then_inc(qt_psum, 1)

            project(0, 512, 0)
            project(1, 512, 1)
            pe.wait_ge(cmp_small_loaded, 64)
            for v in range(2):
                i = nc.tensor.transpose(BANK[3][:, v * NC16:(v + 1) * NC16], cmp_pos[0:NC16, v, :], ident[0:NC16, 0:NC16])
            i.then_inc(pos_psum, 1)
            pe.wait_ge(roped, 1)
            for k in range(2):
                tr(k, [pj[:, t, P * j:P * (j + 1)] for j in (2 * k, 2 * k + 1) for t in range(T)])
            project(2, 280, 2)
            pe.wait_ge(roped, 2)
            pe.wait_ge(pos_ready, 1)
            tr(2, [pj[:, t, c:c + P] for c in (C_KS, C_KC) for t in range(T)])
            tr(3, [pj[:, t, C_VC:C_VC + P] for t in range(T)])
            project(3, 512, 3)
            pe.wait_ge(roped, 3)
            tr(4, [pj[:, t, C_KW:C_KW + P] for t in range(T)])
            project(4, 512, 4)
            pe.wait_ge(roped, 4)
            for k in range(2):
                tr(5 + k, [pj[:, t, C_QM + P * j:C_QM + P * (j + 1)] for j in (2 * k, 2 * k + 1) for t in range(T)])
            project(5, 512, 5)
            pe.wait_ge(roped, 5)
            for k in range(2):
                tr(7 + k, [pj[:, t, C_KM + P * j:C_KM + P * (j + 1)] for j in (2 * k, 2 * k + 1) for t in range(T)])

            cw1 = slot(CMP_CHUNK).rearrange("p (v c n) -> p v c n", v=2, c=NC16)

            def cmp_hidden():
                chunk_loaded(CMP_CHUNK)
                pe.wait_ge(kv2_ready, 2)
                pe.wait_ge(proj_copied, 6)
                for v in range(2):
                    kvv = kv2[:, v, :, :].rearrange("p h (n c) -> p (h n) c", c=NC16)
                    for c in range(NC16):
                        i = mm(BANK[6][0:2 * NC16, v * P:(v + 1) * P], kvv[:, :, c], cw1[:, v, c, :],
                               start=c == 0, stop=c == NC16 - 1)
                i.then_inc(chunk_done, 1)

            def cmp_hiddenT():
                pe.wait_ge(hid_ready, 1)
                for v in range(2):
                    i = nc.tensor.transpose(BANK[7][:, v * 32:v * 32 + 2 * NC16], hid_g[0:2 * NC16, v * P:(v + 1) * P],
                                            ident[0:2 * NC16, 0:2 * NC16])
                i.then_inc(hidT_psum, 1)

            def cmp_keys():
                pe.wait_ge(hidT_ready, 1)
                for h in range(2):
                    mm(BANK[7][HD * h:HD * h + HD, 64:64 + NBLK], cmp_w2[:, 0, :], hidT[:, 0, NC16 * h:NC16 * h + NBLK], start=True, stop=True)
                for h in range(2):
                    i = mm(BANK[7][0:NBLK, P + HD * h:P + HD * (h + 1)], hidT[:, 1, NC16 * h:NC16 * h + NBLK], cmp_w2[:, 1, :], start=True, stop=True)
                i.then_inc(kcvc_psum, 1)

            def cmp_score():
                pe.wait_ge(kcvc_ready, 1)
                pe.wait_ge(consts_loaded, 16)
                mm(BANK[7][:, 0:P], const("spread")[0:NBLK, :], vc[0:NBLK, :], start=True, stop=True)
                for h in range(8):
                    for t in range(T):
                        r = HD * (h // 4)
                        col = S + (t * 4 + h % 4) * NC16
                        i = mm(BANK[7 - h // 4][:, col:col + NBLK], qk[r:r + HD, h % 4, t * P:(t + 1) * P], kcT[r:r + HD, 0:NBLK], start=True, stop=True)
                i.then_inc(cmp_scores, 1)

            def cmp_transpose():
                pe.wait_ge(cmp_probs, 1)
                for t in range(T):
                    i = nc.tensor.transpose(BANK[6][:, S + t * P:S + (t + 1) * P], cmp_p[:, t, :, :].rearrange("p h n -> p (h n)"), ident)
                i.then_inc(cmp_pT_psum, 1)

            pe.wait_ge(qt_act, 7)
            attention(AB_JOBS, 0, 0, {1: cmp_hidden, 3: cmp_hiddenT, 4: cmp_keys, 5: cmp_score, 8: cmp_transpose})
            pe.wait_ge(o_copied, 8)
            project_out(N_AB + 7)

            def moe(L, k, src):
                E, F, _, NR = MOE[L]
                units, pairs, gathers = UNITS[L], PAIRS[L], GATHERS[L]
                n0, per_group = N_MOE[L], 6 * units
                unit0, pair0, gather0 = G * sum(UNITS[:L]), G * sum(PAIRS[:L]), G * sum(GATHERS[:L])
                W = E * CAP
                pairs_per_unit = pairs // units
                transpose_x(k, src, lambda t: pe.wait_ge(normed, NORM_OF_XT[k] + t + 1))
                pe.wait_ge(small_loaded, SMALL_TOTAL)
                for t in range(T):
                    for kt in range(KT):
                        i = mm(BANK[0][:, t * 64:t * 64 + NR], XT[:, kt, t * P:(t + 1) * P], router_w[L][:, kt, :],
                               start=kt == 0, stop=kt == KT - 1)
                i.then_inc(logits_psum, 1)
                for b in range(4, 8):
                    mm(BANK[b][:, :], const("causal")[:, P:2 * P], const("count"), start=True, stop=False)
                pe.wait_ge(onehot_ready, L + 1)
                A = [chosen_[:, t * G * E:(t + 1) * G * E] for t in range(T)]
                rank = [BANK[1][:, n * G * E:(n + 1) * G * E] for n in range(3)]
                mm(rank[0], const("before"), A[0], start=True, stop=True)
                mm(rank[1], const("ones"), A[0], start=True, stop=False)
                mm(rank[1], const("before"), A[1], start=False, stop=True)
                mm(rank[2], const("ones"), A[0], start=True, stop=False)
                mm(rank[2], const("ones"), A[1], start=False, stop=True).then_inc(rank_psum, 1)

                def gather(g):
                    pe.wait_ge(p_ready, (g + G * L) * 2 + 1)
                    per_bank = KT // gathers
                    for n in range(gathers):
                        if n >= 2:
                            pe.wait_ge((xc_act, xc_dve)[n % 2], (g * gathers + gather0) // 2 + n // 2 if isinstance(g, int)
                                       else g * (gathers // 2) + (gather0 // 2 + n // 2))
                        for j in range(per_bank):
                            kt = n * per_bank + j
                            for t in range(T):
                                i = mm(BANK[2 + n % 2][:, j * W:(j + 1) * W], src[:, t, kt::KT], PB[:, t * W:(t + 1) * W],
                                       start=t == 0, stop=t == T - 1)
                        i.then_inc(xc_psum, 1)

                def group(g, last):
                    x = xcT[:, 0:KT * W].rearrange("p (k s) -> p k s", k=KT)

                    def load(kind, u):
                        for c in range(2):
                            n = n0 + first_chunk(units, kind, u) + c
                            pe.wait_ge(slot_loaded[n % NSLOT], g * (16 * per_group // NSLOT) + loaded_value(n))
                        return [slot(n - 1), slot(n)]

                    def hidden(kind, u):
                        w = load(kind, u)
                        b = BANK[0 if kind == "gate" else 1]
                        per_chunk = CH // F
                        for e in range(per_chunk):
                            for kt in range(KT):
                                for c in range(2):
                                    q = (u * per_chunk + e) * 2 + c
                                    col = e * KT * F + kt * F
                                    i = mm(b[CAP * c:CAP * (c + 1), e * F:(e + 1) * F], x[:, kt, q * CAP:(q + 1) * CAP],
                                           w[c][:, col:col + F], start=kt == 0, stop=kt == KT - 1)
                                    if e == per_chunk - 1 and kt == KT - 1:
                                        i.then_inc(chunk_done, 1)

                    def hidden_T(u):
                        pe.wait_ge(h_ready, g * units + (unit0 + u + 1))
                        for f in range(4):
                            step = F // P
                            ap = HB[:, (f // step) * F + f % step:(f // step + 1) * F:step]
                            i = nc.tensor.transpose(BANK[2][:, f * P:(f + 1) * P], ap, ident)
                        i.then_inc(hT_psum, 1)

                    def down(u, a, half):
                        if a == 0 and half == 0:
                            pe.wait_ge(hT_ready, g * units + (unit0 + u + 1))
                            load("down", u)
                        n = n0 + first_chunk(units, "down", u)
                        step = F // P
                        for f in range(step):
                            for c in range(2):
                                col = (a * step + f) * D + half * CH
                                i = mm(BANK[2 + half][CAP * c:CAP * (c + 1), :], HT[:, a * step + f, CAP * c:CAP * (c + 1)],
                                       slot(n + c)[:, col:col + CH], start=f == 0, stop=f == step - 1)
                        i.then_inc(y_psum, 1)

                    def scatter(u, a, half):
                        pair = u * pairs_per_unit + a
                        pe.wait_ge((y_act, y_dve)[half], g * pairs + (pair0 + pair + 1))
                        if pair == 0:
                            pe.wait_ge(pwT_act, g + (G * L + 1))
                        if pair == 2 and half == 0:
                            pe.wait_ge(pwT_dve, g + 1)
                        final = last and pair == pairs - 1
                        for t in range(T):
                            i = mm(BANK[4 + 2 * t + half][:, :], PWT[:, pair, t * P:(t + 1) * P], YS[:, pair % 2, half, :],
                                   start=False, stop=final)
                            if half == 0 and a == pairs_per_unit - 1:
                                i.then_inc(chunk_done, 1)
                            elif half == 1 and final:
                                i.then_inc(acc_ready, 1)

                    for u in range(units):
                        if u == 0:
                            for s_ in (xc_act, xc_dve):
                                pe.wait_ge(s_, g * (gathers // 2) + (gather0 // 2 + gathers // 2))
                        else:
                            pe.wait_ge(silu_done, g * units + (unit0 + u))
                        hidden("gate", u)
                        if u == 0:
                            pe.wait_ge(p_ready, g * 2 + (2 * G * L + 2))
                            for pair in range(pairs):
                                for t in range(T):
                                    i = nc.tensor.transpose(BANK[2 + pair // 2][:, (pair % 2) * S + t * P:(pair % 2) * S + (t + 1) * P],
                                                            PW[:, t * W + pair * P:t * W + (pair + 1) * P], ident)
                                if pair % 2:
                                    i.then_inc(pwT_psum, 1)
                        else:
                            hidden_T(u - 1)
                        hidden("up", u)
                        if u:
                            down(u - 1, 0, 0)
                            down(u - 1, 0, 1)
                            scatter(u - 1, 0, 0)
                            scatter(u - 1, 0, 1)
                    u = units - 1
                    pe.wait_ge(pwT_act, g + (G * L + 1))
                    if not last:
                        gather(g + 1)
                        for s_ in (xc_act, xc_dve):
                            pe.wait_ge(s_, g * (gathers // 2) + (gather0 // 2 + gathers))
                    hidden_T(u)
                    for a in range(pairs_per_unit):
                        down(u, a, 0)
                        if a:
                            scatter(u, a - 1, 1)
                        down(u, a, 1)
                        scatter(u, a, 0)
                    scatter(u, pairs_per_unit - 1, 1)

                gather(0)
                with pe.Fori(0, G - 1) as g:
                    group(g, False)
                group(G - 1, True)

                v = general[L]
                pe.wait_ge(over_ready, L + 1)
                flag = pe.value_load(OVER_I[0:1, 0:1], min_val=0, max_val=1)
                with pe.If(flag > 0):
                    with pe.Fori(0, G * 2 * units) as n:
                        pe.wait_ge(v["loaded"], n * 48 + 48)
                        for t in range(T):
                            for b in range(2):
                                for e in range(CH // F):
                                    for kt in range(KT):
                                        col = e * KT * F + kt * F
                                        i = mm(BANK[b][:, e * F:(e + 1) * F], XT[:, kt, t * P:(t + 1) * P], slot(b)[:, col:col + F],
                                               start=kt == 0, stop=kt == KT - 1)
                                i.then_inc(v["psum"], 1)
                            pe.wait_ge(v["h_ready"], n * 2 + (t + 1))
                            pe.wait_ge(v["added"], n * 2 + (t + 1))
                            for f in range(4):
                                step = F // P
                                ap = HB[:, (f // step) * F + f % step:(f // step + 1) * F:step]
                                i = nc.tensor.transpose(BANK[2][:, f * P:(f + 1) * P], ap, ident)
                            i.then_inc(v["psum"], 1)
                            pe.wait_ge(v["hT_ready"], n * 2 + (t + 1))
                            for half in range(2):
                                for f in range(4):
                                    i = mm(BANK[2 + half][:, :], HT[:, f, :], slot(2)[:, f * D + half * CH:f * D + (half + 1) * CH],
                                           start=f == 0, stop=f == 3)
                            i.then_inc(v["psum"], 1)

            moe(0, 1, X)

            transpose_x(2, X, lambda t: pe.wait_ge(normed, NORM_OF_XT[2] + t + 1))
            for c in range(4):
                project_T(N_SB + c, 6 + c, 4)
            for c in range(2):
                project(N_SB + 4 + c, CH, 10 + c)
            pe.wait_ge(proj_copied, 12)

            def sb_scores(h):
                r, n = HD * (h % 2), h // 2
                if h >= 2:
                    pe.wait_ge(z_abs, h - 1)
                mm(BANK[h % 2][:, 0:S], sbK[r:r + HD, n, 0:P], sbQ[r:r + HD, n, :], start=True, stop=True)
                mm(BANK[h % 2][:, S:BL], sbK[r:r + HD, n, P:S], sbQ[r:r + HD, n, P:S], start=True, stop=True).then_inc(z_psum, 1)

            def sb_suffix(h):
                pe.wait_ge(sp_ready, h + 1)
                if h >= 2:
                    pe.wait_ge(w_log, h - 1)
                b, spv = BANK[2 + h % 2], SP_[h % 3]
                mm(b[:, 0:S], const("neg_suffix"), spv[:, 0:S], start=True, stop=False)
                mm(b[:, P:S], const("neg_ones"), spv[:, S:BL], start=False, stop=True)
                mm(b[:, S:BL], const("neg_suffix"), spv[:, S:BL], start=True, stop=True).then_inc(r_psum, 1)

            def sb_values(h):
                r, pair = HD * (h % 2), h // 2
                if h % 2 == 0 and pair >= 2:
                    pe.wait_ge(sbo_copied, pair - 1)
                pe.wait_ge(w_ready, h + 1)
                b = BANK[4 + pair % 2]
                mm(b[r:r + HD, 0:S], sbV[:, 0, HD * h:HD * h + HD], WT[h % 3][:, 0:S], start=True, stop=False)
                mm(b[r:r + HD, P:S], sbV[:, 1, HD * h:HD * h + HD], WT[h % 3][:, S:BL], start=False, stop=True).then_inc(sbo_psum, 1)

            for s in range(16 + 4):
                if s < 16:
                    sb_scores(s)
                if 0 <= s - 2 < 16:
                    sb_suffix(s - 2)
                if s >= 4:
                    sb_values(s - 4)
            pe.wait_ge(sbo_copied, 8)
            project_out(N_SB + 6)
            moe(1, 3, X)

            transpose_x(4, U, lambda t: pe.wait_ge(normed, NORM_OF_XT[4] + t + 1))
            project_T(N_2, 12, 4)
            project(N_2 + 1, CH, 13)
            project(N_2 + 2, CH, 14)
            project_T(N_2 + 3, 15, 2, RANK)
            project(N_2 + 4, CH, 16)
            project(N_2 + 5, CH, 17)
            project(N_2 + 6, CH, 18)
            for m, src in enumerate((AQ, AK)):
                pe.wait_ge(roped, 6 + m)
                for k in range(2):
                    for n in range(4):
                        j, t = 2 * k + n // 2, n % 2
                        i = nc.tensor.transpose(BANK[2 * m + k][:, n * P:(n + 1) * P], src[:, t, P * j:P * (j + 1)], ident)
                    i.then_inc(qt_psum, 1)
            pe.wait_ge(qt_act, 11)
            for r in range(2):
                for t in range(T):
                    i = mm(BANK[r][:, t * S:(t + 1) * S], LR[0:RANK + 1, r, t * P:(t + 1) * P], gw[0:RANK + 1, r, :], start=True, stop=True)
                i.then_inc(gz_psum, 1)
            pe.wait_ge(la_ready, 1)
            la = by_tok(W3)
            for r in range(2):
                for k in range(2):
                    for t in range(T):
                        i = mm(BANK[2 + r][:, k * S + t * P:k * S + (t + 1) * P], la[:, r, t, k * P:(k + 1) * P],
                               const("up_to" if r == 0 else "from_on"), start=True, stop=True)
                i.then_inc(bt_psum, 1)
            qd, ki, ke = by_key(W1), by_key(W2), by_key(W3)
            ket = by_tok(W0)
            pe.wait_ge(qk_ready, 3)
            pe.wait_ge(proj_copied, 19)
            for r in range(2):
                for t in range(T):
                    for k in range(2):
                        i = nc.tensor.transpose(BANK[4 + r][:, t * S + k * P:t * S + (k + 1) * P], ke[:, r, k, t * P:(t + 1) * P], ident)
                i.then_inc(ket_psum, 1)
            for r in range(2):
                for i8 in range(8):
                    h, t = i8 // 4 + 2 * (i8 % 2), (i8 % 4) // 2
                    rows = slice(HD * (h % 2), HD * (h % 2) + HD)
                    i = mm(BANK[2 * r + i8 // 4][:, (i8 % 4) * P:(i8 % 4 + 1) * P], ki[rows, r, h // 2, t * P:(t + 1) * P],
                           qd[rows, r, h // 2, t * P:(t + 1) * P], start=True, stop=True)
                    if i8 % 4 == 3:
                        i.then_inc(att_psum, 1)
            pe.wait_ge(ket_ready, 2)
            for r in range(2):
                for n in ((0, 2, 1) if r == 0 else (3, 1, 2)):
                    for k in range(2):
                        rows = slice(GCH * (n % 2), GCH * (n % 2) + GCH)
                        for hh in range(2):
                            h = 2 * k + hh
                            col = (n // 2) * S + k * P
                            i = mm(BANK[4 + 2 * r + n % 2][HD * hh:HD * hh + HD, col:col + P],
                                   ket[rows, r, n // 2, h * HD:(h + 1) * HD], GV[rows, n // 2, h * P:(h + 1) * P], start=True, stop=True)
                i.then_inc(kv_psum, 1)
            pe.wait_ge(att_ready, 1)
            pe.wait_ge(state_ready, 1)
            for t in range(T):
                for h in range(4):
                    rows = slice(HD * (h % 2), HD * (h % 2) + HD)
                    b, cols = BANK[2 * t + h % 2], slice((h // 2) * P, (h // 2 + 1) * P)
                    i = mm(b[:, cols], att[:, (h % 2) * 4 + t * 2 + h // 2, :], GV[:, t, h * P:(h + 1) * P], start=True, stop=False)
                    for cc in range(2):
                        n = 2 * t + cc
                        for r in range(2):
                            if (r == 0 and n == 0) or (r == 1 and n == 3):
                                continue
                            sl = n - 1 if r == 0 else 2 - n
                            last = r == 1 or n == 3
                            i = mm(b[GCH * cc:GCH * cc + GCH, cols], qd[rows, r, h // 2, n * GCH:(n + 1) * GCH],
                                   state[rows, r, h // 2, sl, :], start=False, stop=last)
                i.then_inc(go_psum, 1)
            pe.wait_ge(go_ready, 1)
            for k in range(2):
                for n in range(4):
                    j, t = 2 * k + n // 2, n % 2
                    i = nc.tensor.transpose(BANK[4 + k][:, n * P:(n + 1) * P], by_tok2(W0)[:, t, P * j:P * (j + 1)], ident)
                i.then_inc(goT_psum, 1)
            pe.wait_ge(goT_ready, 1)
            attention(DIL_JOBS, len(AB_JOBS), 8, {})
            pe.wait_ge(o_copied, 12)
            project_out(N_2 + 7)
            moe(2, 5, U)

        @block.scalar
        def _(act):
            ac = nc.scalar.activation
            steps = [0]

            def link(i):
                steps[0] += 1
                i.then_inc(act_step, 1)
                act.wait_ge(act_step, steps[0])

            act.dma_start(CONSTS[:, 0:FIRST_CONSTS], a["constants"][:, 0:FIRST_CONSTS]).then_inc(first_consts_loaded, 16)
            act.dma_start(POS_I[:, :], a["positions"][0].rearrange("(t p) -> p t", p=P), allow_slow_non_contiguous=True).then_inc(positions_loaded, 16)
            for i, n in enumerate(("nsa_cmp_w2_k", "nsa_cmp_w2_v")):
                act.dma_start(cmp_w2[:, i, :], a[n][0]).then_inc(cmp_small_loaded, 16)
            for i, n in enumerate(("nsa_cmp_pos_k", "nsa_cmp_pos_v")):
                act.dma_start(cmp_pos[0:NC16, i, :].rearrange("p (h d) -> p h d", h=2),
                              a[n][0].rearrange("(h c) d -> c h d", h=2)).then_inc(cmp_small_loaded, 16)
            act.dma_start(CONSTS[:, FIRST_CONSTS:], a["constants"][:, FIRST_CONSTS:]).then_inc(consts_loaded, 16)
            for L in range(NMOE):
                E = MOE[L][0]
                wg, bg, we, be = ((a["moe_w_grp"][L], a["moe_b_grp"][L], a["moe_w_rt"][L], a["moe_b_rt"][L]) if L < 2 else
                                  (a["router_group_w_2"][0], a["router_group_b_2"][0], a["router_expert_w_2"][0], a["router_expert_b_2"][0]))
                act.dma_start(router_w[L][:, :, 0:G], wg.rearrange("(p k) g -> p k g", k=KT)).then_inc(small_loaded, 16)
                for g in range(G):
                    act.dma_start(router_w[L][:, :, G + g * E:G + (g + 1) * E], we[g].rearrange("(p k) e -> p k e", k=KT)).then_inc(small_loaded, 16)
                act.dma_start(router_b[L][:, 0:G], bg.partition_broadcast(P)).then_inc(small_loaded, 16)
                act.dma_start(router_b[L][:, G:G + G * E], be.rearrange("g e -> (g e)").partition_broadcast(P)).then_inc(small_loaded, 16)
            for r, n in enumerate(("gla_fwd_gate_", "gla_bwd_gate_")):
                act.dma_start(gw[0:RANK, r, :], a[n + "w_2"][0]).then_inc(small_loaded, 16)
                act.dma_start(gw[RANK:RANK + 1, r, :], a[n + "b_2"]).then_inc(small_loaded, 16)
            act.dma_start(gla_norm, a["gla_norm_w_2"][0].partition_broadcast(P)).then_inc(small_loaded, 16)

            def transpose_x(k):
                for b in range(2):
                    act.wait_ge(xt_psum, 4 * k + b + 1)
                    ac(XT[:, 2 * b:2 * b + 2, :], BANK[b][:, :].rearrange("p (k s) -> p k s", k=2), ACT.Copy).then_inc(xt_act, 1)

            def take(seq, n, parts):
                act.wait_ge(chunk_done, n + 1)
                for b, o, rows, ncols, scale in parts:
                    src = BANK[4 + 2 * (seq % 2) + b][0:rows, 0:ncols]
                    if seq == 0:
                        o = o.rearrange("p (j a d) -> p a j d", a=2, j=4)
                        src = src.rearrange("p (a j d) -> p a j d", a=2, j=4)
                    i = ac(o, src, ACT.Copy, scale=scale)
                i.then_inc(proj_copied, 1)

            def rstd_from(k, n):
                act.wait_ge(var_ready, k + 1)
                link(ac(lnv[:, 0:n], veps[:, 0:n], ACT.Ln))
                ac(rstd[:, 0:n], lnv[:, 0:n], ACT.Exp, scale=-0.5).then_inc(rstd_ready, 1)

            transpose_x(0)
            act.wait_ge(angle_ready, 2)
            ac(sin1, angle, ACT.Sin)
            ac(cos1, turns, ACT.Sin).then_inc(sines_ready, 1)
            nc.scalar.preload_act_table_set("natural_log_exp_and_others")
            for c in range(6):
                sc = -SCALE if c in (0, 3) else 1.0
                take(c, c, [(t, pj[:, t, W_COL0[c]:W_COL0[c] + W_NCOLS[c]], P, W_NCOLS[c], sc) for t in range(T)])
                if c == 2:
                    act.wait_ge(proj_copied, 3)
                    ac(pj[:, :, C_GA:C_GA + 24], pj[:, :, C_GA:C_GA + 24], ACT.Exp, scale=-1.0).then_inc(gates_exp, 1)
                if c == 2:
                    for k in range(2):
                        act.wait_ge(qt_psum, k + 1)
                        ac(qk[:, 2 * k:2 * k + 2, :], BANK[k][:, :].rearrange("p (n s) -> p n s", n=2), ACT.Copy).then_inc(qt_act, 1)
                if c == 4:
                    act.wait_ge(qt_psum, 5)
                    ac(qk[:, 5, :], BANK[0][:, 0:S], ACT.Copy).then_inc(qt_act, 1)
                if c == 5:
                    for k in (5, 6):
                        act.wait_ge(qt_psum, k + 1)
                        ac(qk[:, 6 + 2 * (k - 5):8 + 2 * (k - 5), :], BANK[k % 4][:, :].rearrange("p (n s) -> p n s", n=2), ACT.Copy).then_inc(qt_act, 1)
            for k in (7, 8):
                act.wait_ge(qt_psum, k + 1)
                ac(qk[:, 10 + 2 * (k - 7):12 + 2 * (k - 7), :], BANK[k % 4][:, :].rearrange("p (n s) -> p n s", n=2), ACT.Copy).then_inc(qt_act, 1)

            def attention(jobs, first, extras):
                dil = jobs[0][0] == "dil"
                for s in range(len(jobs) + 2):
                    if s < len(jobs):
                        J = first + s
                        act.wait_ge(mins_ready, J + 1)
                        if J >= 3:
                            act.wait_ge(pt_psum, J - 2)
                        for t, (c0, c1) in enumerate(((0, S), (S, 2 * S)) if dil else ((0, P), (P, 3 * P))):
                            i = ac(PR[J % 3][:, c0:c1], SM[J % 2][:, c0:c1], ACT.Exp, scale=-1.0,
                                   bias=least[:, J % 4, t:t + 1], accum_out=psums[:, J % 4, t:t + 1])
                        i.then_inc(probs_ready, 1)
                    if s in extras:
                        extras[s]()
                    if s >= 2:
                        J = first + s - 2
                        n = 2 * S if dil else 3 * P
                        act.wait_ge(pt_psum, J + 1)
                        if J >= 2:
                            act.wait_ge(pv_done, J - 1)
                        ac(PTS[J % 2][:, 0:n], BANK[2 + J % 2][:, 0:n], ACT.Copy).then_inc(pt_copied, 1)

            def gelu_exp():
                act.wait_ge(hid_exp_in, 1)
                ac(hid_t[0:2 * NC16, :], hid_t[0:2 * NC16, :], ACT.Exp, scale=-2.0 * float(np.sqrt(2.0 / np.pi))).then_inc(hid_exp, 1)

            def hiddenT():
                act.wait_ge(hidT_psum, 1)
                ac(hidT, BANK[7][:, 0:64].rearrange("p (v n) -> p v n", v=2), ACT.Copy).then_inc(hidT_ready, 1)

            def cmp_exponent():
                act.wait_ge(cmp_exp_in, 1)
                ac(cmp_p, cmp_p, ACT.Exp, scale=-1.0).then_inc(cmp_exp, 1)

            def cmp_pT_copy():
                act.wait_ge(cmp_pT_psum, 1)
                ac(cmp_pT_sb, BANK[6][:, S:2 * S], ACT.Copy).then_inc(cmp_pT, 1)

            attention(AB_JOBS, 0, {2: gelu_exp, 3: hiddenT, 6: cmp_exponent, 8: cmp_pT_copy})
            rstd_from(0, T)

            def moe(L, k):
                transpose_x(k)
                for _ in range(2):
                    n = L * 2 + _ + 1
                    act.wait_ge(rexp_in, n)
                    w = small_r[1][:, 0:T * G] if _ == 0 else small_r[8][:, 0:T]
                    ac(w, w, ACT.Exp).then_inc(rexp, 1)
                nc.scalar.preload_act_table(ACT.Silu)
                units, pairs, gathers = UNITS[L], PAIRS[L], GATHERS[L]
                n0, per_group = N_MOE[L], 6 * units
                unit0, pair0, gather0 = G * sum(UNITS[:L]), G * sum(PAIRS[:L]), G * sum(GATHERS[:L])

                def gathered(g):
                    for n in range(0, gathers, 2):
                        act.wait_ge(xc_psum, g * gathers + (gather0 + n + 1))
                        ac(xcT[:, n * CH:(n + 1) * CH], BANK[2][:, :], ACT.Copy).then_inc(xc_act, 1)

                def outputs(g, pair):
                    act.wait_ge(y_psum, g * (2 * pairs) + (2 * (pair0 + pair) + 1))
                    ac(YS[:, pair % 2, 0, :], BANK[2][:, :], ACT.Copy).then_inc(y_act, 1)

                def group(g, last):
                    act.wait_ge(pwT_psum, g * (pairs // 2) + (G * sum(PAIRS[:L]) // 2 + 1))
                    ac(PWT[:, 0:2, :], BANK[2][:, :].rearrange("p (a s) -> p a s", a=2), ACT.Copy).then_inc(pwT_act, 1)
                    for u in range(units):
                        act.wait_ge(chunk_done, g * per_group + (n0 + first_chunk(units, "gate", u) + 2))
                        if u:
                            act.wait_ge(h_ready, g * units + (unit0 + u))
                        ac(SG, BANK[0][:, :], ACT.Silu).then_inc(silu_done, 1)
                        if u:
                            outputs(g, u - 1)
                    if not last:
                        gathered(g + 1)
                    for pair in range(units - 1 if units > 1 else 0, pairs):
                        outputs(g, pair)

                gathered(0)
                with act.Fori(0, G - 1) as g:
                    group(g, False)
                group(G - 1, True)

                v = general[L]
                act.wait_ge(over_ready, L + 1)
                flag = act.value_load(OVER_I[0:1, 0:1], min_val=0, max_val=1)
                with act.If(flag > 0):
                    with act.Fori(0, G * 2 * units) as n:
                        for t in range(T):
                            act.wait_ge(v["psum"], n * 8 + (4 * t + 1))
                            ac(SG, BANK[0][:, :], ACT.Silu).then_inc(v["silu_done"], 1)
                nc.scalar.preload_act_table_set("natural_log_exp_and_others")

            moe(0, 1)
            rstd_from(1, T)
            transpose_x(2)
            for c in range(4):
                dst = (sbQ if c < 2 else sbK)
                take(6 + c, N_SB + c, [(b, dst[:, 4 * (c % 2) + 2 * b:4 * (c % 2) + 2 * b + 2, :], P, CH, SCALE if c < 2 else 1.0) for b in range(2)])
            for c in range(2):
                take(10 + c, N_SB + 4 + c, [(t, sbV[:, t, c * CH:(c + 1) * CH], P, CH, 1.0) for t in range(T)])
            for s in range(16 + 3):
                if s < 16:
                    act.wait_ge(z_abs, s + 1)
                    link(ac(AN[s % 2], AN[s % 2], ACT.Exp))
                    ac(AN[s % 2], AN[s % 2], ACT.Ln, bias=1.0).then_inc(z_log, 1)
                if s >= 3:
                    h = s - 3
                    act.wait_ge(w_log, h + 1)
                    if h >= 3:
                        act.wait_ge(sbo_psum, h - 2)
                    ac(WT[h % 3], WL[h % 2], ACT.Exp).then_inc(w_ready, 1)
            rstd_from(2, T)
            moe(1, 3)
            rstd_from(3, T)
            rstd_from(4, T)
            transpose_x(4)
            take(12, N_2, [(0, gqT, P, CH, SCALE), (1, gkT, P, CH, 1.0)])
            take(13, N_2 + 1, [(t, GV[:, t, :], P, CH, 1.0) for t in range(T)])
            take(14, N_2 + 2, [(t, GG[:, t, :], P, CH, 1.0) for t in range(T)])
            act.wait_ge(pool_step, 1)
            take(15, N_2 + 3, [(0, LR[0:RANK, :, :], RANK, CH, 1.0)])
            take(16, N_2 + 4, [(t, AQ[:, t, :], P, CH, -SCALE) for t in range(T)])
            take(17, N_2 + 5, [(t, AK[:, t, :], P, CH, 1.0) for t in range(T)])
            take(18, N_2 + 6, [(t, AV[:, t, :], P, CH, 1.0) for t in range(T)])
            for k in range(4):
                act.wait_ge(qt_psum, 9 + k + 1)
                ac(qk[:, 2 * k:2 * k + 2, :], BANK[k][:, :].rearrange("p (n s) -> p n s", n=2), ACT.Copy).then_inc(qt_act, 1)
            act.wait_ge(gz_abs, 1)
            link(ac(W1, W1, ACT.Exp))
            ac(W1, W1, ACT.Ln, bias=1.0).then_inc(gz_log, 1)
            act.wait_ge(bs_ready, 1)
            bs = by_key(W0)
            ac(W1, W0, ACT.Exp).then_inc(eb_ready, 1)
            ac(W2, W0, ACT.Exp, scale=-1.0).then_inc(eb_ready, 1)
            for r in range(2):
                for k in range(2):
                    for n in range(4):
                        end = n * GCH + (GCH - 1 if r == 0 else 0)
                        i = ac(by_key(W3)[:, r, k, n * GCH:(n + 1) * GCH], bs[:, r, k, n * GCH:(n + 1) * GCH], ACT.Exp,
                               scale=-1.0, bias=bs[:, r, k, end:end + 1])
            i.then_inc(eb_ready, 1)
            for r in range(2):
                act.wait_ge(ket_psum, r + 1)
                ac(W0[:, 512 * r:512 * (r + 1)], BANK[4 + r][:, :], ACT.Copy).then_inc(ket_ready, 1)
            act.wait_ge(ket_psum, 2)
            for t in range(T):
                i = ac(by_tok2(W3)[:, t, :], GG[:, t, :], ACT.Exp, scale=-1.0)
            i.then_inc(silu_exp, 1)
            for t in range(T):
                act.wait_ge(go_psum, t + 1)
                for par in range(2):
                    i = ac(by_tok2(W2)[:, t, :].rearrange("p (hh r v) -> p hh r v", hh=2, r=2)[:, :, par, :],
                           BANK[2 * t + par][:, 0:S].rearrange("p (hh v) -> p hh v", hh=2), ACT.Square)
                i.then_inc(go_square, 1)
            act.wait_ge(var_ready, 6)
            link(ac(go_l, go_ms, ACT.Ln))
            ac(go_r, go_l, ACT.Exp, scale=-0.5).then_inc(rstd_ready, 1)
            for k in range(2):
                act.wait_ge(goT_psum, k + 1)
                i = ac(mixT[:, 2 * k:2 * k + 2, :], BANK[4 + k][:, :].rearrange("p (n s) -> p n s", n=2), ACT.Copy)
            i.then_inc(goT_ready, 1)
            attention(DIL_JOBS, len(AB_JOBS), {})
            rstd_from(6, T)
            moe(2, 5)
            rstd_from(7, T)

        @block.vector
        def _(dve):
            tt, ts, stt = nc.vector.tensor_tensor, nc.vector.tensor_scalar, nc.vector.scalar_tensor_tensor
            cp = nc.vector.tensor_copy
            steps = [0]

            def link(i):
                steps[0] += 1
                i.then_inc(dve_step, 1)
                dve.wait_ge(dve_step, steps[0])

            def transpose_x(k):
                for b in (2, 3):
                    dve.wait_ge(xt_psum, 4 * k + b + 1)
                    cp(XT[:, 2 * b:2 * b + 2, :], BANK[b][:, :].rearrange("p (k s) -> p k s", k=2)).then_inc(xt_dve, 1)

            def sharpen(r, v, q):
                link(tt(q, r, r, ALU.mult))
                link(tt(q, q, v, ALU.mult))
                link(ts(q, q, -0.5, 1.5, ALU.mult, ALU.add))
                link(tt(r, r, q, ALU.mult))

            def norm(k, nvar, kind, dst):
                for t in range(T):
                    for half in range(2):
                        link(nc.vector.bn_stats(stats[:, t, 6 * half:6 * half + 6], X[:, t, half * CH:(half + 1) * CH]))
                    link(nc.vector.bn_aggr(mean_var[:, t, :], stats[:, t, :]))
                if kind == "layer":
                    ts(veps[:, 0:T], mean_var[:, :, 1], LN_EPS, None, ALU.add).then_inc(var_ready, 1)
                else:
                    link(tt(newton[:, 0:T], mean_var[:, :, 0], mean_var[:, :, 0], ALU.mult))
                    stt(veps[:, 0:T], newton[:, 0:T], RMS_EPS, mean_var[:, :, 1], ALU.add, ALU.add).then_inc(var_ready, 1)
                dve.wait_ge(rstd_ready, nvar + 1)
                sharpen(rstd[:, 0:T], veps[:, 0:T], newton[:, 0:T])
                dve.wait_ge(norm_loaded[k % 2], NORM_VALUE[k])
                for t in range(T):
                    if kind == "layer":
                        link(stt(X[:, t, :], X[:, t, :], mean_var[:, t, 0:1], NORM[:, k % 2, 0, :], ALU.subtract, ALU.mult))
                        stt(dst[:, t, :], X[:, t, :], rstd[:, t:t + 1], NORM[:, k % 2, 1, :], ALU.mult, ALU.add).then_inc(normed, 1)
                    else:
                        stt(dst[:, t, :], X[:, t, :], rstd[:, t:t + 1], NORM[:, k % 2, 0, :], ALU.mult, ALU.mult).then_inc(normed, 1)
                    dve.wait_ge(normed, 2 * k + t + 1)

            def residual(n, alpha):
                for half in range(2):
                    dve.wait_ge(chunk_done, n + half + 1)
                    for t in range(T):
                        link(stt(X[:, t, half * CH:(half + 1) * CH], X[:, t, half * CH:(half + 1) * CH], alpha,
                                 BANK[4 + 2 * half + t][:, :], ALU.mult, ALU.add))

            def rope(view, col, n):
                h = heads(view, col, n)
                x1, x2 = h[:, :, :, 0, :], h[:, :, :, 1, :]
                c, s_ = (v.rearrange("p (t d) -> p t d", t=T).unsqueeze(2).to_broadcast([P, T, n, HALF]) for v in (cos1, sin1))
                m = [w[:, 0:T * n * HALF].rearrange("p (t h d) -> p t h d", t=T, h=n) for w in ROPE_TMP]
                tt(m[0], x1, c, ALU.mult)
                tt(m[1], x2, s_, ALU.mult)
                tt(m[2], x2, c, ALU.mult)
                link(tt(m[3], x1, s_, ALU.mult))
                tt(x1, m[0], m[1], ALU.subtract)
                return tt(x2, m[2], m[3], ALU.add)

            transpose_x(0)
            dve.wait_ge(first_consts_loaded, 16)
            dve.wait_ge(positions_loaded, 16)
            link(cp(pos_f, POS_I[:, :]))
            for t in range(T):
                link(ts(cos1[:, t * HALF:(t + 1) * HALF], const("inv_freq"), pos_f[:, t:t + 1], None, ALU.mult))
            TWO_PI = 2 * np.pi
            C1 = 6.28125
            C2 = float(np.float32(TWO_PI - C1))
            C3 = float(TWO_PI - C1 - float(np.float32(TWO_PI - C1)))
            for i, (o, quarter) in enumerate(((angle, 0.0), (turns, 0.25))):
                n = sin1
                link(ts(n, cos1, 1.0 / TWO_PI, quarter, ALU.mult, ALU.add))
                link(ts(n, n, 12582912.0, None, ALU.add))
                link(ts(n, n, 12582912.0, None, ALU.subtract))
                link(stt(o, n, -C1, cos1, ALU.mult, ALU.add))
                link(stt(o, n, -C2, o, ALU.mult, ALU.add))
                link(stt(o, n, -C3, o, ALU.mult, ALU.add))
                if quarter:
                    link(ts(o, o, TWO_PI * quarter, None, ALU.add))
                ts(o, o, 3.1415925, -3.1415925, ALU.min, ALU.max).then_inc(angle_ready, 1)
            dve.wait_ge(pos_psum, 1)
            cp(cmp_posT, BANK[3][:, 0:2 * NC16].rearrange("p (v c) -> p v c", v=2)).then_inc(pos_ready, 1)
            dve.wait_ge(sines_ready, 1)
            dve.wait_ge(proj_copied, 1)
            rope(pj, 0, 8).then_inc(roped, 1)
            dve.wait_ge(roped, 1)
            dve.wait_ge(proj_copied, 2)
            link(rope(pj, C_KC, 2))
            rope(pj, C_KS, 2).then_inc(roped, 1)
            dve.wait_ge(roped, 2)
            dve.wait_ge(proj_copied, 3)
            rope(pj, C_KW, 2).then_inc(roped, 1)
            dve.wait_ge(roped, 3)

            ga = pj[:, :, C_GA:C_GA + 24]
            dve.wait_ge(gates_exp, 1)
            link(ts(ga, ga, 1.0, None, ALU.add))
            nc.vector.reciprocal(ga, ga).then_inc(gates_ready, 1)
            dve.wait_ge(pos_ready, 1)
            dve.wait_ge(qt_psum, 3)
            cp(qk[:, 4, :], BANK[2][:, 0:S])
            link(nc.vector.memset(kv2[HD:P, :, :, NBLK * NC16:S], 0.0))
            for v, (b, col) in enumerate(((2, S), (3, 0))):
                dve.wait_ge(qt_psum, 3 + v)
                for h in range(2):
                    for half in range(2):
                        n = NC16 - half
                        rows = slice(HD * half, HD * half + HD)
                        src = BANK[b][HD * h:HD * h + HD, col + CMP_STRIDE * half:col + S].rearrange("p (n c) -> p n c", c=NC16)
                        dst = kv2[rows, v, h, 0:n * NC16].rearrange("p (n c) -> p n c", c=NC16)
                        i = tt(dst, src, cmp_posT[rows, v, :].unsqueeze(1).to_broadcast([HD, n, NC16]), ALU.add)
                i.then_inc(kv2_ready, 1)
            dve.wait_ge(proj_copied, 4)
            rope(pj, C_QM, 8).then_inc(roped, 1)
            dve.wait_ge(roped, 4)
            dve.wait_ge(proj_copied, 5)
            rope(pj, C_KM, 8).then_inc(roped, 1)
            dve.wait_ge(roped, 5)

            def attention(jobs, first, pairs0, extras):
                dil = jobs[0][0] == "dil"

                def inverse(j):
                    J = first + j
                    dve.wait_ge(probs_ready, J + 1)
                    if dil:
                        for t in range(T):
                            c = PR[J % 3][:, t * S:(t + 1) * S]
                            i = stt(c, c, 1.0, const("count")[:, t * S:(t + 1) * S], ALU.mult, ALU.mult, accum_out=psums[:, J % 4, t:t + 1])
                        link(i)
                    nc.vector.reciprocal(rinv[:, J % 4, :], psums[:, J % 4, :]).then_inc(rinv_ready, 1)

                for s in range(len(jobs) + 4):
                    if s < len(jobs):
                        J = first + s
                        dve.wait_ge(scores_ready, J + 1)
                        if J >= 2:
                            dve.wait_ge(probs_ready, J - 1)
                        for t, (c0, c1) in enumerate(((0, S), (S, 2 * S)) if dil else ((0, P), (P, 3 * P))):
                            i = nc.vector.tensor_tensor_reduce(
                                out=SM[J % 2][:, c0:c1], in0=BANK[J % 2][:, c0:c1],
                                in1=const("unseen" if dil else "causal")[:, c0:c1], scale=1.0, scalar=3e38,
                                op0=ALU.add, op1=ALU.min, accum_out=least[:, J % 4, t:t + 1])
                        i.then_inc(mins_ready, 1)
                    if 1 <= s <= len(jobs):
                        inverse(s - 1)
                    if s in extras:
                        extras[s]()
                    if s >= 4 and last_of_pair(jobs, s - 4):
                        j = s - 4
                        pair = (jobs[j][1] // 2 if dil else job_pair(jobs[j])) + pairs0
                        dve.wait_ge(pv_done, first + j + 1)
                        cp(mixT[:, job_tile(jobs[j]), :], BANK[4 + pair % 2][:, 0:S]).then_inc(o_copied, 1)

            dve.wait_ge(consts_loaded, 16)
            R = slice(0, 2 * NC16)

            def gelu_in():
                dve.wait_ge(chunk_done, CMP_CHUNK + 1)
                link(cp(hid_g[R, :], BANK[6][R, 0:2 * P]))
                link(tt(hid_t[R, :], hid_g[R, :], hid_g[R, :], ALU.mult))
                link(ts(hid_t[R, :], hid_t[R, :], 0.044715, 1.0, ALU.mult, ALU.add))
                tt(hid_t[R, :], hid_t[R, :], hid_g[R, :], ALU.mult).then_inc(hid_exp_in, 1)

            def gelu_out():
                dve.wait_ge(hid_exp, 1)
                link(ts(hid_t[R, :], hid_t[R, :], 1.0, None, ALU.add))
                link(nc.vector.reciprocal(hid_t[R, :], hid_t[R, :]))
                tt(hid_g[R, :], hid_g[R, :], hid_t[R, :], ALU.mult).then_inc(hid_ready, 1)

            def keys_copy():
                dve.wait_ge(kcvc_psum, 1)
                cp(kcT[:, 0:NBLK], BANK[7][:, 64:64 + NBLK])
                cp(vc[0:NBLK, :], BANK[7][0:NBLK, P:2 * P]).then_inc(kcvc_ready, 1)

            def cmp_softmax_in():
                dve.wait_ge(cmp_scores, 1)
                for kv in range(2):
                    tt(v_blocks[:, 4 * kv:4 * kv + 4, :], BANK[7][:, HD * kv:HD * (kv + 1)].unsqueeze(1).to_broadcast([P, 4, HD]),
                       const("own_head")[:, 4 * kv:4 * kv + 4].unsqueeze(2).to_broadcast([P, 4, HD]), ALU.mult)
                link(nc.vector.memset(cmp_p, 0.0))
                big = const("cmp_big").rearrange("p (t n) -> p t n", t=T)[:, :, 0:NBLK].unsqueeze(2).to_broadcast([P, T, 4, NBLK])
                for kv in range(2):
                    sc = BANK[7 - kv][:, S:S + P].rearrange("p (t h n) -> p t h n", t=T, h=4)
                    i = tt(cmp_p[:, :, 4 * kv:4 * kv + 4, 0:NBLK], sc[:, :, :, 0:NBLK], big, ALU.add)
                link(i)
                link(nc.vector.tensor_reduce(cmp_m, cmp_p[:, :, :, 0:NBLK], AX, ALU.min))
                tt(cmp_p[:, :, :, 0:NBLK], cmp_p[:, :, :, 0:NBLK], cmp_m.unsqueeze(3).to_broadcast([P, T, 8, NBLK]), ALU.subtract).then_inc(cmp_exp_in, 1)

            def cmp_softmax_out():
                dve.wait_ge(cmp_exp, 1)
                seen = const("cmp_seen").rearrange("p (t n) -> p t n", t=T).unsqueeze(2).to_broadcast([P, T, 8, NC16])
                link(tt(cmp_p, cmp_p, seen, ALU.mult))
                link(nc.vector.reduce_sum(cmp_m, cmp_p, AX))
                link(ts(cmp_m, cmp_m, 1e-30, None, ALU.max))
                link(nc.vector.reciprocal(cmp_m, cmp_m))
                dve.wait_ge(gates_ready, 1)
                link(tt(cmp_m, cmp_m, pj[:, :, C_GA:C_GA + 24:3], ALU.mult))
                tt(cmp_p, cmp_p, cmp_m.unsqueeze(3).to_broadcast([P, T, 8, NC16]), ALU.mult).then_inc(cmp_probs, 1)

            attention(AB_JOBS, 0, 0, {1: gelu_in, 2: gelu_out, 4: keys_copy, 5: cmp_softmax_in, 7: cmp_softmax_out})
            residual(N_AB + 7, ALPHA)
            norm(0, 0, "layer", X)

            def first_max(vals, eq, m, onehot, w, n, tie):
                link(nc.vector.reduce_max(m, vals, AX))
                mb = m.unsqueeze(2).to_broadcast([P, T, n])
                link(tt(eq, vals, mb, ALU.is_equal))
                link(tt(eq, eq, tie, ALU.mult))
                link(nc.vector.reduce_max(w, eq, AX))
                return tt(onehot, eq, w.unsqueeze(2).to_broadcast([P, T, n]), ALU.is_equal)

            def moe(L, k, alpha):
                E, F, _, NR = MOE[L]
                units, pairs, gathers = UNITS[L], PAIRS[L], GATHERS[L]
                n0, per_group = N_MOE[L], 6 * units
                unit0, pair0, gather0 = G * sum(UNITS[:L]), G * sum(PAIRS[:L]), G * sum(GATHERS[:L])
                W = E * CAP
                transpose_x(k)
                dve.wait_ge(logits_psum, L + 1)
                lg = rlog[:, 0:T * NR].rearrange("p (t n) -> p t n", t=T)
                bias = router_b[L].unsqueeze(1).to_broadcast([P, T, NR])
                dve.wait_ge(small_loaded, SMALL_TOTAL)
                link(tt(lg, BANK[0][:, 0:128].rearrange("p (t n) -> p t n", t=T)[:, :, 0:NR], bias, ALU.add))
                gm, wg = small_r[0][:, 0:T], small_r[0][:, 8:8 + T]
                gd = small_r[1][:, 0:T * G].rearrange("p (t g) -> p t g", t=T)
                oh = small_r[2][:, 0:T * G].rearrange("p (t g) -> p t g", t=T)
                eq = small_r[3].rearrange("p (t g) -> p t g", t=T)
                tie = const("descend").unsqueeze(1)
                link(first_max(lg[:, :, 0:G], eq[:, :, 0:G], gm, oh, small_r[4][:, 0:T], G, tie[:, :, 0:G].to_broadcast([P, T, G])))
                tt(gd, lg[:, :, 0:G], gm.unsqueeze(2).to_broadcast([P, T, G]), ALU.subtract).then_inc(rexp_in, 1)
                rtv = rt[:, 0:T * G * E].rearrange("p (t e g) -> p t e g", t=T, e=E)
                le = lg[:, :, G:NR].rearrange("p t (g e) -> p t e g", g=G)
                link(tt(rtv, le, oh.unsqueeze(2).to_broadcast([P, T, E, G]), ALU.mult))
                by_expert = lambda w: w[:, 0:T * E].rearrange("p (t e) -> p t e", t=T)
                sel, oh1, oh2, chosen, cwv = (by_expert(small_r[n]) for n in (5, 6, 7, 10, 13))
                link(nc.vector.reduce_sum(sel, rtv, AX))
                v1, v2, dv = small_r[9][:, 0:T], small_r[9][:, 8:8 + T], small_r[8][:, 0:T]
                w1, w2 = small_r[11][:, 0:T], small_r[12][:, 0:T]
                eqe = small_r[3][:, 0:T * E].rearrange("p (t e) -> p t e", t=T)
                tie_e = tie[:, :, 0:E].to_broadcast([P, T, E])
                link(first_max(sel, eqe, v1, oh1, small_r[4][:, 0:T], E, tie_e))
                link(stt(sel, oh1, -BIG, sel, ALU.mult, ALU.add))
                link(first_max(sel, eqe, v2, oh2, small_r[4][:, 0:T], E, tie_e))
                link(tt(chosen, oh1, oh2, ALU.add))
                by_ge = lambda w: w[:, 0:T * G * E].rearrange("p (t g e) -> p t g e", t=T, g=G)
                spread_g = oh.unsqueeze(3).to_broadcast([P, T, G, E])
                tt(by_ge(chosen_), spread_g, chosen.unsqueeze(2).to_broadcast([P, T, G, E]), ALU.mult).then_inc(onehot_ready, 1)
                tt(dv, v2, v1, ALU.subtract).then_inc(rexp_in, 1)
                dve.wait_ge(onehot_ready, L + 1)
                far = rt[:, 0:T * G * E]
                link(ts(far, chosen_[:, 0:T * G * E], -4096.0, 4096.0, ALU.mult, ALU.add))

                per_chunk = CH // F
                def by_place(w, t):
                    return w[:, 0:T * G * E].rearrange("p (g t u e c) -> p t g u e c", g=G, t=T, u=units, c=2)[:, t]

                def by_number(w, t):
                    return w[:, 0:T * G * E].rearrange("p (t g u c e) -> p t g u e c", g=G, t=T, u=units, c=2)[:, t]

                def ordered(dst, src, t):
                    d, s_ = by_place(dst, t), by_number(src, t)
                    return (d[:, :, 0], s_[:, :, 0]) if units == 1 else (d[:, :, :, 0, :], s_[:, :, :, 0, :])

                dve.wait_ge(rexp, 2 * L + 1)
                link(nc.vector.reduce_sum(wg, gd, AX))
                dve.wait_ge(rexp, 2 * L + 2)
                link(ts(w1, dv, 1.0, None, ALU.add))
                link(tt(w1, w1, wg, ALU.mult))
                link(nc.vector.reciprocal(w1, w1))
                dve.wait_ge(rank_psum, L + 1)
                for t in range(T):
                    d, s_ = ordered(place_, far, t)
                    if units == 1:
                        r_ = BANK[1][:, t * G * E:(t + 1) * G * E].rearrange("p (g c e) -> p g e c", g=G, c=2)
                    else:
                        r_ = BANK[1][:, t * G * E:(t + 1) * G * E].rearrange("p (g u c) -> p g u c", g=G, c=2)
                    i = tt(d, r_, s_, ALU.add)
                i.then_inc(place_ready, 1)
                dve.wait_ge(place_ready, L + 1)

                def one_hot(g):
                    view = lambda w: w[:, 0:T * W].rearrange("p (n s) -> p n s", s=CAP)
                    at = lambda w: w[:, 0:T * G * E].rearrange("p (g n) -> p g n", g=G)[:, bass.ds(g, 1), :].rearrange(
                        "p o n -> p (o n)").unsqueeze(2).to_broadcast([P, T * E, CAP])
                    places = const("iota")[:, 0:CAP].unsqueeze(1).to_broadcast([P, T * E, CAP])
                    tt(view(PB), places, at(place_), ALU.is_equal).then_inc(p_ready, 1)
                    return lambda: (dve.wait_ge(p_ready, g * 2 + (2 * G * L + 1)),
                                    tt(view(PW), view(PB), at(weight_by_place_), ALU.mult).then_inc(p_ready, 1))

                weighted = one_hot(0)
                link(tt(w2, w1, dv, ALU.mult))
                link(tt(oh1, oh1, w1.unsqueeze(2).to_broadcast([P, T, E]), ALU.mult))
                link(tt(oh2, oh2, w2.unsqueeze(2).to_broadcast([P, T, E]), ALU.mult))
                link(tt(cwv, oh1, oh2, ALU.add))
                link(tt(by_ge(weight_), spread_g, cwv.unsqueeze(2).to_broadcast([P, T, G, E]), ALU.mult))
                for t in range(T):
                    d, s_ = ordered(weight_by_place_, weight_, t)
                    i = cp(d, s_)
                link(i)
                stt(left_[:, 0:T * G * E], BANK[1][:, 0:T * G * E], float(CAP), weight_[:, 0:T * G * E], ALU.is_ge, ALU.mult)
                link(nc.vector.reduce_max(over_f[:, 0:1], BANK[1][:, T * G * E:3 * G * E], AX))
                link(ts(over_f[:, 0:1], over_f[:, 0:1], float(CAP), None, ALU.is_gt))
                cp(OVER_I[:, 0:1], over_f[:, 0:1]).then_inc(over_ready, 1)
                weighted()

                def gathered(g):
                    for n in range(1, gathers, 2):
                        dve.wait_ge(xc_psum, g * gathers + (gather0 + n + 1))
                        cp(xcT[:, n * CH:(n + 1) * CH], BANK[3][:, :]).then_inc(xc_dve, 1)

                def outputs(g, pair):
                    dve.wait_ge(y_psum, g * (2 * pairs) + (2 * (pair0 + pair) + 2))
                    cp(YS[:, pair % 2, 1, :], BANK[3][:, :]).then_inc(y_dve, 1)

                def transposed(g, u):
                    dve.wait_ge(hT_psum, g * units + (unit0 + u + 1))
                    cp(HT, BANK[2][:, :].rearrange("p (f s) -> p f s", f=4)).then_inc(hT_ready, 1)

                def group(g, last):
                    dve.wait_ge(pwT_psum, g * (pairs // 2) + (G * sum(PAIRS[:L]) // 2 + pairs // 2))
                    if pairs > 2:
                        cp(PWT[:, 2:4, :], BANK[3][:, :].rearrange("p (a s) -> p a s", a=2)).then_inc(pwT_dve, 1)
                    if not last:
                        one_hot(g + 1)()
                    for u in range(units):
                        if u:
                            transposed(g, u - 1)
                        dve.wait_ge(silu_done, g * units + (unit0 + u + 1))
                        dve.wait_ge(chunk_done, g * per_group + (n0 + first_chunk(units, "up", u) + 2))
                        tt(HB, SG, BANK[1][:, :], ALU.mult).then_inc(h_ready, 1)
                        if u:
                            outputs(g, u - 1)
                    if not last:
                        gathered(g + 1)
                    transposed(g, units - 1)
                    for pair in range(units - 1 if units > 1 else 0, pairs):
                        outputs(g, pair)

                gathered(0)
                with dve.Fori(0, G - 1) as g:
                    group(g, False)
                group(G - 1, True)

                v = general[L]
                dve.wait_ge(over_ready, L + 1)
                flag = dve.value_load(OVER_I[0:1, 0:1], min_val=0, max_val=1)
                with dve.If(flag > 0):
                    left = left_[:, 0:T * G * E].rearrange("p (t n) -> p t n", t=T)
                    nc.vector.memset(over_f, 0.0).then_inc(v["added"], 1)
                    with dve.Fori(0, G * 2 * units) as n:
                        for t in range(T):
                            dve.wait_ge(v["psum"], n * 8 + (4 * t + 2))
                            dve.wait_ge(v["silu_done"], n * 2 + (t + 1))
                            for e in range(per_chunk):
                                c0, c1 = e * F, (e + 1) * F
                                i = stt(HB[:, c0:c1], SG[:, c0:c1], left[:, t, bass.ds(n * per_chunk + e, 1)], BANK[1][:, c0:c1],
                                        ALU.mult, ALU.mult)
                            i.then_inc(v["h_ready"], 1)
                            dve.wait_ge(v["psum"], n * 8 + (4 * t + 3))
                            cp(HT, BANK[2][:, :].rearrange("p (f s) -> p f s", f=4)).then_inc(v["hT_ready"], 1)
                            dve.wait_ge(v["psum"], n * 8 + (4 * t + 4))
                            dve.wait_ge(v["added"], n * 2 + (t + 1))
                            for half in range(2):
                                c = X[:, t, half * CH:(half + 1) * CH]
                                i = stt(c, BANK[2 + half][:, :], 1.0 / alpha, c, ALU.mult, ALU.add)
                            i.then_inc(v["added"], 1)
                    dve.wait_ge(v["added"], G * 2 * units * T + 1)
                for t in range(T):
                    dve.wait_ge(acc_ready, 2 * L + t + 1)
                    for half in range(2):
                        c = X[:, t, half * CH:(half + 1) * CH]
                        link(stt(c, c, alpha, BANK[4 + 2 * t + half][:, :], ALU.mult, ALU.add))

            moe(0, 1, ALPHA)
            norm(1, 1, "layer", X)
            transpose_x(2)
            dve.wait_ge(proj_copied, 12)

            def sb_mask(h):
                dve.wait_ge(z_psum, h + 1)
                if h >= 4:
                    dve.wait_ge(w_log, h - 3)
                tt(ZM[h % 4], BANK[h % 2][:, 0:BL], const("strict"), ALU.add).then_inc(dve_step, 1)
                steps[0] += 1
                dve.wait_ge(dve_step, steps[0])
                stt(AN[h % 2], ZM[h % 4], -1.0, ZM[h % 4], ALU.mult, ALU.min).then_inc(z_abs, 1)

            def sb_softplus(h):
                dve.wait_ge(z_log, h + 1)
                if h >= 3:
                    dve.wait_ge(r_psum, h - 2)
                stt(SP_[h % 3], ZM[h % 4], 0.0, AN[h % 2], ALU.max, ALU.add).then_inc(sp_ready, 1)

            def sb_weight(h):
                dve.wait_ge(r_psum, h + 1)
                if h >= 2:
                    dve.wait_ge(w_ready, h - 1)
                tt(WL[h % 2], ZM[h % 4], BANK[2 + h % 2][:, 0:BL], ALU.add).then_inc(w_log, 1)

            for s in range(16 + 5):
                if s < 16:
                    sb_mask(s)
                if 0 <= s - 1 < 16:
                    sb_softplus(s - 1)
                if 0 <= s - 3 < 16:
                    sb_weight(s - 3)
                if s >= 5 and (s - 5) % 2:
                    h = s - 5
                    dve.wait_ge(sbo_psum, h + 1)
                    cp(mixT[:, h // 2, :], BANK[4 + (h // 2) % 2][:, 0:S]).then_inc(sbo_copied, 1)
            residual(N_SB + 6, ALPHA)
            norm(2, 2, "layer", X)
            moe(1, 3, ALPHA)
            norm(3, 3, "layer", X)
            norm(4, 4, "rms", U)
            transpose_x(4)

            def rope2(view):
                h = view.rearrange("p t (h d) -> p t h d", h=8)
                x1, x2 = h[:, :, :, 0:ROT], h[:, :, :, ROT:2 * ROT]
                c, s_ = (const(v).rearrange("p (t d) -> p t d", t=T).unsqueeze(2).to_broadcast([P, T, 8, ROT]) for v in ("cos2", "sin2"))
                m = [w[:, 0:T * 8 * ROT].rearrange("p (t h d) -> p t h d", t=T, h=8) for w in ROPE_TMP]
                tt(m[0], x1, c, ALU.mult)
                tt(m[1], x2, s_, ALU.mult)
                tt(m[2], x2, c, ALU.mult)
                link(tt(m[3], x1, s_, ALU.mult))
                tt(x1, m[0], m[1], ALU.subtract)
                return tt(x2, m[2], m[3], ALU.add)

            for m, view in enumerate((AQ, AK)):
                dve.wait_ge(proj_copied, 17 + m)
                rope2(view).then_inc(roped, 1)
                dve.wait_ge(roped, 6 + m)
            for r in range(2):
                dve.wait_ge(gz_psum, r + 1)
                link(cp(W0[:, 512 * r:512 * (r + 1)], BANK[r][:, :]))
            stt(W1, W0, -1.0, W0, ALU.mult, ALU.min).then_inc(gz_abs, 1)
            link(ts(W2, W0, 0.0, 1.0 / 16, ALU.min, ALU.mult))
            dve.wait_ge(gz_log, 1)
            stt(W3, W1, -1.0 / 16, W2, ALU.mult, ALU.add).then_inc(la_ready, 1)
            for r in range(2):
                dve.wait_ge(bt_psum, r + 1)
                i = cp(W0[:, 512 * r:512 * (r + 1)], BANK[2 + r][:, :])
            i.then_inc(bs_ready, 1)
            dve.wait_ge(eb_ready, 1)
            qd, ki, ke = by_key(W1), by_key(W2), by_key(W3)
            for r in range(2):
                first_ = GCH - 1 if r == 0 else 0
                link(cp(decay[:, r], qd[:, r, :, first_::GCH]))
            for n, w in enumerate((qd, ki, ke)):
                dve.wait_ge(eb_ready, n + 1)
                for r in range(2):
                    i = tt(w[:, r], w[:, r], gqT if n == 0 else gkT, ALU.mult)
                i.then_inc(qk_ready, 1)
            for b in range(2):
                dve.wait_ge(att_psum, b + 1)
                tt(att[:, 4 * b:4 * b + 4, :], BANK[b][:, :].rearrange("p (i s) -> p i s", s=P),
                   const("up_to").unsqueeze(1).to_broadcast([P, 4, P]), ALU.mult)
            dve.wait_ge(att_psum, 4)
            for b in range(2):
                i = tt(W2[:, 512 * b:512 * (b + 1)].rearrange("p (i s) -> p i s", s=P), BANK[2 + b][:, :].rearrange("p (i s) -> p i s", s=P),
                       const("from_on").unsqueeze(1).to_broadcast([P, 4, P]), ALU.mult)
            link(i)
            tt(W5, W5, W2, ALU.add).then_inc(att_ready, 1)
            dve.wait_ge(kv_psum, 2)
            dve.wait_ge(normed, 10)
            for sl in range(3):
                for r in range(2):
                    n = sl if r == 0 else 3 - sl
                    for k in range(2):
                        kvn = BANK[4 + 2 * r + n % 2][:, (n // 2) * S + k * P:(n // 2) * S + (k + 1) * P]
                        if sl == 0:
                            i = cp(state[:, r, k, 0, :], kvn)
                        else:
                            i = stt(state[:, r, k, sl, :], state[:, r, k, sl - 1, :], decay[:, r, k, n:n + 1], kvn, ALU.mult, ALU.add)
                if sl < 2:
                    link(i)
            i.then_inc(state_ready, 1)
            dve.wait_ge(silu_exp, 1)
            link(ts(W3, W3, 1.0, None, ALU.add))
            link(nc.vector.reciprocal(W3, W3))
            link(tt(by_tok2(W3), by_tok2(W3), GG, ALU.mult))
            w3h = W3.rearrange("p (i v) -> p i v", v=P)
            link(tt(w3h, w3h, gla_norm.unsqueeze(1).to_broadcast([P, 8, P]), ALU.mult))
            dve.wait_ge(go_square, 2)
            link(nc.vector.reduce_sum(go_ms, W2.rearrange("p (i v) -> p i v", v=P), AX))
            link(ts(go_ms, go_ms, 1.0 / P, RMS_EPS, ALU.mult, ALU.add))
            nc.vector.memset(go_n, 0.0).then_inc(var_ready, 1)
            dve.wait_ge(rstd_ready, 6)
            dve.wait_ge(var_ready, 6)
            sharpen(go_r, go_ms, go_n)
            w0h = W0.rearrange("p (i v) -> p i v", v=P)
            for t in range(T):
                for par in range(2):
                    i = tt(w0h[:, 4 * t + par:4 * t + 4:2, :], BANK[2 * t + par][:, 0:S].rearrange("p (i v) -> p i v", v=P),
                           go_r[:, 4 * t + par:4 * t + 4:2].unsqueeze(2).to_broadcast([P, 2, P]), ALU.mult)
            link(i)
            tt(W0, W0, W3, ALU.mult).then_inc(go_ready, 1)
            dve.wait_ge(go_ready, 1)
            dve.wait_ge(goT_ready, 1)
            attention(DIL_JOBS, len(AB_JOBS), 8, {})
            residual(N_2 + 7, 1.0)
            norm(5, 6, "rms", U)
            moe(2, 5, 1.0)
            norm(6, 7, "rms", X)


SMALL_TOTAL = 16 * (NMOE * (1 + G + 2) + 4 + 1)
NORM_OF_XT = {1: 0, 2: 2, 3: 4, 4: 8, 5: 10}
NORM_VALUE = {0: 32, 1: 32, 2: 64, 3: 64, 4: 80, 5: 80, 6: 96}


def by_tok2(w):
    return w.rearrange("p (t n) -> p t n", t=T)


_INS = ["x", "positions", "ab_w_in", "ab_w_out", "nsa_cmp_pos_k", "nsa_cmp_pos_v", "nsa_cmp_w1_k", "nsa_cmp_w2_k",
        "nsa_cmp_w1_v", "nsa_cmp_w2_v", "sb_w_in", "sb_w_out", "ln_mix_g", "ln_mix_b", "ln_ffn_g", "ln_ffn_b",
        "moe_w_grp", "moe_b_grp", "moe_w_rt", "moe_b_rt", "moe_w_gate", "moe_w_up", "moe_w_down", "norm1_w_2",
        "w_in_2", "gla_fwd_gate_w_2", "gla_fwd_gate_b_2", "gla_bwd_gate_w_2", "gla_bwd_gate_b_2",
        "gla_norm_w_2", "w_out_2", "norm2_w_2", "router_group_w_2", "router_group_b_2", "router_expert_w_2",
        "router_expert_b_2", "expert_w_gate_2", "expert_w_up_2", "expert_w_down_2", "final_norm_w_2"]


def _launchable(nc, inputs):
    arrays, a = {}, {}
    for name in _INS:
        v = np.ascontiguousarray(inputs[name])
        arrays[f"in_{name}_dram"] = v
        a[name] = nc.dram_tensor(f"in_{name}_dram", v.shape, mybir.dt.from_np(v.dtype), kind="ExternalInput").ap()
    table = np.ascontiguousarray(np.concatenate([CONST[k] for k in CONST], 1))
    arrays["constants_dram"] = table
    a["constants"] = nc.dram_tensor("constants_dram", table.shape, F32, kind="ExternalInput").ap()
    out = nc.dram_tensor("out_dram", (1, S, D), F32, kind="ExternalOutput").ap()
    build(nc, a, out)
    return arrays


def kernel(**inputs):
    import concourse.bacc as bacc
    from concourse.bass_utils import run_bass_kernel_spmd
    nc = bacc.Bacc("TRN2", target_bir_lowering=False, num_devices=1, dynamic_dma_scratch_size=1024)
    arrays = _launchable(nc, inputs)
    r = run_bass_kernel_spmd(nc, [arrays], core_ids=[0])
    return r.results[0]["out_dram"]
```

```python
import numpy as np
import concourse.bass as bass
from concourse import mybir
from concourse.alu_op_type import AluOpType as ALU
from contextlib import ExitStack

F32 = mybir.dt.float32
I32 = mybir.dt.int32
ACT = mybir.ActivationFunctionType
AX = mybir.AxisListType.X

P = 128
S = 256
T = S // P
D = 1024
KT = D // P
HD = 64
HALF = HD // 2
CH = 512
SLOT = 4096
NSLOT = 6
BIG = 1e30
ALPHA = float((2 * 2) ** 0.25)
LN_EPS = 1e-5
RMS_EPS = 1e-6
SCALE = HD ** -0.5

CMP_STRIDE = 16
NBLK = (S - 32) // CMP_STRIDE + 1
NC16 = S // CMP_STRIDE

C_KC, C_VC, C_KS, C_VS, C_KW, C_VW, C_GA, C_QM, C_KM, C_VM = (
    512, 640, 768, 896, 1024, 1152, 1280, 1304, 1816, 2328)
W_AB = 2840
C_GV, C_GG, C_LF, C_LB, C_AQ, C_AK, C_AV = 512, 1024, 1536, 1552, 1568, 2080, 2592
RANK = 16
GCH = 64
ROT = 8

MOE = [(4, 256, 2, 20), (4, 256, 2, 20), (8, 512, 8, 36)]
G = 4
CAP = 64
NMOE = len(MOE)


def _constants():
    j = np.arange(P)[:, None]
    i = np.arange(P)[None, :]
    t = np.arange(S)
    tok = np.arange(P)[:, None] + P * np.arange(T)[None, :]
    same = (j // GCH) == (i // GCH)
    z = np.zeros((P, P))
    c = {}
    c["ident"] = np.eye(P)
    tri = np.where(i > j, BIG, 0.0)
    c["inv_freq"] = np.broadcast_to(
        (np.float32(10000.0) ** (-np.arange(HALF, dtype=np.float32) / np.float32(HALF)))[None, :], (P, HALF))
    c["causal"] = np.concatenate([tri, z, tri], 1)
    st = np.where(j < i, 0.0, -BIG)
    c["strict"] = np.concatenate([st, z, st], 1)
    c["neg_suffix"] = np.where(j >= i, -1.0, 0.0)
    c["neg_ones"] = np.full((P, P), -1.0)
    c["ones"] = np.full((P, P), 1.0)
    c["before"] = np.where(j < i, 1.0, 0.0)
    c["up_to"] = np.where(same & (j <= i), 1.0, 0.0)
    c["from_on"] = np.where(same & (j >= i), 1.0, 0.0)
    n = np.arange(NC16)
    seen = (n[None, None, :] * CMP_STRIDE + 31 <= tok[:, :, None]) & (n < NBLK)[None, None, :]
    c["cmp_big"] = np.where(seen, 0.0, BIG).reshape(P, T * NC16)
    c["cmp_seen"] = np.where(seen, 1.0, 0.0).reshape(P, T * NC16)
    c["alpha"] = ALPHA * np.eye(P)
    c["own_head"] = np.where(j // NC16 == np.arange(8)[None, :], 1.0, 0.0)
    c["spread"] = np.where((j < NC16) & (i % NC16 == j), 1.0, 0.0)
    c["iota"] = np.broadcast_to(i, (P, P))
    c["descend"] = np.broadcast_to(8.0 - np.arange(8)[None, :], (P, 8))
    inv2 = np.float32(500000.0) ** (-(np.arange(0, 2 * ROT, 2, dtype=np.float32) / np.float32(2 * ROT)))
    ang = tok[:, :, None].astype(np.float32) * inv2[None, None, :].astype(np.float32)
    c["cos2"] = np.cos(ang).reshape(P, T * ROT)
    c["sin2"] = np.sin(ang).reshape(P, T * ROT)
    d = np.abs(tok[:, :, None] - t[None, None, :])
    count = (d <= 64).astype(float) + (d % 4 == 0) + (d % 16 == 0)
    c["count"] = count.reshape(P, T * S)
    c["unseen"] = np.where(count > 0, 0.0, BIG).reshape(P, T * S)
    return {k: np.ascontiguousarray(v, dtype=np.float32) for k, v in c.items()}


CONST = _constants()
CONST_AT = {}
_at = 0
for _k, _v in CONST.items():
    CONST_AT[_k] = (_at, _v.shape[1])
    _at += _v.shape[1]
CONST_W = _at
FIRST_CONSTS = P + HALF


UNITS = [m[2] // 2 for m in MOE]
PAIRS = [m[0] // 2 for m in MOE]
GATHERS = [KT * m[0] * CAP // CH for m in MOE]
N_AB = 0
CMP_CHUNK = 6
N_M0 = N_AB + 9
N_SB = N_M0 + 6 * G * UNITS[0]
N_M1 = N_SB + 8
N_2 = N_M1 + 6 * G * UNITS[1]
N_M2 = N_2 + 9
N_MOE = [N_M0, N_M1, N_M2]
CMP_DMAS = 4


def loaded_value(n):
    v = 16 * (n // NSLOT + 1)
    if n >= CMP_CHUNK and (n - CMP_CHUNK) % NSLOT == 0:
        v += 16 * (CMP_DMAS - 1)
    return v


def expert_order(units):
    order = []
    for u in range(units):
        order += [("gate", u), ("up", u)]
        if u:
            order.append(("down", u - 1))
    return order + [("down", units - 1)]


def first_chunk(units, kind, u):
    return 2 * expert_order(units).index((kind, u))


AB_JOBS = [("moba", h) for h in range(8)]
for _i in range(4):
    AB_JOBS += [("slc", 2 * _i), ("slc", 2 * _i + 1), ("win", 2 * _i), ("win", 2 * _i + 1)]
DIL_JOBS = [("dil", h) for h in range(8)]


def job_pair(job):
    kind, h = job
    return h // 2 + (4 if kind in ("slc", "win") else 0)


def job_tile(job):
    kind, h = job
    return h // 2 + (0 if kind in ("slc", "win") else 4)


def last_of_pair(jobs, j):
    return j + 1 == len(jobs) or job_pair(jobs[j + 1]) != job_pair(jobs[j])


def first_of_pair(jobs, j):
    return j == 0 or job_pair(jobs[j - 1]) != job_pair(jobs[j])


def tile_no(k, t):
    return 7 + 2 * t + (k - 3) if k in (3, 4) else 2 * k + t + 1


def root_no(k, t):
    return tile_no(k, t) + (k > 4)


NORM_OF_XT = {1: 0, 2: 1, 3: 2, 4: 4, 5: 5}


def build(nc, a, out):
    ctx = ExitStack()
    with ctx:
        def sb(name, cols, dt=F32):
            return ctx.enter_context(nc.sbuf_tensor(name, [P, cols], dt))

        def sem(name):
            return ctx.enter_context(nc.semaphore(name))

        WEIGHTS = sb("weights", NSLOT * SLOT)
        CONSTS = sb("consts", CONST_W)
        X_ = sb("residual", T * D)
        XT_ = sb("x_transposed", KT * S)
        MIX = sb("mixed", T * D)
        NORM_ = sb("norm_params", 2 * 2 * D)
        PJ = sb("projected", 6208)
        QK = sb("heads_transposed", 14 * S)
        WK = sb("work", 4352)
        SMALL = sb("small_params", 2000)
        MISC = sb("misc", 2200)
        GATE_W = sb("gla_gate_w", 2 * S)
        POS_I = sb("positions", T, I32)
        OVER_I = sb("overflow", 1, I32)
        BANK = [ctx.enter_context(nc.psum_tensor(f"bank{i}", [P, CH], F32)) for i in range(8)]

        def const(name):
            o, n = CONST_AT[name]
            return CONSTS[:, o:o + n]

        ident = const("ident")
        X = X_[:, :].rearrange("p (t d) -> p t d", t=T)
        XT = XT_[:, :].rearrange("p (k s) -> p k s", k=KT)
        mixT = MIX[:, :].rearrange("p (k s) -> p k s", k=KT)
        U = MIX[:, :].rearrange("p (t d) -> p t d", t=T)
        NORM = NORM_[:, :].rearrange("p (b w d) -> p b w d", b=2, w=2)

        def slot(n):
            return WEIGHTS[:, (n % NSLOT) * SLOT:(n % NSLOT + 1) * SLOT]

        small_at = [0]

        def small(n):
            small_at[0] += n
            assert small_at[0] <= 2000
            return SMALL[:, small_at[0] - n:small_at[0]]

        misc_at = [0]

        def misc(n):
            misc_at[0] += n
            assert misc_at[0] <= 2200
            return MISC[:, misc_at[0] - n:misc_at[0]]

        router_w = [small(KT * m[3]).rearrange("p (k n) -> p k n", k=KT) for m in MOE]
        router_b = [small(m[3]) for m in MOE]
        cmp_w2 = small(2 * HD).rearrange("p (v d) -> p v d", v=2)
        cmp_pos = small(2 * P).rearrange("p (v d) -> p v d", v=2)
        gla_norm = small(P)

        cos1, sin1, angle, turns = (misc(T * HALF) for _ in range(4))
        pos_f = misc(T)
        cmp_posT = misc(2 * NC16).rearrange("p (v c) -> p v c", v=2)
        stats = misc(T * 12).rearrange("p (t w) -> p t w", t=T)
        mean_var = misc(T * 2).rearrange("p (t w) -> p t w", t=T)
        veps, lnv, rstd, newton = (misc(8) for _ in range(4))
        least = misc(8).rearrange("p (b t) -> p b t", b=4)
        psums = misc(8).rearrange("p (b t) -> p b t", b=4)
        rinv = misc(8).rearrange("p (b t) -> p b t", b=4)

        slot_loaded = [sem(f"slot{i}_loaded") for i in range(NSLOT)]
        x_loaded = sem("x_loaded")
        first_consts_loaded = sem("first_consts_loaded")
        consts_loaded = sem("consts_loaded")
        positions_loaded = sem("positions_loaded")
        cmp_small_loaded = sem("cmp_small_loaded")
        small_loaded = sem("small_loaded")
        norm_loaded = [sem("norm0_loaded"), sem("norm1_loaded")]
        chunk_done = sem("chunk_done")
        xt_psum = sem("xt_psum")
        xt_act = sem("xt_act")
        xt_dve = sem("xt_dve")
        proj_copied = sem("proj_copied")
        roped = sem("roped")
        qt_psum = sem("qt_psum")
        qt_act = sem("qt_act")
        kv2_ready = sem("kv2_ready")
        angle_ready = sem("angle_ready")
        sines_ready = sem("sines_ready")
        gates_exp = sem("gates_exp")
        gates_ready = sem("gates_ready")
        dve_step = sem("dve_step")
        act_step = sem("act_step")
        pool_step = sem("pool_step")
        pos_psum = sem("pos_psum")
        pos_ready = sem("pos_ready")
        hid_exp_in = sem("hid_exp_in")
        hid_exp = sem("hid_exp")
        hid_ready = sem("hid_ready")
        hidT_psum = sem("hidT_psum")
        hidT_ready = sem("hidT_ready")
        kcvc_psum = sem("kcvc_psum")
        kcvc_ready = sem("kcvc_ready")
        cmp_scores = sem("cmp_scores")
        cmp_exp_in = sem("cmp_exp_in")
        cmp_exp = sem("cmp_exp")
        cmp_probs = sem("cmp_probs")
        cmp_pT_psum = sem("cmp_pT_psum")
        cmp_pT = sem("cmp_pT")
        scores_ready = sem("scores_ready")
        mins_ready = sem("mins_ready")
        probs_ready = sem("probs_ready")
        scaled_ready = sem("scaled_ready")
        pt_psum = sem("pt_psum")
        pt_copied = sem("pt_copied")
        pv_done = sem("pv_done")
        o_copied = sem("o_copied")
        out_psum = sem("out_psum")
        var_ready = sem("var_ready")
        rstd_ready = sem("rstd_ready")
        normed = sem("normed")
        logits_psum = sem("logits_psum")
        rexp_in = sem("rexp_in")
        rexp = sem("rexp")
        onehot_ready = sem("onehot_ready")
        rank_psum = sem("rank_psum")
        place_ready = sem("place_ready")
        over_ready = sem("over_ready")
        z_psum = sem("z_psum")
        z_masked = sem("z_masked")
        z_log = sem("z_log")
        sp_ready = sem("sp_ready")
        r_psum = sem("r_psum")
        w_log = sem("w_log")
        w_ready = sem("w_ready")
        sbo_psum = sem("sbo_psum")
        sbo_copied = sem("sbo_copied")
        gz_psum = sem("gz_psum")
        gz_abs = sem("gz_abs")
        gz_log = sem("gz_log")
        la_ready = sem("la_ready")
        bt_psum = sem("bt_psum")
        bs_ready = sem("bs_ready")
        eb_ready = sem("eb_ready")
        qk_ready = sem("qk_ready")
        ket_psum = sem("ket_psum")
        ket_ready = sem("ket_ready")
        att_psum = sem("att_psum")
        att_ready = sem("att_ready")
        kv_psum = sem("kv_psum")
        state_ready = sem("state_ready")
        go_psum = sem("go_psum")
        go_square = sem("go_square")
        go_ready = sem("go_ready")
        goT_psum = sem("goT_psum")
        goT_ready = sem("goT_ready")
        silu_exp = sem("silu_exp")
        out_stored = sem("out_stored")

        p_ready = sem("p_ready")
        pwT_psum = sem("pwT_psum")
        pwT_act = sem("pwT_act")
        pwT_dve = sem("pwT_dve")
        xc_psum = sem("xc_psum")
        xc_act = sem("xc_act")
        xc_dve = sem("xc_dve")
        silu_done = sem("silu_done")
        h_ready = sem("h_ready")
        hT_psum = sem("hT_psum")
        hT_ready = sem("hT_ready")
        y_psum = sem("y_psum")
        y_act = sem("y_act")
        y_dve = sem("y_dve")
        acc_ready = sem("acc_ready")
        GENERAL_SIGNALS = ("loaded", "psum", "silu_done", "h_ready", "hT_ready", "sums_kept")
        general = [{k: sem(f"general{L}_" + k) for k in GENERAL_SIGNALS} for L in range(NMOE)]

        pj = PJ[:, 0:T * W_AB].rearrange("p (t n) -> p t n", t=T)
        qk = QK[:, :].rearrange("p (n s) -> p n s", s=S)
        kv2 = MIX[:, 0:4 * S].rearrange("p (v h s) -> p v h s", v=2, h=2)
        ROPE_TMP = [WK[:, 512 * i:512 * (i + 1)] for i in range(4)]
        SM = [WK[:, 512 * i:512 * (i + 1)] for i in range(2)]
        PR = [WK[:, 1024 + 512 * i:1024 + 512 * (i + 1)] for i in range(3)] + [XT_[:, 1024:1536]]
        PTS = [WK[:, 2560:3072], WK[:, 3072:3584], XT_[:, 0:512], XT_[:, 512:1024]]

        hid_g = misc(2 * P)
        hid_t = misc(2 * P)
        hidT = misc(2 * 32).rearrange("p (v n) -> p v n", v=2)
        kcT = misc(NC16)
        vc = misc(P)
        v_blocks = PJ[:, 5680:5680 + 512].rearrange("p (h d) -> p h d", h=8)
        cmp_p = hid_g.rearrange("p (t h n) -> p t h n", t=T, h=8)
        cmp_m = misc(16).rearrange("p (t h) -> p t h", t=T)
        cmp_pT_sb = misc(S)

        def heads(view, col, n):
            return view[:, :, col:col + n * HD].rearrange("p t (h x d) -> p t h x d", x=2, d=HALF)

        def job_operands(job):
            kind, h = job
            if kind == "moba":
                r = HD * (h % 2)
                return qk[r:r + HD, 6 + h // 2, :], qk[r:r + HD, 10 + h // 2, :], pj[:, :, C_VM + HD * h:C_VM + HD * h + HD], None
            if kind == "dil":
                r = HD * (h % 2)
                return qk[r:r + HD, h // 2, :], qk[r:r + HD, 4 + h // 2, :], AV[:, :, HD * h:HD * h + HD], None
            kv = h // 4
            r = HD * kv
            k, v, gate = (4, C_VS, 1) if kind == "slc" else (5, C_VW, 2)
            return qk[r:r + HD, h % 4, :], qk[r:r + HD, k, :], pj[:, :, v + HD * kv:v + HD * kv + HD], pj[:, :, C_GA + 3 * h + gate]

        sbQ = PJ[:, 0:8 * S].rearrange("p (n s) -> p n s", s=S)
        sbK = PJ[:, 8 * S:16 * S].rearrange("p (n s) -> p n s", s=S)
        sbV = PJ[:, 16 * S:16 * S + T * D].rearrange("p (t n) -> p t n", t=T)
        BL = 3 * P
        ZM = [QK[:, BL * i:BL * (i + 1)] for i in range(4)]
        WT = [QK[:, BL * (4 + i):BL * (5 + i)] for i in range(4)]
        AN = [WK[:, BL * i:BL * (i + 1)] for i in range(2)]
        SP_ = [WK[:, BL * (2 + i):BL * (3 + i)] for i in range(3)]
        WL = [WK[:, BL * (5 + i):BL * (6 + i)] for i in range(2)]

        GV, GG, AQ, AK, AV = (PJ[:, 1024 * i:1024 * (i + 1)].rearrange("p (t n) -> p t n", t=T) for i in range(5))
        W5 = PJ[:, 5120:6144]
        gqT, gkT = qk[:, 8:10, :], qk[:, 10:12, :]
        LR = QK[:, 12 * S:14 * S].rearrange("p (r s) -> p r s", r=2)
        W0, W1, W2, W3 = (WK[:, 1024 * i:1024 * (i + 1)] for i in range(4))
        by_tok = lambda w: w.rearrange("p (r t n) -> p r t n", r=2, t=T)
        by_key = lambda w: w.rearrange("p (r k s) -> p r k s", r=2, k=2)
        gw = GATE_W[:, :].rearrange("p (r n) -> p r n", r=2)
        decay = misc(16).rearrange("p (r k n) -> p r k n", r=2, k=2)
        state = MIX[:, 0:1536].rearrange("p (r k n v) -> p r k n v", r=2, k=2, n=3)
        att = W5.rearrange("p (i s) -> p i s", s=P)
        go_ms = misc(8)
        go_r = misc(8)
        go_l = misc(8)
        go_n = misc(8)

        xcT = PJ[:, 0:KT * 8 * CAP]
        U2 = PJ[:, KT * 8 * CAP:KT * 8 * CAP + T * D].rearrange("p (t d) -> p t d", t=T)
        PB, PW = QK[:, 0:1024], QK[:, 1024:2048]
        PWT = QK[:, 2048:3072].rearrange("p (a s) -> p a s", a=4)
        SG, HB = WK[:, 0:512], WK[:, 512:1024]
        HT = WK[:, 1024:1536].rearrange("p (f s) -> p f s", f=4)
        YS = WK[:, 1536:3584].rearrange("p (a h d) -> p a h d", a=2, h=2)
        work_at = [3584]

        def work(n):
            work_at[0] += n
            assert work_at[0] <= 4352
            return WK[:, work_at[0] - n:work_at[0]]

        rlog = work(T * 36)
        rt = work(T * 32)
        small_r = [work(16) for i in range(14)]
        chosen_, weight_, left_ = (work(T * 32) for _ in range(3))
        place_, weight_by_place_ = (misc(T * 32) for _ in range(2))
        over_f = misc(2)

        W_NCOLS = [512, 512, 280, 512, 512, 512]
        W_COL0 = [0, 512, 1024, 1304, 1816, 2328]
        W2_NCOLS = [512, 512, 32, 512, 512, 512, 512]
        W2_COL0 = [C_GV, 0, C_LF, C_GG, C_AQ, C_AK, C_AV]

        block = ctx.enter_context(nc.Block())

        @block.sync
        def _(sp):
            def free_slot(n):
                if n >= NSLOT:
                    sp.wait_ge(chunk_done, n - NSLOT + 1)

            def load_cols(n, w, col, ncols):
                free_slot(n)
                sp.dma_start(slot(n)[:, 0:KT * ncols].rearrange("p (k c) -> p k c", k=KT),
                             w.rearrange("(p k) c -> p k c", k=KT)[:, :, col:col + ncols]).then_inc(slot_loaded[n % NSLOT], 16)

            def load_out(n, w, half):
                free_slot(n)
                sp.dma_start(slot(n).rearrange("p (k c) -> p k c", k=KT),
                             w.rearrange("(k p) c -> p k c", p=P)[:, :, half * CH:(half + 1) * CH]).then_inc(slot_loaded[n % NSLOT], 16)

            def load_norm(k, params):
                if k >= 2:
                    sp.wait_ge(normed, tile_no(k - 2, 1))
                for i, v in enumerate(params):
                    sp.dma_start(NORM[:, k % 2, i, :], v.partition_broadcast(P)).then_inc(norm_loaded[k % 2], 16)

            def expert_source(L, kind, e):
                name = ("moe_w_", "moe_w_", "expert_w_")[L] + kind + ("", "", "_2")[L]
                w = a[name][L if L < 2 else 0]
                if MOE[L][1] == CH:
                    w = w[bass.ds(e, 1)]
                    if kind == "down":
                        return w.rearrange("a (p f) d -> p (a f d)", p=P)
                    return w.rearrange("a (p k) f -> p (a k f)", p=P)
                w = w[bass.ds(e * 2, 2)]
                if kind == "down":
                    return w.rearrange("a (p f) d -> p a (f d)", p=P)
                return w.rearrange("a (p k) f -> p a (k f)", p=P)

            def unit_slot(L, n):
                return slot(n) if MOE[L][1] == CH else slot(n).rearrange("p (a w) -> p a w", a=2)

            def moe(L):
                n0, units = N_MOE[L], UNITS[L]
                per_group = 6 * units
                with sp.Fori(0, G) as g:
                    for j in range(per_group):
                        kind, u = expert_order(units)[j // 2]
                        n = n0 + j
                        sp.wait_ge(chunk_done, g * per_group + (n - NSLOT + 1))
                        sp.dma_start(unit_slot(L, n), expert_source(L, kind, g * (2 * units) + (2 * u + j % 2))
                                     ).then_inc(slot_loaded[n % NSLOT], 16)
                v = general[L]
                sp.wait_ge(over_ready, L + 1)
                flag = sp.value_load(OVER_I[0:1, 0:1], min_val=0, max_val=1)
                with sp.If(flag > 0):
                    sp.wait_ge(chunk_done, n0 + G * per_group)
                    def load_unit(n):
                        for i, kind in enumerate(("gate", "up", "down")):
                            sp.dma_start(unit_slot(L, i), expert_source(L, kind, n)).then_inc(v["loaded"], 16)

                    load_unit(0)
                    with sp.Fori(1, G * 2 * units) as n:
                        sp.wait_ge(v["psum"], n * 8)
                        load_unit(n)
                    sp.wait_ge(v["psum"], 8 * G * 2 * units)

            x_src = a["x"][0].rearrange("(t p) d -> p t d", p=P)
            for t in range(T):
                sp.dma_start(X[:, t, :], x_src[:, t, :]).then_inc(x_loaded, 16)
            w = a["ab_w_in"][0]
            for c in range(6):
                load_cols(N_AB + c, w, W_COL0[c], W_NCOLS[c])
            for L in range(NMOE):
                E = MOE[L][0]
                wg, bg, we, be = ((a["moe_w_grp"][L], a["moe_b_grp"][L], a["moe_w_rt"][L], a["moe_b_rt"][L]) if L < 2 else
                                  (a["router_group_w_2"][0], a["router_group_b_2"][0], a["router_expert_w_2"][0], a["router_expert_b_2"][0]))
                sp.dma_start(router_w[L][:, :, 0:G], wg.rearrange("(p k) g -> p k g", k=KT)).then_inc(small_loaded, 16)
                for g in range(G):
                    sp.dma_start(router_w[L][:, :, G + g * E:G + (g + 1) * E], we[g].rearrange("(p k) e -> p k e", k=KT)).then_inc(small_loaded, 16)
                sp.dma_start(router_b[L][:, 0:G], bg.partition_broadcast(P)).then_inc(small_loaded, 16)
                sp.dma_start(router_b[L][:, G:G + G * E], be.rearrange("g e -> (g e)").partition_broadcast(P)).then_inc(small_loaded, 16)
            for r, n in enumerate(("gla_fwd_gate_", "gla_bwd_gate_")):
                sp.dma_start(gw[0:RANK, r, :], a[n + "w_2"][0]).then_inc(small_loaded, 16)
                sp.dma_start(gw[RANK:RANK + 1, r, :], a[n + "b_2"]).then_inc(small_loaded, 16)
            sp.dma_start(gla_norm, a["gla_norm_w_2"][0].partition_broadcast(P)).then_inc(small_loaded, 16)
            free_slot(CMP_CHUNK)
            cslot = slot(CMP_CHUNK).rearrange("p (v c n) -> p v c n", v=2, c=NC16)
            for i, name in enumerate(("nsa_cmp_w1_k", "nsa_cmp_w1_v")):
                for h in range(2):
                    sp.dma_start(cslot[HD * h:HD * h + HD, i, :, :],
                                 a[name][0][h * 1024:(h + 1) * 1024, :].rearrange("(c d) n -> d c n", d=HD)
                                 ).then_inc(slot_loaded[CMP_CHUNK % NSLOT], 16)
            load_norm(0, (a["ln_mix_g"][0], a["ln_mix_b"][0]))
            for half in range(2):
                load_out(N_AB + 7 + half, a["ab_w_out"][0], half)
            moe(0)
            load_norm(1, (a["ln_ffn_g"][0], a["ln_ffn_b"][0]))
            for n, c in enumerate((4, 5, 0, 1, 2, 3)):
                load_cols(N_SB + n, a["sb_w_in"][0], c * CH, CH)
            load_norm(2, (a["ln_mix_g"][1], a["ln_mix_b"][1]))
            for half in range(2):
                load_out(N_SB + 6 + half, a["sb_w_out"][0], half)
            moe(1)
            load_norm(3, (a["ln_ffn_g"][1], a["ln_ffn_b"][1]))
            load_norm(4, (a["norm1_w_2"][0],))
            for c in range(7):
                load_cols(N_2 + c, a["w_in_2"][0], W2_COL0[c], W2_NCOLS[c])
            load_norm(5, (a["norm2_w_2"][0],))
            for half in range(2):
                load_out(N_2 + 7 + half, a["w_out_2"][0], half)
            moe(2)
            load_norm(6, (a["final_norm_w_2"],))
            o = out[0].rearrange("(t p) d -> p t d", p=P)
            for t in range(T):
                sp.wait_ge(normed, 12 + t + 1)
                sp.dma_start(o[:, t, :], X[:, t, :]).then_inc(out_stored, 16)
            sp.wait_ge(out_stored, 16 * T)

        @block.gpsimd
        def _(pool):
            pool.wait_ge(normed, 10)
            nc.gpsimd.memset(LR[0:RANK + 1, :, :], 1.0).then_inc(pool_step, 1)

        @block.tensor
        def _(pe):
            mm = nc.tensor.matmul

            def chunk_loaded(n):
                pe.wait_ge(slot_loaded[n % NSLOT], loaded_value(n))

            def transpose_x(k, src, waits, then=None):
                for t in range(T):
                    waits(t)
                    for kt in range(KT):
                        i = nc.tensor.transpose(BANK[2 * t + kt // 4][:, (kt % 4) * P:(kt % 4 + 1) * P], src[:, t, kt::KT], ident)
                        if kt % 4 == 3:
                            i.then_inc(xt_psum, 1)
                    if t < T - 1 and then:
                        pe.wait_ge(xt_act, 3 * k + 2)
                        then(t)
                pe.wait_ge(xt_act, 3 * k + 3)
                pe.wait_ge(xt_dve, k + 1)
                if then:
                    then(T - 1)

            def keep_clock_up(n, bank):
                for _ in range(n):
                    mm(BANK[bank][:, :], ident, XT_[:, 0:CH], start=True, stop=True)

            def project(n, ncols, seq, between=None, tiles=range(T)):
                if seq >= 2:
                    pe.wait_ge(proj_copied, seq - 1)
                chunk_loaded(n)
                w = slot(n)[:, 0:KT * ncols].rearrange("p (k c) -> p k c", k=KT)
                for t in tiles:
                    for kt in range(KT):
                        i = mm(BANK[4 + 2 * (seq % 2) + t][:, 0:ncols], XT[:, kt, t * P:(t + 1) * P], w[:, kt, :],
                               start=kt == 0, stop=kt == KT - 1)
                    if t == 0 and between:
                        between()
                if t == T - 1:
                    i.then_inc(chunk_done, 1)

            def project_T(n, seq, tiles, width=P):
                if seq >= 2:
                    pe.wait_ge(proj_copied, seq - 1)
                chunk_loaded(n)
                w = slot(n)[:, 0:KT * tiles * width].rearrange("p (k c) -> p k c", k=KT)
                for c in range(tiles):
                    for kt in range(KT):
                        i = mm(BANK[4 + 2 * (seq % 2) + c // 2][0:width, (c % 2) * S:(c % 2 + 1) * S],
                               w[:, kt, c * width:(c + 1) * width], XT[:, kt, :], start=kt == 0, stop=kt == KT - 1)
                i.then_inc(chunk_done, 1)

            def project_out(n):
                for half in range(2):
                    chunk_loaded(n + half)
                    w = slot(n + half).rearrange("p (k c) -> p k c", k=KT)
                    for t in range(T):
                        for kt in range(KT):
                            i = mm(BANK[4 + 2 * half + t][:, :], mixT[:, kt, t * P:(t + 1) * P], w[:, kt, :],
                                   start=kt == 0, stop=kt == KT - 1)
                        if half and t == 0:
                            i.then_inc(out_psum, 1)
                    i.then_inc(chunk_done, 1)

            def attention(jobs, first, pairs0, extras):
                dil = jobs[0][0] == "dil"

                def scores(j):
                    J = first + j
                    q, k, _, _ = job_operands(jobs[j])
                    if J >= 2:
                        pe.wait_ge(mins_ready, J - 1)
                    if dil:
                        for t in range(T):
                            i = mm(BANK[J % 2][:, t * S:(t + 1) * S], q[:, t * P:(t + 1) * P], k, start=True, stop=True)
                    else:
                        mm(BANK[J % 2][:, 0:P], q[:, 0:P], k[:, 0:P], start=True, stop=True)
                        i = mm(BANK[J % 2][:, P:3 * P], q[:, P:S], k, start=True, stop=True)
                    i.then_inc(scores_ready, 1)

                def transposed(j):
                    J = first + j
                    pe.wait_ge(scaled_ready, J + 1)
                    if J >= 2:
                        pe.wait_ge(pt_copied, J - 1)
                    pr, b = PR[J % 4], BANK[2 + J % 2]
                    for blk, src in enumerate((0, 2, 1, 3) if dil else (0, 1, 2)):
                        i = nc.tensor.transpose(b[:, blk * P:(blk + 1) * P], pr[:, src * P:(src + 1) * P], ident)
                    i.then_inc(pt_psum, 1)

                def values(j):
                    two = (j - 1, j)
                    kind, h = jobs[j - 1]
                    pair = (h // 2 if dil else job_pair(jobs[j])) + pairs0
                    ob = BANK[4 + pair % 2]
                    opens = first_of_pair(jobs, j - 1)
                    if opens and pair >= 2:
                        pe.wait_ge(o_copied, pair - 1)
                    gated = kind in ("slc", "win")
                    if gated and opens:
                        if h == 0:
                            pe.wait_ge(cmp_pT, 1)
                        mm(ob[:, 0:S], v_blocks[:, h:h + 2, :], cmp_pT_sb, start=True, stop=False)
                    pe.wait_ge(pt_copied, first + j + 1)
                    closes = last_of_pair(jobs, j)
                    for t in range(T):
                        q0 = 0 if dil or t == 0 else P
                        k0 = t * S
                        for jj in two:
                            r = HD * (jobs[jj][1] % 2)
                            v = job_operands(jobs[jj])[2]
                            i = mm(ob[r:r + HD, q0:S], v[:, t, :], PTS[(first + jj) % 4][:, k0:k0 + S - q0],
                                   start=t == 0 and not gated, stop=t == T - 1 and closes)
                            if t == T - 1:
                                i.then_inc(pv_done, 1)

                for s in range(len(jobs) + 4):
                    if s < len(jobs):
                        scores(s)
                    if s in extras:
                        extras[s]()
                    if 0 <= s - 3 < len(jobs):
                        transposed(s - 3)
                    if s >= 5 and s % 2:
                        values(s - 4)

            pe.wait_ge(first_consts_loaded, 16)
            transpose_x(0, X, lambda t: pe.wait_ge(x_loaded, 16 * T) if t == 0 else None)

            def tr(k, aps):
                if k >= 4:
                    for s_, v in {4: [(qt_act, 1)], 5: [(qt_act, 2)], 6: [(kv2_ready, 1)], 7: [(kv2_ready, 2)], 8: [(qt_act, 3)]}[k]:
                        pe.wait_ge(s_, v)
                for n, ap in enumerate(aps):
                    i = nc.tensor.transpose(BANK[k % 4][:, n * P:(n + 1) * P], ap, ident)
                i.then_inc(qt_psum, 1)

            project(0, 512, 0)
            project(1, 512, 1)
            pe.wait_ge(cmp_small_loaded, 64)
            for v in range(2):
                i = nc.tensor.transpose(BANK[3][:, v * NC16:(v + 1) * NC16], cmp_pos[0:NC16, v, :], ident[0:NC16, 0:NC16])
            i.then_inc(pos_psum, 1)
            project(2, 280, 2)
            pe.wait_ge(roped, 1)
            for k in range(2):
                tr(k, [pj[:, t, P * j:P * (j + 1)] for j in (2 * k, 2 * k + 1) for t in range(T)])
            pe.wait_ge(roped, 2)
            pe.wait_ge(pos_ready, 1)
            tr(2, [pj[:, t, c:c + P] for c in (C_KS, C_KC) for t in range(T)])
            tr(3, [pj[:, t, C_VC:C_VC + P] for t in range(T)])
            project(3, 512, 3)
            pe.wait_ge(roped, 3)
            tr(4, [pj[:, t, C_KW:C_KW + P] for t in range(T)])
            project(4, 512, 4)
            pe.wait_ge(roped, 4)
            for k in range(2):
                tr(5 + k, [pj[:, t, C_QM + P * j:C_QM + P * (j + 1)] for j in (2 * k, 2 * k + 1) for t in range(T)])

            def moba_keys():
                pe.wait_ge(roped, 5)
                for k in range(2):
                    tr(7 + k, [pj[:, t, C_KM + P * j:C_KM + P * (j + 1)] for j in (2 * k, 2 * k + 1) for t in range(T)])

            project(5, 512, 5, moba_keys)

            cw1 = slot(CMP_CHUNK).rearrange("p (v c n) -> p v c n", v=2, c=NC16)

            def cmp_hidden():
                chunk_loaded(CMP_CHUNK)
                pe.wait_ge(kv2_ready, 2)
                pe.wait_ge(proj_copied, 6)
                for v in range(2):
                    kvv = kv2[:, v, :, :].rearrange("p h (n c) -> p (h n) c", c=NC16)
                    for c in range(NC16):
                        i = mm(BANK[6][0:2 * NC16, v * P:(v + 1) * P], kvv[:, :, c], cw1[:, v, c, :],
                               start=c == 0, stop=c == NC16 - 1)
                i.then_inc(chunk_done, 1)

            def cmp_hiddenT():
                pe.wait_ge(hid_ready, 1)
                for v in range(2):
                    i = nc.tensor.transpose(BANK[7][:, v * 32:v * 32 + 2 * NC16], hid_g[0:2 * NC16, v * P:(v + 1) * P],
                                            ident[0:2 * NC16, 0:2 * NC16])
                i.then_inc(hidT_psum, 1)

            def cmp_keys():
                pe.wait_ge(hidT_ready, 1)
                for h in range(2):
                    mm(BANK[7][HD * h:HD * h + HD, 64:64 + NBLK], cmp_w2[:, 0, :], hidT[:, 0, NC16 * h:NC16 * h + NBLK], start=True, stop=True)
                for h in range(2):
                    i = mm(BANK[7][0:NBLK, P + HD * h:P + HD * (h + 1)], hidT[:, 1, NC16 * h:NC16 * h + NBLK], cmp_w2[:, 1, :], start=True, stop=True)
                i.then_inc(kcvc_psum, 1)

            def cmp_score():
                pe.wait_ge(kcvc_ready, 1)
                pe.wait_ge(consts_loaded, 16)
                mm(BANK[7][:, 0:P], const("spread")[0:NBLK, :], vc[0:NBLK, :], start=True, stop=True)
                for h in range(8):
                    for t in range(T):
                        r = HD * (h // 4)
                        col = S + (t * 4 + h % 4) * NC16
                        i = mm(BANK[7 - h // 4][:, col:col + NBLK], qk[r:r + HD, h % 4, t * P:(t + 1) * P], kcT[r:r + HD, 0:NBLK], start=True, stop=True)
                i.then_inc(cmp_scores, 1)

            def cmp_transpose():
                pe.wait_ge(cmp_probs, 1)
                for t in range(T):
                    i = nc.tensor.transpose(BANK[6][:, S + t * P:S + (t + 1) * P], cmp_p[:, t, :, :].rearrange("p h n -> p (h n)"), ident)
                i.then_inc(cmp_pT_psum, 1)

            pe.wait_ge(qt_act, 7)
            attention(AB_JOBS, 0, 0, {2: cmp_hidden, 6: cmp_hiddenT, 7: cmp_keys, 8: cmp_score, 11: cmp_transpose})
            pe.wait_ge(o_copied, 8)
            project_out(N_AB + 7)

            def moe(L, k, src):
                E, F, _, NR = MOE[L]
                units, pairs, gathers = UNITS[L], PAIRS[L], GATHERS[L]
                n0, per_group = N_MOE[L], 6 * units
                unit0, pair0, gather0 = G * sum(UNITS[:L]), G * sum(PAIRS[:L]), G * sum(GATHERS[:L])
                W = E * CAP
                pairs_per_unit = pairs // units

                def logits(t):
                    for kt in range(KT):
                        i = mm(BANK[0][:, t * 64:t * 64 + NR], XT[:, kt, t * P:(t + 1) * P], router_w[L][:, kt, :],
                               start=kt == 0, stop=kt == KT - 1)
                    if t == T - 1:
                        i.then_inc(logits_psum, 1)

                pe.wait_ge(small_loaded, SMALL_TOTAL)
                transpose_x(k, src, lambda t: pe.wait_ge(normed, tile_no(NORM_OF_XT[k], t)), logits)
                for t in range(T):
                    for half in range(2):
                        mm(BANK[4 + 2 * t + half][:, :], const("alpha") if L < 2 else ident, X[:, t, half * CH:(half + 1) * CH],
                           start=True, stop=False)
                pe.wait_ge(onehot_ready, L + 1)
                A = [chosen_[:, t * G * E:(t + 1) * G * E] for t in range(T)]
                rank = [BANK[1][:, n * G * E:(n + 1) * G * E] for n in range(3)]
                mm(rank[0], const("before"), A[0], start=True, stop=True)
                mm(rank[1], const("ones"), A[0], start=True, stop=False)
                mm(rank[1], const("before"), A[1], start=False, stop=True)
                mm(rank[2], const("ones"), A[0], start=True, stop=False)
                mm(rank[2], const("ones"), A[1], start=False, stop=True).then_inc(rank_psum, 1)
                keep_clock_up(1, 2)

                def gather(g, after_two=None):
                    pe.wait_ge(p_ready, (g + G * L) * 2 + 1)
                    per_bank = KT // gathers
                    for n in range(gathers):
                        if n >= 2:
                            pe.wait_ge((xc_act, xc_dve)[n % 2], (g * gathers + gather0) // 2 + n // 2 if isinstance(g, int)
                                       else g * (gathers // 2) + (gather0 // 2 + n // 2))
                        for j in range(per_bank):
                            kt = n * per_bank + j
                            for t in range(T):
                                i = mm(BANK[2 + n % 2][:, j * W:(j + 1) * W], src[:, t, kt::KT], PB[:, t * W:(t + 1) * W],
                                       start=t == 0, stop=t == T - 1)
                        i.then_inc(xc_psum, 1)
                        if n == 1 and after_two:
                            after_two()

                def group(g, last):
                    x = xcT[:, 0:KT * W].rearrange("p (k s) -> p k s", k=KT)

                    def load(kind, u):
                        for c in range(2):
                            n = n0 + first_chunk(units, kind, u) + c
                            pe.wait_ge(slot_loaded[n % NSLOT], g * (16 * per_group // NSLOT) + loaded_value(n))
                        return [slot(n - 1), slot(n)]

                    def hidden(kind, u):
                        w = load(kind, u)
                        b = BANK[0 if kind == "gate" else 1]
                        per_chunk = CH // F
                        for e in range(per_chunk):
                            for kt in range(KT):
                                for c in range(2):
                                    q = (u * per_chunk + e) * 2 + c
                                    col = e * KT * F + kt * F
                                    i = mm(b[CAP * c:CAP * (c + 1), e * F:(e + 1) * F], x[:, kt, q * CAP:(q + 1) * CAP],
                                           w[c][:, col:col + F], start=kt == 0, stop=kt == KT - 1)
                                    if e == per_chunk - 1 and kt == KT - 1:
                                        i.then_inc(chunk_done, 1)

                    def hidden_T(u):
                        b = BANK[0 if u == units - 1 else 2]
                        pe.wait_ge(h_ready, g * units + (unit0 + u + 1))
                        for f in range(4):
                            step = F // P
                            ap = HB[:, (f // step) * F + f % step:(f // step + 1) * F:step]
                            i = nc.tensor.transpose(b[:, f * P:(f + 1) * P], ap, ident)
                        i.then_inc(hT_psum, 1)

                    def down(u, a, half):
                        if a == 0 and half == 0:
                            pe.wait_ge(hT_ready, g * units + (unit0 + u + 1))
                            load("down", u)
                        if a == 0 and u == units - 1 and not last:
                            pe.wait_ge((xc_act, xc_dve)[half], g * (gathers // 2) + (gather0 // 2 + gathers))
                        n = n0 + first_chunk(units, "down", u)
                        step = F // P
                        for f in range(step):
                            for c in range(2):
                                col = (a * step + f) * D + half * CH
                                i = mm(BANK[2 + half][CAP * c:CAP * (c + 1), :], HT[:, a * step + f, CAP * c:CAP * (c + 1)],
                                       slot(n + c)[:, col:col + CH], start=f == 0, stop=f == step - 1)
                        i.then_inc(y_psum, 1)

                    def scatter(u, a, half):
                        pair = u * pairs_per_unit + a
                        pe.wait_ge((y_act, y_dve)[half], g * pairs + (pair0 + pair + 1))
                        if pair == 0:
                            pe.wait_ge(pwT_act, g + (G * L + 1))
                        if pair == 2 and half == 0:
                            pe.wait_ge(pwT_dve, g + 1)
                        final = last and pair == pairs - 1
                        for t in range(T):
                            i = mm(BANK[4 + 2 * t + half][:, :], PWT[:, pair, t * P:(t + 1) * P], YS[:, pair % 2, half, :],
                                   start=False, stop=final)
                            if half == 0 and a == pairs_per_unit - 1:
                                i.then_inc(chunk_done, 1)
                            elif half == 1 and final:
                                i.then_inc(acc_ready, 1)

                    for u in range(units):
                        if u == 0:
                            for s_ in (xc_act, xc_dve):
                                pe.wait_ge(s_, g * (gathers // 2) + (gather0 // 2 + gathers // 2))
                        else:
                            pe.wait_ge(silu_done, g * units + (unit0 + u))
                        hidden("gate", u)
                        if u == 0:
                            pe.wait_ge(p_ready, g * 2 + (2 * G * L + 2))
                            for pair in range(pairs):
                                for t in range(T):
                                    i = nc.tensor.transpose(BANK[2 + pair // 2][:, (pair % 2) * S + t * P:(pair % 2) * S + (t + 1) * P],
                                                            PW[:, t * W + pair * P:t * W + (pair + 1) * P], ident)
                                if pair % 2:
                                    i.then_inc(pwT_psum, 1)
                        else:
                            hidden_T(u - 1)
                        hidden("up", u)
                        if u:
                            down(u - 1, 0, 0)
                            down(u - 1, 0, 1)
                            scatter(u - 1, 0, 0)
                            scatter(u - 1, 0, 1)
                    u = units - 1
                    pe.wait_ge(pwT_act, g + (G * L + 1))
                    if last:
                        hidden_T(u)
                    else:
                        gather(g + 1, lambda: hidden_T(u))
                    for a in range(pairs_per_unit):
                        down(u, a, 0)
                        if a:
                            scatter(u, a - 1, 1)
                        down(u, a, 1)
                        scatter(u, a, 0)
                    scatter(u, pairs_per_unit - 1, 1)

                gather(0)
                with pe.Fori(0, G - 1) as g:
                    group(g, False)
                group(G - 1, True)

                v = general[L]
                pe.wait_ge(over_ready, L + 1)
                flag = pe.value_load(OVER_I[0:1, 0:1], min_val=0, max_val=1)
                with pe.If(flag > 0):
                    pe.wait_ge(v["sums_kept"], 1)
                    for t in range(T):
                        for half in range(2):
                            mm(BANK[4 + 2 * t + half][:, :], ident, X[:, t, half * CH:(half + 1) * CH], start=True, stop=False)
                    with pe.Fori(0, G * 2 * units) as n:
                        pe.wait_ge(v["loaded"], n * 48 + 48)
                        for t in range(T):
                            for b in range(2):
                                for e in range(CH // F):
                                    for kt in range(KT):
                                        col = e * KT * F + kt * F
                                        i = mm(BANK[b][:, e * F:(e + 1) * F], XT[:, kt, t * P:(t + 1) * P], slot(b)[:, col:col + F],
                                               start=kt == 0, stop=kt == KT - 1)
                                i.then_inc(v["psum"], 1)
                            pe.wait_ge(v["h_ready"], n * 2 + (t + 1))
                            for f in range(4):
                                step = F // P
                                ap = HB[:, (f // step) * F + f % step:(f // step + 1) * F:step]
                                i = nc.tensor.transpose(BANK[2][:, f * P:(f + 1) * P], ap, ident)
                            i.then_inc(v["psum"], 1)
                            pe.wait_ge(v["hT_ready"], n * 2 + (t + 1))
                            for half in range(2):
                                for f in range(4):
                                    i = mm(BANK[4 + 2 * t + half][:, :], HT[:, f, :], slot(2)[:, f * D + half * CH:f * D + (half + 1) * CH],
                                           start=False, stop=False)
                            i.then_inc(v["psum"], 1)
                    for b in range(4, 8):
                        i = mm(BANK[b][:, :], const("causal")[:, P:2 * P], const("count"), start=False, stop=True)
                    i.then_inc(v["psum"], 1)

            moe(0, 1, X)

            keep_clock_up(4, 1)
            transpose_x(2, X, lambda t: pe.wait_ge(normed, tile_no(NORM_OF_XT[2], t)),
                        lambda t: project(N_SB, CH, 6, tiles=(t,)))
            project(N_SB + 1, CH, 7)
            for c in range(4):
                project_T(N_SB + 2 + c, 8 + c, 4)
            pe.wait_ge(proj_copied, 12)

            def sb_scores(h):
                r, n = HD * (h % 2), h // 2
                if h >= 2:
                    pe.wait_ge(z_masked, h - 1)
                mm(BANK[h % 2][:, 0:S], sbK[r:r + HD, n, 0:P], sbQ[r:r + HD, n, :], start=True, stop=True)
                mm(BANK[h % 2][:, S:BL], sbK[r:r + HD, n, P:S], sbQ[r:r + HD, n, P:S], start=True, stop=True).then_inc(z_psum, 1)

            def sb_suffix(h):
                pe.wait_ge(sp_ready, h + 1)
                if h >= 2:
                    pe.wait_ge(w_log, h - 1)
                b, spv = BANK[2 + h % 2], SP_[h % 3]
                mm(b[:, 0:S], const("neg_suffix"), spv[:, 0:S], start=True, stop=False)
                mm(b[:, P:S], const("neg_ones"), spv[:, S:BL], start=False, stop=True)
                mm(b[:, S:BL], const("neg_suffix"), spv[:, S:BL], start=True, stop=True).then_inc(r_psum, 1)

            def sb_values(h):
                pair = h // 2
                if pair >= 2:
                    pe.wait_ge(sbo_copied, pair - 1)
                pe.wait_ge(w_ready, h + 1)
                b = BANK[4 + pair % 2]
                for t in range(T):
                    for hh in (h - 1, h):
                        r = HD * (hh % 2)
                        i = mm(b[r:r + HD, t * P:S], sbV[:, t, HD * hh:HD * hh + HD], WT[hh % 4][:, t * S:t * P + S],
                               start=t == 0, stop=t == T - 1)
                        if t == T - 1:
                            i.then_inc(sbo_psum, 1)

            for s in range(16 + 4):
                if s < 16:
                    sb_scores(s)
                if 0 <= s - 2 < 16:
                    sb_suffix(s - 2)
                if s >= 4 and (s - 4) % 2:
                    sb_values(s - 4)
            pe.wait_ge(sbo_copied, 8)
            project_out(N_SB + 6)
            moe(1, 3, X)

            keep_clock_up(9, 1)
            transpose_x(4, U, lambda t: pe.wait_ge(normed, tile_no(NORM_OF_XT[4], t)),
                        lambda t: project(N_2, CH, 12, tiles=(t,)))
            project_T(N_2 + 1, 13, 4)
            project_T(N_2 + 2, 14, 2, RANK)
            pe.wait_ge(proj_copied, 15)
            for r in range(2):
                for t in range(T):
                    i = mm(BANK[r][:, t * S:(t + 1) * S], LR[0:RANK + 1, r, t * P:(t + 1) * P], gw[0:RANK + 1, r, :], start=True, stop=True)
                i.then_inc(gz_psum, 1)
            project(N_2 + 3, CH, 15)
            pe.wait_ge(la_ready, 1)
            la = by_tok(W3)
            for r in range(2):
                for k in range(2):
                    for t in range(T):
                        i = mm(BANK[2 + r][:, k * S + t * P:k * S + (t + 1) * P], la[:, r, t, k * P:(k + 1) * P],
                               const("up_to" if r == 0 else "from_on"), start=True, stop=True)
                i.then_inc(bt_psum, 1)
            for n in range(4, 7):
                project(N_2 + n, CH, 12 + n)
            pe.wait_ge(bs_ready, 1)
            for m, src in enumerate((AQ, AK)):
                pe.wait_ge(roped, 6 + m)
                for k in range(2):
                    for n in range(4):
                        j, t = 2 * k + n // 2, n % 2
                        i = nc.tensor.transpose(BANK[2 * m + k][:, n * P:(n + 1) * P], src[:, t, P * j:P * (j + 1)], ident)
                    i.then_inc(qt_psum, 1)
            qd, ki, ke = by_key(W1), by_key(W2), by_key(W3)
            ket = by_tok(W0)
            pe.wait_ge(qk_ready, 3)
            pe.wait_ge(proj_copied, 19)
            for r in range(2):
                for t in range(T):
                    for k in range(2):
                        i = nc.tensor.transpose(BANK[4 + r][:, t * S + k * P:t * S + (k + 1) * P], ke[:, r, k, t * P:(t + 1) * P], ident)
                i.then_inc(ket_psum, 1)
            pe.wait_ge(qt_act, 11)
            for r in range(2):
                for i8 in range(8):
                    h, t = i8 // 4 + 2 * (i8 % 2), (i8 % 4) // 2
                    rows = slice(HD * (h % 2), HD * (h % 2) + HD)
                    i = mm(BANK[2 * r + i8 // 4][:, (i8 % 4) * P:(i8 % 4 + 1) * P], ki[rows, r, h // 2, t * P:(t + 1) * P],
                           qd[rows, r, h // 2, t * P:(t + 1) * P], start=True, stop=True)
                    if i8 % 4 == 3:
                        i.then_inc(att_psum, 1)
            pe.wait_ge(ket_ready, 2)
            for r in range(2):
                for n in ((0, 2, 1) if r == 0 else (3, 1, 2)):
                    for k in range(2):
                        rows = slice(GCH * (n % 2), GCH * (n % 2) + GCH)
                        for hh in range(2):
                            h = 2 * k + hh
                            col = (n // 2) * S + k * P
                            i = mm(BANK[4 + 2 * r + n % 2][HD * hh:HD * hh + HD, col:col + P],
                                   ket[rows, r, n // 2, h * HD:(h + 1) * HD], GV[rows, n // 2, h * P:(h + 1) * P], start=True, stop=True)
                i.then_inc(kv_psum, 1)
            pe.wait_ge(att_ready, 1)
            pe.wait_ge(state_ready, 1)
            for t in range(T):
                for h in range(4):
                    rows = slice(HD * (h % 2), HD * (h % 2) + HD)
                    b, cols = BANK[2 * t + h % 2], slice((h // 2) * P, (h // 2 + 1) * P)
                    i = mm(b[:, cols], att[:, (h % 2) * 4 + t * 2 + h // 2, :], GV[:, t, h * P:(h + 1) * P], start=True, stop=False)
                    for cc in range(2):
                        n = 2 * t + cc
                        for r in range(2):
                            if (r == 0 and n == 0) or (r == 1 and n == 3):
                                continue
                            sl = n - 1 if r == 0 else 2 - n
                            last = r == 1 or n == 3
                            i = mm(b[GCH * cc:GCH * cc + GCH, cols], qd[rows, r, h // 2, n * GCH:(n + 1) * GCH],
                                   state[rows, r, h // 2, sl, :], start=False, stop=last)
                i.then_inc(go_psum, 1)
            pe.wait_ge(go_ready, 1)
            for k in range(2):
                for n in range(4):
                    j, t = 2 * k + n // 2, n % 2
                    i = nc.tensor.transpose(BANK[4 + k][:, n * P:(n + 1) * P], by_tok2(W0)[:, t, P * j:P * (j + 1)], ident)
                i.then_inc(goT_psum, 1)
            pe.wait_ge(goT_ready, 1)
            attention(DIL_JOBS, len(AB_JOBS), 8, {})
            pe.wait_ge(o_copied, 12)
            project_out(N_2 + 7)
            moe(2, 5, U2)

        @block.scalar
        def _(act):
            ac = nc.scalar.activation
            steps = [0]

            def link(i):
                steps[0] += 1
                i.then_inc(act_step, 1)
                act.wait_ge(act_step, steps[0])

            act.dma_start(CONSTS[:, 0:FIRST_CONSTS], a["constants"][:, 0:FIRST_CONSTS]).then_inc(first_consts_loaded, 16)
            act.dma_start(POS_I[:, :], a["positions"][0].rearrange("(t p) -> p t", p=P), allow_slow_non_contiguous=True).then_inc(positions_loaded, 16)
            for i, n in enumerate(("nsa_cmp_w2_k", "nsa_cmp_w2_v")):
                act.dma_start(cmp_w2[:, i, :], a[n][0]).then_inc(cmp_small_loaded, 16)
            for i, n in enumerate(("nsa_cmp_pos_k", "nsa_cmp_pos_v")):
                act.dma_start(cmp_pos[0:NC16, i, :].rearrange("p (h d) -> p h d", h=2),
                              a[n][0].rearrange("(h c) d -> c h d", h=2)).then_inc(cmp_small_loaded, 16)
            act.dma_start(CONSTS[:, FIRST_CONSTS:], a["constants"][:, FIRST_CONSTS:]).then_inc(consts_loaded, 16)
            def transpose_x(k, before_last=None):
                for b in range(3):
                    if b == 2 and before_last:
                        before_last()
                    t, h = b // 2, b % 2
                    act.wait_ge(xt_psum, 4 * k + b + 1)
                    ac(XT[:, 4 * h:4 * h + 4, t * P:(t + 1) * P], BANK[b][:, :].rearrange("p (k s) -> p k s", k=4), ACT.Copy).then_inc(xt_act, 1)

            def take(seq, n, parts):
                act.wait_ge(chunk_done, n + 1)
                for b, o, rows, ncols, scale in parts:
                    src = BANK[4 + 2 * (seq % 2) + b][0:rows, 0:ncols]
                    if seq == 0:
                        o = o.rearrange("p (j a d) -> p a j d", a=2, j=4)
                        src = src.rearrange("p (a j d) -> p a j d", a=2, j=4)
                    i = ac(o, src, ACT.Copy, scale=scale)
                i.then_inc(proj_copied, 1)

            def rstd_from(k, tiles=range(T)):
                for t in tiles:
                    act.wait_ge(var_ready, root_no(k, t))
                    link(ac(lnv[:, t:t + 1], veps[:, t:t + 1], ACT.Ln))
                    ac(rstd[:, t:t + 1], lnv[:, t:t + 1], ACT.Exp, scale=-0.5).then_inc(rstd_ready, 1)

            transpose_x(0)
            act.wait_ge(angle_ready, 2)
            ac(sin1, angle, ACT.Sin)
            ac(cos1, turns, ACT.Sin).then_inc(sines_ready, 1)
            nc.scalar.preload_act_table_set("natural_log_exp_and_others")
            for c in range(6):
                sc = -SCALE if c in (0, 3) else 1.0
                take(c, c, [(t, pj[:, t, W_COL0[c]:W_COL0[c] + W_NCOLS[c]], P, W_NCOLS[c], sc) for t in range(T)])
                if c == 2:
                    act.wait_ge(proj_copied, 3)
                    ac(pj[:, :, C_GA:C_GA + 24], pj[:, :, C_GA:C_GA + 24], ACT.Exp, scale=-1.0).then_inc(gates_exp, 1)
                if c == 2:
                    for k in range(2):
                        act.wait_ge(qt_psum, k + 1)
                        ac(qk[:, 2 * k:2 * k + 2, :], BANK[k][:, :].rearrange("p (n s) -> p n s", n=2), ACT.Copy).then_inc(qt_act, 1)
                if c == 4:
                    act.wait_ge(qt_psum, 5)
                    ac(qk[:, 5, :], BANK[0][:, 0:S], ACT.Copy).then_inc(qt_act, 1)
                    for k in range(5, 9):
                        act.wait_ge(qt_psum, k + 1)
                        ac(qk[:, 2 * k - 4:2 * k - 2, :], BANK[k % 4][:, :].rearrange("p (n s) -> p n s", n=2), ACT.Copy).then_inc(qt_act, 1)

            def attention(jobs, first, extras):
                dil = jobs[0][0] == "dil"
                for s in range(len(jobs) + 3):
                    if s < len(jobs):
                        J = first + s
                        act.wait_ge(mins_ready, J + 1)
                        if J >= 4:
                            act.wait_ge(pt_psum, J - 3)
                        for t, (c0, c1) in enumerate(((0, S), (S, 2 * S)) if dil else ((0, P), (P, 3 * P))):
                            i = ac(PR[J % 4][:, c0:c1], SM[J % 2][:, c0:c1], ACT.Exp, scale=-1.0,
                                   bias=least[:, J % 4, t:t + 1], accum_out=psums[:, J % 4, t:t + 1])
                        i.then_inc(probs_ready, 1)
                    if s in extras:
                        extras[s]()
                    if s >= 3:
                        J = first + s - 3
                        n = 2 * S if dil else 3 * P
                        act.wait_ge(pt_psum, J + 1)
                        if J >= 4:
                            act.wait_ge(pv_done, J - 3)
                        ac(PTS[J % 4][:, 0:n], BANK[2 + J % 2][:, 0:n], ACT.Copy).then_inc(pt_copied, 1)

            def gelu_exp():
                act.wait_ge(hid_exp_in, 1)
                ac(hid_t[0:2 * NC16, :], hid_t[0:2 * NC16, :], ACT.Exp, scale=-2.0 * float(np.sqrt(2.0 / np.pi))).then_inc(hid_exp, 1)

            def hiddenT():
                act.wait_ge(hidT_psum, 1)
                ac(hidT, BANK[7][:, 0:64].rearrange("p (v n) -> p v n", v=2), ACT.Copy).then_inc(hidT_ready, 1)

            def cmp_exponent():
                act.wait_ge(cmp_exp_in, 1)
                ac(cmp_p, cmp_p, ACT.Exp, scale=-1.0).then_inc(cmp_exp, 1)

            def cmp_pT_copy():
                act.wait_ge(cmp_pT_psum, 1)
                ac(cmp_pT_sb, BANK[6][:, S:2 * S], ACT.Copy).then_inc(cmp_pT, 1)

            attention(AB_JOBS, 0, {4: gelu_exp, 6: hiddenT, 9: cmp_exponent, 11: cmp_pT_copy})

            def moe(L, k):
                n = NORM_OF_XT[k]
                rstd_from(n, (0,))
                transpose_x(k, lambda: rstd_from(n, (1,)))
                for _ in range(2):
                    n = L * 2 + _ + 1
                    act.wait_ge(rexp_in, n)
                    w = small_r[1][:, 0:T * G] if _ == 0 else small_r[8][:, 0:T]
                    ac(w, w, ACT.Exp).then_inc(rexp, 1)
                nc.scalar.preload_act_table(ACT.Silu)
                units, pairs, gathers = UNITS[L], PAIRS[L], GATHERS[L]
                n0, per_group = N_MOE[L], 6 * units
                unit0, pair0, gather0 = G * sum(UNITS[:L]), G * sum(PAIRS[:L]), G * sum(GATHERS[:L])

                def gathered(g):
                    for n in range(0, gathers, 2):
                        act.wait_ge(xc_psum, g * gathers + (gather0 + n + 1))
                        ac(xcT[:, n * CH:(n + 1) * CH], BANK[2][:, :], ACT.Copy).then_inc(xc_act, 1)

                def outputs(g, pair):
                    act.wait_ge(y_psum, g * (2 * pairs) + (2 * (pair0 + pair) + 1))
                    ac(YS[:, pair % 2, 0, :], BANK[2][:, :], ACT.Copy).then_inc(y_act, 1)

                def group(g, last):
                    act.wait_ge(pwT_psum, g * (pairs // 2) + (G * sum(PAIRS[:L]) // 2 + 1))
                    ac(PWT[:, 0:2, :], BANK[2][:, :].rearrange("p (a s) -> p a s", a=2), ACT.Copy).then_inc(pwT_act, 1)
                    for u in range(units):
                        act.wait_ge(chunk_done, g * per_group + (n0 + first_chunk(units, "gate", u) + 2))
                        if u:
                            act.wait_ge(h_ready, g * units + (unit0 + u))
                        ac(SG, BANK[0][:, :], ACT.Silu).then_inc(silu_done, 1)
                        if u:
                            outputs(g, u - 1)
                    if not last:
                        gathered(g + 1)
                    for pair in range(units - 1 if units > 1 else 0, pairs):
                        outputs(g, pair)

                gathered(0)
                with act.Fori(0, G - 1) as g:
                    group(g, False)
                group(G - 1, True)

                v = general[L]
                act.wait_ge(over_ready, L + 1)
                flag = act.value_load(OVER_I[0:1, 0:1], min_val=0, max_val=1)
                with act.If(flag > 0):
                    with act.Fori(0, G * 2 * units) as n:
                        for t in range(T):
                            act.wait_ge(v["psum"], n * 8 + (4 * t + 1))
                            ac(SG, BANK[0][:, :], ACT.Silu).then_inc(v["silu_done"], 1)
                nc.scalar.preload_act_table_set("natural_log_exp_and_others")

            moe(0, 1)
            rstd_from(1, (0,))
            transpose_x(2, lambda: rstd_from(1, (1,)))
            for c in range(2):
                take(6 + c, N_SB + c, [(t, sbV[:, t, c * CH:(c + 1) * CH], P, CH, 1.0) for t in range(T)])
            for c in range(4):
                dst = (sbQ if c < 2 else sbK)
                take(8 + c, N_SB + 2 + c, [(b, dst[:, 4 * (c % 2) + 2 * b:4 * (c % 2) + 2 * b + 2, :], P, CH, SCALE if c < 2 else 1.0) for b in range(2)])
            for s in range(16 + 3):
                if s < 16:
                    act.wait_ge(z_masked, s + 1)
                    if s >= 2:
                        act.wait_ge(sp_ready, s - 1)
                    link(ac(AN[s % 2], ZM[s % 4], ACT.Abs))
                    link(ac(AN[s % 2], AN[s % 2], ACT.Exp, scale=-1.0))
                    ac(AN[s % 2], AN[s % 2], ACT.Ln, bias=1.0).then_inc(z_log, 1)
                if s >= 3:
                    h = s - 3
                    act.wait_ge(w_log, h + 1)
                    if h >= 4:
                        act.wait_ge(sbo_psum, h - 3)
                    ac(WT[h % 4], WL[h % 2], ACT.Exp).then_inc(w_ready, 1)
            moe(1, 3)

            def two_roots(t):
                rstd_from(3, (t,))
                rstd_from(4, (t,))

            two_roots(0)
            transpose_x(4, lambda: two_roots(1))
            take(12, N_2, [(t, GV[:, t, :], P, CH, 1.0) for t in range(T)])
            take(13, N_2 + 1, [(0, gqT, P, CH, SCALE), (1, gkT, P, CH, 1.0)])
            act.wait_ge(pool_step, 1)
            take(14, N_2 + 2, [(0, LR[0:RANK, :, :], RANK, CH, 1.0)])
            act.wait_ge(gz_abs, 1)
            link(ac(W1, W1, ACT.Exp))
            ac(W1, W1, ACT.Ln, bias=1.0).then_inc(gz_log, 1)
            take(15, N_2 + 3, [(t, GG[:, t, :], P, CH, 1.0) for t in range(T)])
            act.wait_ge(bs_ready, 1)
            bs = by_key(W0)
            ac(W1, W0, ACT.Exp).then_inc(eb_ready, 1)
            ac(W2, W0, ACT.Exp, scale=-1.0).then_inc(eb_ready, 1)
            for r in range(2):
                for k in range(2):
                    for n in range(4):
                        end = n * GCH + (GCH - 1 if r == 0 else 0)
                        i = ac(by_key(W3)[:, r, k, n * GCH:(n + 1) * GCH], bs[:, r, k, n * GCH:(n + 1) * GCH], ACT.Exp,
                               scale=-1.0, bias=bs[:, r, k, end:end + 1])
            i.then_inc(eb_ready, 1)
            take(16, N_2 + 4, [(t, AQ[:, t, :], P, CH, -SCALE) for t in range(T)])
            take(17, N_2 + 5, [(t, AK[:, t, :], P, CH, 1.0) for t in range(T)])
            take(18, N_2 + 6, [(t, AV[:, t, :], P, CH, 1.0) for t in range(T)])
            for k in range(4):
                act.wait_ge(qt_psum, 9 + k + 1)
                ac(qk[:, 2 * k:2 * k + 2, :], BANK[k][:, :].rearrange("p (n s) -> p n s", n=2), ACT.Copy).then_inc(qt_act, 1)
            for r in range(2):
                act.wait_ge(ket_psum, r + 1)
                ac(W0[:, 512 * r:512 * (r + 1)], BANK[4 + r][:, :], ACT.Copy).then_inc(ket_ready, 1)
            act.wait_ge(ket_psum, 2)
            for t in range(T):
                i = ac(by_tok2(W3)[:, t, :], GG[:, t, :], ACT.Exp, scale=-1.0)
            i.then_inc(silu_exp, 1)
            for t in range(T):
                act.wait_ge(go_psum, t + 1)
                for par in range(2):
                    i = ac(by_tok2(W2)[:, t, :].rearrange("p (hh r v) -> p hh r v", hh=2, r=2)[:, :, par, :],
                           BANK[2 * t + par][:, 0:S].rearrange("p (hh v) -> p hh v", hh=2), ACT.Square)
                i.then_inc(go_square, 1)
            act.wait_ge(var_ready, 2 * 5 + 1)
            link(ac(go_l, go_ms, ACT.Ln))
            ac(go_r, go_l, ACT.Exp, scale=-0.5).then_inc(rstd_ready, 1)
            for k in range(2):
                act.wait_ge(goT_psum, k + 1)
                i = ac(mixT[:, 2 * k:2 * k + 2, :], BANK[4 + k][:, :].rearrange("p (n s) -> p n s", n=2), ACT.Copy)
            i.then_inc(goT_ready, 1)
            attention(DIL_JOBS, len(AB_JOBS), {})
            moe(2, 5)
            rstd_from(6)

        @block.vector
        def _(dve):
            tt, ts, stt = nc.vector.tensor_tensor, nc.vector.tensor_scalar, nc.vector.scalar_tensor_tensor
            cp = nc.vector.tensor_copy
            steps = [0]

            def link(i):
                steps[0] += 1
                i.then_inc(dve_step, 1)
                dve.wait_ge(dve_step, steps[0])

            def transpose_x(k):
                dve.wait_ge(xt_psum, 4 * k + 4)
                cp(XT[:, 4:8, P:S], BANK[3][:, :].rearrange("p (k s) -> p k s", k=4)).then_inc(xt_dve, 1)

            def sharpen(r, v, q):
                link(tt(q, r, r, ALU.mult))
                link(tt(q, q, v, ALU.mult))
                link(ts(q, q, -0.5, 1.5, ALU.mult, ALU.add))
                link(tt(r, r, q, ALU.mult))

            def statistics(t, halves, from_psum=False):
                for half in halves:
                    src = BANK[4 + 2 * t + half][:, :] if from_psum else X[:, t, half * CH:(half + 1) * CH]
                    i = nc.vector.bn_stats(stats[:, t, 6 * half:6 * half + 6], src)
                link(i)

            def ask_rstd(kind, t):
                link(nc.vector.bn_aggr(mean_var[:, t, :], stats[:, t, :]))
                if kind == "layer":
                    ts(veps[:, t:t + 1], mean_var[:, t, 1:2], LN_EPS, None, ALU.add).then_inc(var_ready, 1)
                else:
                    link(tt(newton[:, t:t + 1], mean_var[:, t, 0:1], mean_var[:, t, 0:1], ALU.mult))
                    stt(veps[:, t:t + 1], newton[:, t:t + 1], RMS_EPS, mean_var[:, t, 1:2], ALU.add, ALU.add).then_inc(var_ready, 1)

            def normalise(k, kind, dst, t, from_psum=False):
                dve.wait_ge(norm_loaded[k % 2], NORM_VALUE[k])
                if kind == "layer":
                    for cols in (slice(0, CH), slice(CH, D)) if from_psum else (slice(0, D),):
                        src = BANK[4 + 2 * t + cols.start // CH][:, :] if from_psum else X[:, t, cols]
                        i = stt(X[:, t, cols], src, mean_var[:, t, 0:1], NORM[:, k % 2, 0, cols], ALU.subtract, ALU.mult)
                    link(i)
                dve.wait_ge(rstd_ready, root_no(k, t))
                sharpen(rstd[:, t:t + 1], veps[:, t:t + 1], newton[:, t:t + 1])
                if kind == "layer":
                    stt(dst[:, t, :], X[:, t, :], rstd[:, t:t + 1], NORM[:, k % 2, 1, :], ALU.mult, ALU.add).then_inc(normed, 1)
                else:
                    for cols in (slice(0, CH), slice(CH, D)) if from_psum else (slice(0, D),):
                        src = BANK[4 + 2 * t + cols.start // CH][:, :] if from_psum else X[:, t, cols]
                        i = stt(dst[:, t, cols], src, rstd[:, t:t + 1], NORM[:, k % 2, 0, cols], ALU.mult, ALU.mult)
                    i.then_inc(normed, 1)
                dve.wait_ge(normed, tile_no(k, t))

            def add_scaled(t, half, alpha, bank):
                c = X[:, t, half * CH:(half + 1) * CH]
                link(stt(c, c, alpha, bank, ALU.mult, ALU.add))

            def mixer_residual(n, nproj, alpha, k, kind, dst):
                dve.wait_ge(chunk_done, n + 1)
                for t in range(T):
                    add_scaled(t, 0, alpha, BANK[4 + t][:, :])
                    statistics(t, (0,))
                for t in range(T):
                    if t == 0:
                        dve.wait_ge(out_psum, nproj + 1)
                    else:
                        dve.wait_ge(chunk_done, n + 2)
                    add_scaled(t, 1, alpha, BANK[6 + t][:, :])
                    statistics(t, (1,))
                    ask_rstd(kind, t)
                    normalise(k, kind, dst, t)

            def rope(view, col, n):
                h = heads(view, col, n)
                x1, x2 = h[:, :, :, 0, :], h[:, :, :, 1, :]
                c, s_ = (v.rearrange("p (t d) -> p t d", t=T).unsqueeze(2).to_broadcast([P, T, n, HALF]) for v in (cos1, sin1))
                m = [w[:, 0:T * n * HALF].rearrange("p (t h d) -> p t h d", t=T, h=n) for w in ROPE_TMP]
                tt(m[0], x1, c, ALU.mult)
                tt(m[1], x2, s_, ALU.mult)
                tt(m[2], x2, c, ALU.mult)
                link(tt(m[3], x1, s_, ALU.mult))
                tt(x1, m[0], m[1], ALU.subtract)
                return tt(x2, m[2], m[3], ALU.add)

            transpose_x(0)
            dve.wait_ge(first_consts_loaded, 16)
            dve.wait_ge(positions_loaded, 16)
            link(cp(pos_f, POS_I[:, :]))
            for t in range(T):
                link(ts(cos1[:, t * HALF:(t + 1) * HALF], const("inv_freq"), pos_f[:, t:t + 1], None, ALU.mult))
            TWO_PI = 2 * np.pi
            C1 = 6.28125
            C2 = float(np.float32(TWO_PI - C1))
            C3 = float(TWO_PI - C1 - float(np.float32(TWO_PI - C1)))
            for i, (o, quarter) in enumerate(((angle, 0.0), (turns, 0.25))):
                n = sin1
                link(ts(n, cos1, 1.0 / TWO_PI, quarter, ALU.mult, ALU.add))
                link(ts(n, n, 12582912.0, None, ALU.add))
                link(ts(n, n, 12582912.0, None, ALU.subtract))
                link(stt(o, n, -C1, cos1, ALU.mult, ALU.add))
                link(stt(o, n, -C2, o, ALU.mult, ALU.add))
                link(stt(o, n, -C3, o, ALU.mult, ALU.add))
                if quarter:
                    link(ts(o, o, TWO_PI * quarter, None, ALU.add))
                ts(o, o, 3.1415925, -3.1415925, ALU.min, ALU.max).then_inc(angle_ready, 1)
            dve.wait_ge(pos_psum, 1)
            cp(cmp_posT, BANK[3][:, 0:2 * NC16].rearrange("p (v c) -> p v c", v=2)).then_inc(pos_ready, 1)
            dve.wait_ge(sines_ready, 1)
            dve.wait_ge(proj_copied, 1)
            rope(pj, 0, 8).then_inc(roped, 1)
            dve.wait_ge(roped, 1)
            dve.wait_ge(proj_copied, 2)
            link(rope(pj, C_KC, 2))
            rope(pj, C_KS, 2).then_inc(roped, 1)
            dve.wait_ge(roped, 2)
            dve.wait_ge(proj_copied, 3)
            rope(pj, C_KW, 2).then_inc(roped, 1)
            dve.wait_ge(roped, 3)

            ga = pj[:, :, C_GA:C_GA + 24]
            dve.wait_ge(gates_exp, 1)
            link(ts(ga, ga, 1.0, None, ALU.add))
            nc.vector.reciprocal(ga, ga).then_inc(gates_ready, 1)
            dve.wait_ge(pos_ready, 1)
            dve.wait_ge(qt_psum, 3)
            cp(qk[:, 4, :], BANK[2][:, 0:S])
            link(nc.vector.memset(kv2[HD:P, :, :, NBLK * NC16:S], 0.0))
            for v, (b, col) in enumerate(((2, S), (3, 0))):
                dve.wait_ge(qt_psum, 3 + v)
                for h in range(2):
                    for half in range(2):
                        n = NC16 - half
                        rows = slice(HD * half, HD * half + HD)
                        src = BANK[b][HD * h:HD * h + HD, col + CMP_STRIDE * half:col + S].rearrange("p (n c) -> p n c", c=NC16)
                        dst = kv2[rows, v, h, 0:n * NC16].rearrange("p (n c) -> p n c", c=NC16)
                        i = tt(dst, src, cmp_posT[rows, v, :].unsqueeze(1).to_broadcast([HD, n, NC16]), ALU.add)
                i.then_inc(kv2_ready, 1)
            dve.wait_ge(proj_copied, 4)
            rope(pj, C_QM, 8).then_inc(roped, 1)
            dve.wait_ge(roped, 4)
            dve.wait_ge(proj_copied, 5)
            rope(pj, C_KM, 8).then_inc(roped, 1)
            dve.wait_ge(roped, 5)

            def attention(jobs, first, pairs0, extras):
                dil = jobs[0][0] == "dil"

                def inverse(j):
                    J = first + j
                    dve.wait_ge(probs_ready, J + 1)
                    if dil:
                        for t in range(T):
                            c = PR[J % 4][:, t * S:(t + 1) * S]
                            i = stt(c, c, 1.0, const("count")[:, t * S:(t + 1) * S], ALU.mult, ALU.mult, accum_out=psums[:, J % 4, t:t + 1])
                        link(i)
                    link(nc.vector.reciprocal(rinv[:, J % 4, :], psums[:, J % 4, :]))
                    gate = job_operands(jobs[j])[3]
                    if gate is not None and J == 8:
                        dve.wait_ge(gates_ready, 1)
                    for t, (c0, c1) in enumerate(((0, S), (S, 2 * S)) if dil else ((0, P), (P, 3 * P))):
                        c = PR[J % 4][:, c0:c1]
                        if gate is None:
                            i = ts(c, c, rinv[:, J % 4, t:t + 1], None, ALU.mult)
                        else:
                            i = ts(c, c, rinv[:, J % 4, t:t + 1], gate[:, t:t + 1], ALU.mult, ALU.mult)
                    i.then_inc(scaled_ready, 1)

                for s in range(len(jobs) + 5):
                    if s < len(jobs):
                        J = first + s
                        dve.wait_ge(scores_ready, J + 1)
                        if J >= 2:
                            dve.wait_ge(probs_ready, J - 1)
                        for t, (c0, c1) in enumerate(((0, S), (S, 2 * S)) if dil else ((0, P), (P, 3 * P))):
                            i = nc.vector.tensor_tensor_reduce(
                                out=SM[J % 2][:, c0:c1], in0=BANK[J % 2][:, c0:c1],
                                in1=const("unseen" if dil else "causal")[:, c0:c1], scale=1.0, scalar=3e38,
                                op0=ALU.add, op1=ALU.min, accum_out=least[:, J % 4, t:t + 1])
                        i.then_inc(mins_ready, 1)
                    if 1 <= s <= len(jobs):
                        inverse(s - 1)
                    if s in extras:
                        extras[s]()
                    if s >= 5 and last_of_pair(jobs, s - 5):
                        j = s - 5
                        pair = (jobs[j][1] // 2 if dil else job_pair(jobs[j])) + pairs0
                        dve.wait_ge(pv_done, first + j + 1)
                        cp(mixT[:, job_tile(jobs[j]), :], BANK[4 + pair % 2][:, 0:S]).then_inc(o_copied, 1)

            dve.wait_ge(consts_loaded, 16)
            R = slice(0, 2 * NC16)

            def gelu_in():
                dve.wait_ge(chunk_done, CMP_CHUNK + 1)
                link(cp(hid_g[R, :], BANK[6][R, 0:2 * P]))
                link(tt(hid_t[R, :], hid_g[R, :], hid_g[R, :], ALU.mult))
                link(ts(hid_t[R, :], hid_t[R, :], 0.044715, 1.0, ALU.mult, ALU.add))
                tt(hid_t[R, :], hid_t[R, :], hid_g[R, :], ALU.mult).then_inc(hid_exp_in, 1)

            def gelu_out():
                dve.wait_ge(hid_exp, 1)
                link(ts(hid_t[R, :], hid_t[R, :], 1.0, None, ALU.add))
                link(nc.vector.reciprocal(hid_t[R, :], hid_t[R, :]))
                tt(hid_g[R, :], hid_g[R, :], hid_t[R, :], ALU.mult).then_inc(hid_ready, 1)

            def keys_copy():
                dve.wait_ge(kcvc_psum, 1)
                cp(kcT[:, 0:NBLK], BANK[7][:, 64:64 + NBLK])
                cp(vc[0:NBLK, :], BANK[7][0:NBLK, P:2 * P]).then_inc(kcvc_ready, 1)

            def cmp_softmax_in():
                dve.wait_ge(cmp_scores, 1)
                for kv in range(2):
                    tt(v_blocks[:, 4 * kv:4 * kv + 4, :], BANK[7][:, HD * kv:HD * (kv + 1)].unsqueeze(1).to_broadcast([P, 4, HD]),
                       const("own_head")[:, 4 * kv:4 * kv + 4].unsqueeze(2).to_broadcast([P, 4, HD]), ALU.mult)
                link(nc.vector.memset(cmp_p, 0.0))
                big = const("cmp_big").rearrange("p (t n) -> p t n", t=T)[:, :, 0:NBLK].unsqueeze(2).to_broadcast([P, T, 4, NBLK])
                for kv in range(2):
                    sc = BANK[7 - kv][:, S:S + P].rearrange("p (t h n) -> p t h n", t=T, h=4)
                    i = tt(cmp_p[:, :, 4 * kv:4 * kv + 4, 0:NBLK], sc[:, :, :, 0:NBLK], big, ALU.add)
                link(i)
                link(nc.vector.tensor_reduce(cmp_m, cmp_p[:, :, :, 0:NBLK], AX, ALU.min))
                tt(cmp_p[:, :, :, 0:NBLK], cmp_p[:, :, :, 0:NBLK], cmp_m.unsqueeze(3).to_broadcast([P, T, 8, NBLK]), ALU.subtract).then_inc(cmp_exp_in, 1)

            def cmp_softmax_out():
                dve.wait_ge(cmp_exp, 1)
                seen = const("cmp_seen").rearrange("p (t n) -> p t n", t=T).unsqueeze(2).to_broadcast([P, T, 8, NC16])
                link(tt(cmp_p, cmp_p, seen, ALU.mult))
                link(nc.vector.reduce_sum(cmp_m, cmp_p, AX))
                link(ts(cmp_m, cmp_m, 1e-30, None, ALU.max))
                link(nc.vector.reciprocal(cmp_m, cmp_m))
                dve.wait_ge(gates_ready, 1)
                link(tt(cmp_m, cmp_m, pj[:, :, C_GA:C_GA + 24:3], ALU.mult))
                tt(cmp_p, cmp_p, cmp_m.unsqueeze(3).to_broadcast([P, T, 8, NC16]), ALU.mult).then_inc(cmp_probs, 1)

            attention(AB_JOBS, 0, 0, {3: gelu_in, 4: gelu_out, 7: keys_copy, 8: cmp_softmax_in, 10: cmp_softmax_out})
            mixer_residual(N_AB + 7, 0, ALPHA, 0, "layer", X)

            def first_max(vals, eq, m, onehot, w, n, tie):
                link(nc.vector.reduce_max(m, vals, AX))
                mb = m.unsqueeze(2).to_broadcast([P, T, n])
                link(tt(eq, vals, mb, ALU.is_equal))
                link(tt(eq, eq, tie, ALU.mult))
                link(nc.vector.reduce_max(w, eq, AX))
                return tt(onehot, eq, w.unsqueeze(2).to_broadcast([P, T, n]), ALU.is_equal)

            def moe(L, k, norms):
                E, F, _, NR = MOE[L]
                units, pairs, gathers = UNITS[L], PAIRS[L], GATHERS[L]
                n0, per_group = N_MOE[L], 6 * units
                unit0, pair0, gather0 = G * sum(UNITS[:L]), G * sum(PAIRS[:L]), G * sum(GATHERS[:L])
                W = E * CAP
                transpose_x(k)
                dve.wait_ge(logits_psum, L + 1)
                lg = rlog[:, 0:T * NR].rearrange("p (t n) -> p t n", t=T)
                bias = router_b[L].unsqueeze(1).to_broadcast([P, T, NR])
                dve.wait_ge(small_loaded, SMALL_TOTAL)
                link(tt(lg, BANK[0][:, 0:128].rearrange("p (t n) -> p t n", t=T)[:, :, 0:NR], bias, ALU.add))
                gm, wg = small_r[0][:, 0:T], small_r[0][:, 8:8 + T]
                gd = small_r[1][:, 0:T * G].rearrange("p (t g) -> p t g", t=T)
                oh = small_r[2][:, 0:T * G].rearrange("p (t g) -> p t g", t=T)
                eq = small_r[3].rearrange("p (t g) -> p t g", t=T)
                tie = const("descend").unsqueeze(1)
                link(first_max(lg[:, :, 0:G], eq[:, :, 0:G], gm, oh, small_r[4][:, 0:T], G, tie[:, :, 0:G].to_broadcast([P, T, G])))
                tt(gd, lg[:, :, 0:G], gm.unsqueeze(2).to_broadcast([P, T, G]), ALU.subtract).then_inc(rexp_in, 1)
                rtv = rt[:, 0:T * G * E].rearrange("p (t e g) -> p t e g", t=T, e=E)
                le = lg[:, :, G:NR].rearrange("p t (g e) -> p t e g", g=G)
                link(tt(rtv, le, oh.unsqueeze(2).to_broadcast([P, T, E, G]), ALU.mult))
                by_expert = lambda w: w[:, 0:T * E].rearrange("p (t e) -> p t e", t=T)
                sel, oh1, oh2, chosen, cwv = (by_expert(small_r[n]) for n in (5, 6, 7, 10, 13))
                link(nc.vector.reduce_sum(sel, rtv, AX))
                v1, v2, dv = small_r[9][:, 0:T], small_r[9][:, 8:8 + T], small_r[8][:, 0:T]
                w1, w2 = small_r[11][:, 0:T], small_r[12][:, 0:T]
                eqe = small_r[3][:, 0:T * E].rearrange("p (t e) -> p t e", t=T)
                tie_e = tie[:, :, 0:E].to_broadcast([P, T, E])
                link(first_max(sel, eqe, v1, oh1, small_r[4][:, 0:T], E, tie_e))
                link(stt(sel, oh1, -BIG, sel, ALU.mult, ALU.add))
                link(first_max(sel, eqe, v2, oh2, small_r[4][:, 0:T], E, tie_e))
                link(tt(chosen, oh1, oh2, ALU.add))
                by_ge = lambda w: w[:, 0:T * G * E].rearrange("p (t g e) -> p t g e", t=T, g=G)
                spread_g = oh.unsqueeze(3).to_broadcast([P, T, G, E])
                tt(by_ge(chosen_), spread_g, chosen.unsqueeze(2).to_broadcast([P, T, G, E]), ALU.mult).then_inc(onehot_ready, 1)
                tt(dv, v2, v1, ALU.subtract).then_inc(rexp_in, 1)
                dve.wait_ge(onehot_ready, L + 1)
                far = rt[:, 0:T * G * E]
                link(ts(far, chosen_[:, 0:T * G * E], -4096.0, 4096.0, ALU.mult, ALU.add))

                per_chunk = CH // F
                def by_place(w, t):
                    return w[:, 0:T * G * E].rearrange("p (g t u e c) -> p t g u e c", g=G, t=T, u=units, c=2)[:, t]

                def by_number(w, t):
                    return w[:, 0:T * G * E].rearrange("p (t g u c e) -> p t g u e c", g=G, t=T, u=units, c=2)[:, t]

                def ordered(dst, src, t):
                    d, s_ = by_place(dst, t), by_number(src, t)
                    return (d[:, :, 0], s_[:, :, 0]) if units == 1 else (d[:, :, :, 0, :], s_[:, :, :, 0, :])

                dve.wait_ge(rexp, 2 * L + 1)
                link(nc.vector.reduce_sum(wg, gd, AX))
                dve.wait_ge(rexp, 2 * L + 2)
                link(ts(w1, dv, 1.0, None, ALU.add))
                link(tt(w1, w1, wg, ALU.mult))
                link(nc.vector.reciprocal(w1, w1))
                dve.wait_ge(rank_psum, L + 1)
                for t in range(T):
                    d, s_ = ordered(place_, far, t)
                    if units == 1:
                        r_ = BANK[1][:, t * G * E:(t + 1) * G * E].rearrange("p (g c e) -> p g e c", g=G, c=2)
                    else:
                        r_ = BANK[1][:, t * G * E:(t + 1) * G * E].rearrange("p (g u c) -> p g u c", g=G, c=2)
                    i = tt(d, r_, s_, ALU.add)
                i.then_inc(place_ready, 1)
                dve.wait_ge(place_ready, L + 1)

                def one_hot(g):
                    view = lambda w: w[:, 0:T * W].rearrange("p (n s) -> p n s", s=CAP)
                    at = lambda w: w[:, 0:T * G * E].rearrange("p (g n) -> p g n", g=G)[:, bass.ds(g, 1), :].rearrange(
                        "p o n -> p (o n)").unsqueeze(2).to_broadcast([P, T * E, CAP])
                    places = const("iota")[:, 0:CAP].unsqueeze(1).to_broadcast([P, T * E, CAP])
                    tt(view(PB), places, at(place_), ALU.is_equal).then_inc(p_ready, 1)
                    return lambda: (dve.wait_ge(p_ready, g * 2 + (2 * G * L + 1)),
                                    tt(view(PW), view(PB), at(weight_by_place_), ALU.mult).then_inc(p_ready, 1))

                weighted = one_hot(0)
                link(tt(w2, w1, dv, ALU.mult))
                link(tt(oh1, oh1, w1.unsqueeze(2).to_broadcast([P, T, E]), ALU.mult))
                link(tt(oh2, oh2, w2.unsqueeze(2).to_broadcast([P, T, E]), ALU.mult))
                link(tt(cwv, oh1, oh2, ALU.add))
                link(tt(by_ge(weight_), spread_g, cwv.unsqueeze(2).to_broadcast([P, T, G, E]), ALU.mult))
                for t in range(T):
                    d, s_ = ordered(weight_by_place_, weight_, t)
                    i = cp(d, s_)
                link(i)
                stt(left_[:, 0:T * G * E], BANK[1][:, 0:T * G * E], float(CAP), weight_[:, 0:T * G * E], ALU.is_ge, ALU.mult)
                link(nc.vector.reduce_max(over_f[:, 0:1], BANK[1][:, T * G * E:3 * G * E], AX))
                link(ts(over_f[:, 0:1], over_f[:, 0:1], float(CAP), None, ALU.is_gt))
                cp(OVER_I[:, 0:1], over_f[:, 0:1]).then_inc(over_ready, 1)
                weighted()

                def gathered(g, after_one=None):
                    for n in range(1, gathers, 2):
                        dve.wait_ge(xc_psum, g * gathers + (gather0 + n + 1))
                        cp(xcT[:, n * CH:(n + 1) * CH], BANK[3][:, :]).then_inc(xc_dve, 1)
                        if n == 1 and after_one:
                            after_one()

                def outputs(g, pair):
                    dve.wait_ge(y_psum, g * (2 * pairs) + (2 * (pair0 + pair) + 2))
                    cp(YS[:, pair % 2, 1, :], BANK[3][:, :]).then_inc(y_dve, 1)

                def transposed(g, u):
                    dve.wait_ge(hT_psum, g * units + (unit0 + u + 1))
                    cp(HT, BANK[0 if u == units - 1 else 2][:, :].rearrange("p (f s) -> p f s", f=4)).then_inc(hT_ready, 1)

                def group(g, last):
                    dve.wait_ge(pwT_psum, g * (pairs // 2) + (G * sum(PAIRS[:L]) // 2 + pairs // 2))
                    if pairs > 2:
                        cp(PWT[:, 2:4, :], BANK[3][:, :].rearrange("p (a s) -> p a s", a=2)).then_inc(pwT_dve, 1)
                    if not last:
                        one_hot(g + 1)()
                    for u in range(units):
                        if u:
                            transposed(g, u - 1)
                        dve.wait_ge(silu_done, g * units + (unit0 + u + 1))
                        dve.wait_ge(chunk_done, g * per_group + (n0 + first_chunk(units, "up", u) + 2))
                        tt(HB, SG, BANK[1][:, :], ALU.mult).then_inc(h_ready, 1)
                        if u:
                            outputs(g, u - 1)
                    if last:
                        transposed(g, units - 1)
                    else:
                        gathered(g + 1, lambda: transposed(g, units - 1))
                    for pair in range(units - 1 if units > 1 else 0, pairs):
                        outputs(g, pair)

                gathered(0)
                with dve.Fori(0, G - 1) as g:
                    group(g, False)
                group(G - 1, True)

                v = general[L]
                dve.wait_ge(over_ready, L + 1)
                flag = dve.value_load(OVER_I[0:1, 0:1], min_val=0, max_val=1)
                with dve.If(flag > 0):
                    dve.wait_ge(acc_ready, 2 * L + 2)
                    for t in range(T):
                        for half in range(2):
                            i = cp(X[:, t, half * CH:(half + 1) * CH], BANK[4 + 2 * t + half][:, :])
                    i.then_inc(v["sums_kept"], 1)
                    left = left_[:, 0:T * G * E].rearrange("p (t n) -> p t n", t=T)
                    with dve.Fori(0, G * 2 * units) as n:
                        for t in range(T):
                            dve.wait_ge(v["psum"], n * 8 + (4 * t + 2))
                            dve.wait_ge(v["silu_done"], n * 2 + (t + 1))
                            for e in range(per_chunk):
                                c0, c1 = e * F, (e + 1) * F
                                i = stt(HB[:, c0:c1], SG[:, c0:c1], left[:, t, bass.ds(n * per_chunk + e, 1)], BANK[1][:, c0:c1],
                                        ALU.mult, ALU.mult)
                            i.then_inc(v["h_ready"], 1)
                            dve.wait_ge(v["psum"], n * 8 + (4 * t + 3))
                            cp(HT, BANK[2][:, :].rearrange("p (f s) -> p f s", f=4)).then_inc(v["hT_ready"], 1)
                    dve.wait_ge(v["psum"], 8 * G * 2 * units + 1)
                for t in range(T):
                    dve.wait_ge(acc_ready, 2 * L + t + 1)
                    statistics(t, (0, 1), from_psum=True)
                    ask_rstd("rms" if L == 2 else "layer", t)
                    norms(t)

            moe(0, 1, lambda t: normalise(1, "layer", X, t, from_psum=True))
            transpose_x(2)
            dve.wait_ge(proj_copied, 12)

            def sb_mask(h):
                dve.wait_ge(z_psum, h + 1)
                if h >= 4:
                    dve.wait_ge(w_log, h - 3)
                tt(ZM[h % 4], BANK[h % 2][:, 0:BL], const("strict"), ALU.add).then_inc(z_masked, 1)

            def sb_softplus(h):
                dve.wait_ge(z_log, h + 1)
                if h >= 3:
                    dve.wait_ge(r_psum, h - 2)
                stt(SP_[h % 3], ZM[h % 4], 0.0, AN[h % 2], ALU.max, ALU.add).then_inc(sp_ready, 1)

            def sb_weight(h):
                dve.wait_ge(r_psum, h + 1)
                if h >= 2:
                    dve.wait_ge(w_ready, h - 1)
                tt(WL[h % 2], ZM[h % 4], BANK[2 + h % 2][:, 0:BL], ALU.add).then_inc(w_log, 1)

            for s in range(16 + 5):
                if s < 16:
                    sb_mask(s)
                if 0 <= s - 1 < 16:
                    sb_softplus(s - 1)
                if 0 <= s - 3 < 16:
                    sb_weight(s - 3)
                if s >= 5 and (s - 5) % 2:
                    h = s - 5
                    dve.wait_ge(sbo_psum, h + 1)
                    cp(mixT[:, h // 2, :], BANK[4 + (h // 2) % 2][:, 0:S]).then_inc(sbo_copied, 1)
            mixer_residual(N_SB + 6, 1, ALPHA, 2, "layer", X)

            def norms_3_and_4(t):
                normalise(3, "layer", X, t, from_psum=True)
                statistics(t, (0, 1))
                ask_rstd("rms", t)
                normalise(4, "rms", U, t)

            moe(1, 3, norms_3_and_4)
            transpose_x(4)

            def rope2(view):
                h = view.rearrange("p t (h d) -> p t h d", h=8)
                x1, x2 = h[:, :, :, 0:ROT], h[:, :, :, ROT:2 * ROT]
                c, s_ = (const(v).rearrange("p (t d) -> p t d", t=T).unsqueeze(2).to_broadcast([P, T, 8, ROT]) for v in ("cos2", "sin2"))
                m = [MIX[:, 1536 + P * i:1536 + P * (i + 1)].rearrange("p (t h d) -> p t h d", t=T, h=8) for i in range(4)]
                tt(m[0], x1, c, ALU.mult)
                tt(m[1], x2, s_, ALU.mult)
                tt(m[2], x2, c, ALU.mult)
                link(tt(m[3], x1, s_, ALU.mult))
                tt(x1, m[0], m[1], ALU.subtract)
                return tt(x2, m[2], m[3], ALU.add)

            for r in range(2):
                dve.wait_ge(gz_psum, r + 1)
                link(cp(W0[:, 512 * r:512 * (r + 1)], BANK[r][:, :]))
            stt(W1, W0, -1.0, W0, ALU.mult, ALU.min).then_inc(gz_abs, 1)
            link(ts(W2, W0, 0.0, 1.0 / 16, ALU.min, ALU.mult))
            dve.wait_ge(gz_log, 1)
            stt(W3, W1, -1.0 / 16, W2, ALU.mult, ALU.add).then_inc(la_ready, 1)
            for r in range(2):
                dve.wait_ge(bt_psum, r + 1)
                i = cp(W0[:, 512 * r:512 * (r + 1)], BANK[2 + r][:, :])
            i.then_inc(bs_ready, 1)
            dve.wait_ge(eb_ready, 1)
            qd, ki, ke = by_key(W1), by_key(W2), by_key(W3)
            for r in range(2):
                first_ = GCH - 1 if r == 0 else 0
                link(cp(decay[:, r], qd[:, r, :, first_::GCH]))
            for n, w in enumerate((qd, ki, ke)):
                dve.wait_ge(eb_ready, n + 1)
                for r in range(2):
                    i = tt(w[:, r], w[:, r], gqT if n == 0 else gkT, ALU.mult)
                i.then_inc(qk_ready, 1)
            for m, view in enumerate((AQ, AK)):
                dve.wait_ge(proj_copied, 17 + m)
                rope2(view).then_inc(roped, 1)
                dve.wait_ge(roped, 6 + m)
            for b in range(2):
                dve.wait_ge(att_psum, b + 1)
                tt(att[:, 4 * b:4 * b + 4, :], BANK[b][:, :].rearrange("p (i s) -> p i s", s=P),
                   const("up_to").unsqueeze(1).to_broadcast([P, 4, P]), ALU.mult)
            dve.wait_ge(att_psum, 4)
            for b in range(2):
                i = tt(W2[:, 512 * b:512 * (b + 1)].rearrange("p (i s) -> p i s", s=P), BANK[2 + b][:, :].rearrange("p (i s) -> p i s", s=P),
                       const("from_on").unsqueeze(1).to_broadcast([P, 4, P]), ALU.mult)
            link(i)
            tt(W5, W5, W2, ALU.add).then_inc(att_ready, 1)
            dve.wait_ge(kv_psum, 2)
            dve.wait_ge(normed, 10)
            for sl in range(3):
                for r in range(2):
                    n = sl if r == 0 else 3 - sl
                    for k in range(2):
                        kvn = BANK[4 + 2 * r + n % 2][:, (n // 2) * S + k * P:(n // 2) * S + (k + 1) * P]
                        if sl == 0:
                            i = cp(state[:, r, k, 0, :], kvn)
                        else:
                            i = stt(state[:, r, k, sl, :], state[:, r, k, sl - 1, :], decay[:, r, k, n:n + 1], kvn, ALU.mult, ALU.add)
                if sl < 2:
                    link(i)
            i.then_inc(state_ready, 1)
            dve.wait_ge(silu_exp, 1)
            link(ts(W3, W3, 1.0, None, ALU.add))
            link(nc.vector.reciprocal(W3, W3))
            link(tt(by_tok2(W3), by_tok2(W3), GG, ALU.mult))
            w3h = W3.rearrange("p (i v) -> p i v", v=P)
            link(tt(w3h, w3h, gla_norm.unsqueeze(1).to_broadcast([P, 8, P]), ALU.mult))
            dve.wait_ge(go_square, 2)
            link(nc.vector.reduce_sum(go_ms, W2.rearrange("p (i v) -> p i v", v=P), AX))
            link(ts(go_ms, go_ms, 1.0 / P, RMS_EPS, ALU.mult, ALU.add))
            nc.vector.memset(go_n, 0.0).then_inc(var_ready, 1)
            dve.wait_ge(rstd_ready, 2 * 5 + 1)
            dve.wait_ge(var_ready, 2 * 5 + 1)
            sharpen(go_r, go_ms, go_n)
            w0h = W0.rearrange("p (i v) -> p i v", v=P)
            for t in range(T):
                for h in range(4):
                    i = stt(w0h[:, 4 * t + h, :], BANK[2 * t + h % 2][:, (h // 2) * P:(h // 2 + 1) * P], go_r[:, 4 * t + h:4 * t + h + 1],
                            w3h[:, 4 * t + h, :], ALU.mult, ALU.mult)
            i.then_inc(go_ready, 1)
            dve.wait_ge(go_ready, 1)
            dve.wait_ge(goT_ready, 1)
            attention(DIL_JOBS, len(AB_JOBS), 8, {})
            mixer_residual(N_2 + 7, 2, 1.0, 5, "rms", U2)
            moe(2, 5, lambda t: normalise(6, "rms", X, t, from_psum=True))


SMALL_TOTAL = 16 * (NMOE * (1 + G + 2) + 4 + 1)
NORM_VALUE = {0: 32, 1: 32, 2: 64, 3: 64, 4: 80, 5: 80, 6: 96}


def by_tok2(w):
    return w.rearrange("p (t n) -> p t n", t=T)


_INS = ["x", "positions", "ab_w_in", "ab_w_out", "nsa_cmp_pos_k", "nsa_cmp_pos_v", "nsa_cmp_w1_k", "nsa_cmp_w2_k",
        "nsa_cmp_w1_v", "nsa_cmp_w2_v", "sb_w_in", "sb_w_out", "ln_mix_g", "ln_mix_b", "ln_ffn_g", "ln_ffn_b",
        "moe_w_grp", "moe_b_grp", "moe_w_rt", "moe_b_rt", "moe_w_gate", "moe_w_up", "moe_w_down", "norm1_w_2",
        "w_in_2", "gla_fwd_gate_w_2", "gla_fwd_gate_b_2", "gla_bwd_gate_w_2", "gla_bwd_gate_b_2",
        "gla_norm_w_2", "w_out_2", "norm2_w_2", "router_group_w_2", "router_group_b_2", "router_expert_w_2",
        "router_expert_b_2", "expert_w_gate_2", "expert_w_up_2", "expert_w_down_2", "final_norm_w_2"]


def _launchable(nc, inputs):
    arrays, a = {}, {}
    for name in _INS:
        v = np.ascontiguousarray(inputs[name])
        arrays[f"in_{name}_dram"] = v
        a[name] = nc.dram_tensor(f"in_{name}_dram", v.shape, mybir.dt.from_np(v.dtype), kind="ExternalInput").ap()
    table = np.ascontiguousarray(np.concatenate([CONST[k] for k in CONST], 1))
    arrays["constants_dram"] = table
    a["constants"] = nc.dram_tensor("constants_dram", table.shape, F32, kind="ExternalInput").ap()
    out = nc.dram_tensor("out_dram", (1, S, D), F32, kind="ExternalOutput").ap()
    build(nc, a, out)
    return arrays


def kernel(**inputs):
    import concourse.bacc as bacc
    from concourse.bass_utils import run_bass_kernel_spmd
    nc = bacc.Bacc("TRN2", target_bir_lowering=False, num_devices=1, dynamic_dma_scratch_size=1024)
    arrays = _launchable(nc, inputs)
    r = run_bass_kernel_spmd(nc, [arrays], core_ids=[0])
    return r.results[0]["out_dram"]
```
